# Optimizing a Trainium2 kernel written in Bass

```python
import math
import jax, jax.numpy as jnp
from jax import lax
import numpy as np

D_MODEL = 1024
BATCH = 1
SEQ = 1024
DEPTH = 2

MEM_LEN = 256
MIX_W = D_MODEL
GROUP_W = MIX_W // 4
N_FOX_HEADS = 4
N_SB_HEADS = 4
N_MLA_HEADS = 4
N_MEM_HEADS = 4
HEAD_DIM = GROUP_W // 4
MLA_Q_RANK = 256
MLA_KV_RANK = 128
MLA_NOPE = HEAD_DIM
MLA_ROPE = 32
MLA_V = GROUP_W // N_MLA_HEADS
ROPE_THETA = 10000.0
BLOCK_Q = 128
LN_EPS = 1e-5
RMS_EPS = 1e-6
FOX_FORGET_BIAS_INIT = 3.0
DEEPNORM_ALPHA = (2 * DEPTH) ** 0.25
DEEPNORM_BETA = (8 * DEPTH) ** -0.25
SPLIT_SIZES = (GROUP_W, GROUP_W, GROUP_W, N_FOX_HEADS,
               GROUP_W, GROUP_W, GROUP_W,
               MLA_Q_RANK, MLA_KV_RANK, MLA_ROPE,
               GROUP_W,
               MIX_W)
IN_COLS = sum(SPLIT_SIZES)


def _layer_norm(x, g, b):
    xf = x.astype(jnp.float32)
    mu = jnp.mean(xf, axis=-1, keepdims=True)
    var = jnp.mean(jnp.square(xf - mu), axis=-1, keepdims=True)
    y = (xf - mu) * lax.rsqrt(var + LN_EPS) * g.astype(jnp.float32) + b.astype(jnp.float32)
    return y.astype(x.dtype)

def _rms_norm(x, g):
    xf = x.astype(jnp.float32)
    y = xf * lax.rsqrt(jnp.mean(jnp.square(xf), axis=-1, keepdims=True) + RMS_EPS)
    return (y * g.astype(jnp.float32)).astype(x.dtype)

def _heads(t, n):
    b, s, _ = t.shape
    return t.reshape(b, s, n, -1).transpose(0, 2, 1, 3)

def _merge(t):
    b, h, s, d = t.shape
    return t.transpose(0, 2, 1, 3).reshape(b, s, h * d)

def _rope(x, positions):
    half = x.shape[-1] // 2
    inv_freq = ROPE_THETA ** (-jnp.arange(half, dtype=jnp.float32) / half)
    ang = positions.astype(jnp.float32)[:, None] * inv_freq[None, :]
    ang = ang.reshape((ang.shape[0],) + (1,) * (x.ndim - 3) + (half,))
    cos, sin = jnp.cos(ang), jnp.sin(ang)
    xf = x.astype(jnp.float32)
    x1, x2 = xf[..., :half], xf[..., half:]
    return jnp.concatenate([x1 * cos - x2 * sin, x1 * sin + x2 * cos], axis=-1).astype(x.dtype)

def _sweep_query_blocks(block_fn, per_query):
    b, h, s = per_query[0].shape[:3]
    nb = s // BLOCK_Q
    blocks = tuple(jnp.moveaxis(a.reshape((b, h, nb, BLOCK_Q) + a.shape[3:]), 2, 0) for a in per_query)
    out = lax.map(lambda args: block_fn(args[0], *args[1:]), (jnp.arange(nb),) + blocks)
    out = jnp.moveaxis(out, 0, 2)
    return out.reshape(b, h, s, out.shape[-1])

def _causal_softmax_attention(q, k, v, scale, log_forget_cum=None):
    key_pos = jnp.arange(k.shape[2])

    def block(i, qb, *fq):
        q_pos = i * BLOCK_Q + jnp.arange(BLOCK_Q)
        logits = jnp.einsum('bhqd,bhkd->bhqk', qb, k).astype(jnp.float32) * scale
        if log_forget_cum is not None:
            logits = logits + fq[0][..., :, None] - log_forget_cum[:, :, None, :]
        mask = key_pos[None, :] <= q_pos[:, None]
        probs = jax.nn.softmax(jnp.where(mask, logits, -jnp.inf), axis=-1)
        return jnp.einsum('bhqk,bhkd->bhqd', probs.astype(v.dtype), v)

    per_query = (q,) if log_forget_cum is None else (q, log_forget_cum)
    return _sweep_query_blocks(block, per_query)

def _stick_breaking_attention(q, k, v, scale):
    key_pos = jnp.arange(k.shape[2])

    def block(i, qb):
        q_pos = i * BLOCK_Q + jnp.arange(BLOCK_Q)
        valid = key_pos[None, :] < q_pos[:, None]
        z = jnp.einsum('bhqd,bhkd->bhqk', qb, k).astype(jnp.float32) * scale
        log_keep = jnp.where(valid, jax.nn.log_sigmoid(-z), 0.0)
        log_tail = lax.cumsum(log_keep, axis=3, reverse=True) - log_keep
        w = jnp.where(valid, jnp.exp(jax.nn.log_sigmoid(z) + log_tail), 0.0)
        return jnp.einsum('bhqk,bhkd->bhqd', w.astype(v.dtype), v)

    return _sweep_query_blocks(block, (q,))

def first_inputs(seed: int = 0) -> dict:
    key = jax.random.key(seed)
    ks = jax.random.split(key, 18)
    f32 = jnp.float32
    nrm = lambda k, shape: jax.random.normal(k, shape, f32)
    return {
        'x': nrm(ks[0], (BATCH, SEQ, D_MODEL)),
        'mem': nrm(ks[1], (BATCH, MEM_LEN, D_MODEL)),
        'ln_in_g': 1.0 + 0.02 * nrm(ks[2], (D_MODEL,)),
        'ln_in_b': 0.02 * nrm(ks[3], (D_MODEL,)),
        'mem_ln_g': 1.0 + 0.02 * nrm(ks[4], (D_MODEL,)),
        'mem_ln_b': 0.02 * nrm(ks[5], (D_MODEL,)),
        'w_in': nrm(ks[6], (DEPTH, D_MODEL, IN_COLS)) * D_MODEL ** -0.5,
        'b_forget': FOX_FORGET_BIAS_INIT + 0.1 * nrm(ks[7], (DEPTH, N_FOX_HEADS)),
        'mla_q_norm_g': 1.0 + 0.02 * nrm(ks[8], (DEPTH, MLA_Q_RANK)),
        'w_mla_q_up': nrm(ks[9], (DEPTH, MLA_Q_RANK, N_MLA_HEADS * (MLA_NOPE + MLA_ROPE))) * MLA_Q_RANK ** -0.5,
        'mla_kv_norm_g': 1.0 + 0.02 * nrm(ks[10], (DEPTH, MLA_KV_RANK)),
        'w_mla_kv_up': nrm(ks[11], (DEPTH, MLA_KV_RANK, N_MLA_HEADS * (MLA_NOPE + MLA_V))) * MLA_KV_RANK ** -0.5,
        'w_mem_kv': nrm(ks[12], (DEPTH, D_MODEL, 2 * GROUP_W)) * D_MODEL ** -0.5,
        'w_out': nrm(ks[13], (DEPTH, MIX_W, D_MODEL)) * (MIX_W ** -0.5 * DEEPNORM_BETA),
        'ln_g': 1.0 + 0.02 * nrm(ks[14], (DEPTH, D_MODEL)),
        'ln_b': 0.02 * nrm(ks[15], (DEPTH, D_MODEL)),
    }

def first_block(x, mem, ln_in_g, ln_in_b, mem_ln_g, mem_ln_b, w_in, b_forget,
              mla_q_norm_g, w_mla_q_up, mla_kv_norm_g, w_mla_kv_up, w_mem_kv,
              w_out, ln_g, ln_b):
    b, s, _ = x.shape
    positions = jnp.arange(s)
    offsets = [int(o) for o in np.cumsum(SPLIT_SIZES)[:-1]]
    head_scale = HEAD_DIM ** -0.5
    mla_scale = (MLA_NOPE + MLA_ROPE) ** -0.5

    h_res = _layer_norm(x, ln_in_g, ln_in_b)
    mem_n = _layer_norm(mem, mem_ln_g, mem_ln_b)

    for l in range(DEPTH):
        proj = jnp.einsum('bsd,dc->bsc', h_res, w_in[l])
        (fq, fk, fv, f_logit, sq, sk, sv, c_q, c_kv, k_rot, mq, gate) = jnp.split(proj, offsets, axis=-1)

        log_f = jax.nn.log_sigmoid((f_logit + b_forget[l]).astype(jnp.float32))
        f_cum = jnp.cumsum(log_f, axis=1).transpose(0, 2, 1)
        out_fox = _causal_softmax_attention(_heads(fq, N_FOX_HEADS), _heads(fk, N_FOX_HEADS),
                                            _heads(fv, N_FOX_HEADS), head_scale, f_cum)

        out_sb = _stick_breaking_attention(_heads(sq, N_SB_HEADS), _heads(sk, N_SB_HEADS),
                                           _heads(sv, N_SB_HEADS), head_scale)

        q_mla = jnp.einsum('bsr,rc->bsc', _rms_norm(c_q, mla_q_norm_g[l]), w_mla_q_up[l])
        q_mla = q_mla.reshape(b, s, N_MLA_HEADS, MLA_NOPE + MLA_ROPE)
        q_full = jnp.concatenate([q_mla[..., :MLA_NOPE], _rope(q_mla[..., MLA_NOPE:], positions)], axis=-1)
        kv_mla = jnp.einsum('bsr,rc->bsc', _rms_norm(c_kv, mla_kv_norm_g[l]), w_mla_kv_up[l])
        kv_mla = kv_mla.reshape(b, s, N_MLA_HEADS, MLA_NOPE + MLA_V)
        k_rope = jnp.broadcast_to(_rope(k_rot, positions)[:, :, None, :], (b, s, N_MLA_HEADS, MLA_ROPE))
        k_full = jnp.concatenate([kv_mla[..., :MLA_NOPE], k_rope], axis=-1)
        v_mla = kv_mla[..., MLA_NOPE:]
        out_mla = _causal_softmax_attention(q_full.transpose(0, 2, 1, 3), k_full.transpose(0, 2, 1, 3),
                                            v_mla.transpose(0, 2, 1, 3), mla_scale)

        mkv = jnp.einsum('bmd,dc->bmc', mem_n, w_mem_kv[l])
        mk, mv = _heads(mkv[..., :GROUP_W], N_MEM_HEADS), _heads(mkv[..., GROUP_W:], N_MEM_HEADS)
        mem_logits = jnp.einsum('bhsd,bhmd->bhsm', _heads(mq, N_MEM_HEADS), mk).astype(jnp.float32) * head_scale
        mem_p = jax.nn.softmax(mem_logits, axis=-1)
        out_mem = jnp.einsum('bhsm,bhmd->bhsd', mem_p.astype(mv.dtype), mv)

        mixed = jnp.concatenate([_merge(out_fox), _merge(out_sb), _merge(out_mla), _merge(out_mem)], axis=-1)
        y = jnp.einsum('bsc,cd->bsd', mixed * jax.nn.silu(gate), w_out[l])

        h_res = _layer_norm(DEEPNORM_ALPHA * h_res + y, ln_g[l], ln_b[l])

    return h_res


DEPTH_2 = 1

HEAD_DIM_2 = 64
ATTN_GROUPS = ((128, 1), (512, 4), (2048, 16))
ATTN_HEADS_PER_GROUP = 4
ATTN_HEADS = ATTN_HEADS_PER_GROUP * len(ATTN_GROUPS)
ATTN_WIDTH = ATTN_HEADS * HEAD_DIM_2
ATTN_OUT_WIDTH = ATTN_HEADS_PER_GROUP * HEAD_DIM_2
ATTN_BLOCK = 128
ROPE_THETA_2 = 500000.0
ROPE_DIM = HEAD_DIM_2 // 4
RWKV_HEADS = D_MODEL // HEAD_DIM_2
RWKV_WIDTH = RWKV_HEADS * HEAD_DIM_2
DECAY_LORA = 64
ICLR_LORA = 64
GATE_LORA = 128
D_FF = 4 * D_MODEL
NORM_EPS = 1e-6
GN_EPS = 64e-5
NEG_INF = -1e30
SPLITS = (ATTN_WIDTH, ATTN_WIDTH, ATTN_WIDTH,
          RWKV_WIDTH, RWKV_WIDTH, RWKV_WIDTH,
          DECAY_LORA, ICLR_LORA, GATE_LORA,
          D_MODEL, D_MODEL)
ATTN_QKV_WIDTH = 3 * ATTN_WIDTH
SHIFT_WIDTH = 3 * RWKV_WIDTH + DECAY_LORA + ICLR_LORA + GATE_LORA
IN_WIDTH = sum(SPLITS)


def rms_norm(t, gain):
    t32 = t.astype(jnp.float32)
    y = t32 * lax.rsqrt(jnp.mean(t32 * t32, axis=-1, keepdims=True) + NORM_EPS)
    return (y * gain.astype(jnp.float32)).astype(t.dtype)

def partial_rope(t, positions):
    half = ROPE_DIM // 2
    inv = ROPE_THETA_2 ** (-jnp.arange(half, dtype=jnp.float32) * 2.0 / ROPE_DIM)
    ang = positions.astype(jnp.float32)[..., None] * inv
    cos = jnp.cos(ang)[:, :, None, :]
    sin = jnp.sin(ang)[:, :, None, :]
    t32 = t.astype(jnp.float32)
    x1 = t32[..., :half]
    x2 = t32[..., half:ROPE_DIM]
    out = jnp.concatenate([x1 * cos - x2 * sin, x1 * sin + x2 * cos, t32[..., ROPE_DIM:]], axis=-1)
    return out.astype(t.dtype)

def dilated_band_attention(q, k, v, dilation, span):
    B, S, H, Dh = q.shape
    unit = dilation * ATTN_BLOCK
    Sp = -(-S // unit) * unit
    L = Sp // dilation
    nb = L // ATTN_BLOCK

    def to_blocks(t):
        t = jnp.pad(t.astype(jnp.float32), ((0, 0), (0, Sp - S), (0, 0), (0, 0)))
        t = t.reshape(B, L, dilation, H, Dh).transpose(0, 2, 1, 3, 4)
        return t.reshape(B, dilation, nb, ATTN_BLOCK, H, Dh)

    qb, kb, vb = to_blocks(q), to_blocks(k), to_blocks(v)

    def with_prev(t):
        prev = jnp.pad(t[:, :, :-1], ((0, 0), (0, 0), (1, 0), (0, 0), (0, 0), (0, 0)))
        return jnp.concatenate([prev, t], axis=3)

    kw, vw = with_prev(kb), with_prev(vb)
    s = jnp.einsum('bdnqhe,bdnkhe->bdnhqk', qb, kw) * (HEAD_DIM_2 ** -0.5)
    qi = jnp.arange(ATTN_BLOCK)[:, None]
    kj = jnp.arange(2 * ATTN_BLOCK)[None, :]
    lag = qi + ATTN_BLOCK - kj
    band = (lag >= 0) & (lag <= span)
    has_prev = (jnp.arange(nb) > 0)[:, None, None] | (kj >= ATTN_BLOCK)[None]
    mask = band[None] & has_prev
    s = jnp.where(mask[None, None, :, None], s, NEG_INF)
    m = jnp.max(s, axis=-1, keepdims=True)
    p = jnp.exp(s - m)
    l = jnp.sum(p, axis=-1, keepdims=True)
    o = jnp.einsum('bdnhqk,bdnkhe->bdnqhe', p / l, vw)
    lse = jnp.swapaxes((m + jnp.log(l))[..., 0], -1, -2)

    def from_blocks(t):
        t = t.reshape((B, dilation, L) + t.shape[4:])
        t = jnp.swapaxes(t, 1, 2)
        return t.reshape((B, Sp) + t.shape[3:])[:, :S]

    return from_blocks(o), from_blocks(lse)

def dilated_attention_mixer(q, k, v, positions):
    B, S = q.shape[:2]
    q = partial_rope(q, positions)
    k = partial_rope(k, positions)
    outs, lses = [], []
    for g, (window, dilation) in enumerate(ATTN_GROUPS):
        sl = slice(g * ATTN_HEADS_PER_GROUP, (g + 1) * ATTN_HEADS_PER_GROUP)
        o, lse = dilated_band_attention(q[:, :, sl], k[:, :, sl], v[:, :, sl], dilation, window // dilation)
        outs.append(o)
        lses.append(lse)
    o = jnp.stack(outs)
    w = jax.nn.softmax(jnp.stack(lses), axis=0)
    out = jnp.sum(w[..., None] * o, axis=0)
    return out.reshape(B, S, ATTN_OUT_WIDTH).astype(q.dtype)

def token_shift(u, mu):
    prev = jnp.pad(u, ((0, 0), (1, 0), (0, 0)))[:, :-1]
    return u + (prev - u) * mu

def wkv7_scan(r, w, k, v, a, b):
    B, S, H, N = r.shape
    xs = tuple(jnp.moveaxis(t, 1, 0) for t in (r, w, k, v, a, b))

    def step(state, inp):
        r_t, w_t, k_t, v_t, a_t, b_t = inp
        sa = jnp.einsum('bhvk,bhk->bhv', state, a_t)
        state = (state * w_t[:, :, None, :] + sa[..., None] * b_t[:, :, None, :]
                 + v_t[..., None] * k_t[:, :, None, :])
        return state, jnp.einsum('bhvk,bhk->bhv', state, r_t)

    s0 = jnp.zeros((B, H, N, N), jnp.float32)
    _, ys = lax.scan(step, s0, xs)
    return jnp.moveaxis(ys, 0, 1)

def rwkv7_mixer(r, k, v, dw, da, dg, w0, w2, a0, a2, g2, k_k, k_a, r_k, gn_w, gn_b):
    B, S, C = r.shape
    H, N = RWKV_HEADS, HEAD_DIM_2
    f32 = jnp.float32
    w_log = -jax.nn.softplus(-(w0 + jnp.tanh(dw) @ w2).astype(f32)) - 0.5
    decay = jnp.exp(-jnp.exp(w_log))
    a = jax.nn.sigmoid((a0 + da @ a2).astype(f32))
    g = (jax.nn.sigmoid(dg) @ g2).astype(f32)
    kk = (k * k_k).astype(f32).reshape(B, S, H, N)
    kk = kk / jnp.maximum(jnp.sqrt(jnp.sum(kk * kk, axis=-1, keepdims=True)), 1e-12)
    k = k.astype(f32) * (1.0 + (a - 1.0) * k_a.astype(f32))
    heads = lambda t: t.astype(f32).reshape(B, S, H, N)
    rh, kh, vh, wh, ah = heads(r), heads(k), heads(v), heads(decay), heads(a)
    y = wkv7_scan(rh, wh, kh, vh, -kk, kk * ah)
    mu = jnp.mean(y, axis=-1, keepdims=True)
    var = jnp.mean(jnp.square(y - mu), axis=-1, keepdims=True)
    y = ((y - mu) * lax.rsqrt(var + GN_EPS)).reshape(B, S, C) * gn_w + gn_b
    bonus = jnp.sum(rh * kh * r_k.astype(f32), axis=-1, keepdims=True) * vh
    y = y + bonus.reshape(B, S, C)
    return (y * g).astype(r.dtype)

def second_inputs(seed: int = 0) -> dict:
    key = jax.random.key(seed)
    ks = jax.random.split(key, 32)
    f32 = jnp.float32
    L, D = DEPTH_2, D_MODEL
    nrm = lambda kk, shape, scale: jax.random.normal(kk, shape, f32) * scale
    x = nrm(ks[0], (BATCH, SEQ, D), 1.0)
    c = nrm(ks[1], (BATCH, D), 1.0)
    offset = jax.random.randint(ks[2], (BATCH, 1), 0, 4096, dtype=jnp.int32)
    positions = offset + jnp.arange(SEQ, dtype=jnp.int32)[None, :]
    return {
        "x": x,
        "c": c,
        "positions": positions,
        "ada_w": nrm(ks[3], (L, D, 6 * D), 0.5 * D ** -0.5),
        "ada_b": nrm(ks[4], (L, 6 * D), 0.02),
        "norm_mix_pre": 1.0 + nrm(ks[5], (L, D), 0.05),
        "norm_mix_post": 1.0 + nrm(ks[6], (L, D), 0.05),
        "norm_ffn_pre": 1.0 + nrm(ks[7], (L, D), 0.05),
        "norm_ffn_post": 1.0 + nrm(ks[8], (L, D), 0.05),
        "w_in": nrm(ks[9], (L, D, IN_WIDTH), D ** -0.5),
        "shift_mu": jax.random.uniform(ks[10], (L, SHIFT_WIDTH), f32),
        "decay_w0": jax.random.uniform(ks[11], (L, RWKV_WIDTH), f32, -6.0, 1.0),
        "decay_w2": nrm(ks[12], (L, DECAY_LORA, RWKV_WIDTH), DECAY_LORA ** -0.5),
        "iclr_a0": nrm(ks[13], (L, RWKV_WIDTH), 0.1),
        "iclr_a2": nrm(ks[14], (L, ICLR_LORA, RWKV_WIDTH), ICLR_LORA ** -0.5),
        "gate_g2": nrm(ks[15], (L, GATE_LORA, RWKV_WIDTH), GATE_LORA ** -0.5),
        "k_k": 0.85 + nrm(ks[16], (L, RWKV_WIDTH), 0.05),
        "k_a": 1.0 + nrm(ks[17], (L, RWKV_WIDTH), 0.05),
        "r_k": nrm(ks[18], (L, RWKV_HEADS, HEAD_DIM_2), 0.1),
        "gn_w": 1.0 + nrm(ks[19], (L, RWKV_WIDTH), 0.05),
        "gn_b": nrm(ks[20], (L, RWKV_WIDTH), 0.02),
        "w_branch": jnp.concatenate([nrm(ks[21], (L, ATTN_OUT_WIDTH, D), ATTN_OUT_WIDTH ** -0.5),
                                     nrm(ks[22], (L, RWKV_WIDTH, D), RWKV_WIDTH ** -0.5)], axis=1),
        "w_out": nrm(ks[23], (L, D, D), D ** -0.5),
        "w_ff1": nrm(ks[24], (L, D, D_FF), D ** -0.5),
        "w_ff2": nrm(ks[25], (L, D_FF, D), D_FF ** -0.5),
    }

def second_block(x, c, positions, ada_w, ada_b, norm_mix_pre, norm_mix_post, norm_ffn_pre,
              norm_ffn_post, w_in, shift_mu, decay_w0, decay_w2, iclr_a0, iclr_a2, gate_g2,
              k_k, k_a, r_k, gn_w, gn_b, w_branch, w_out, w_ff1, w_ff2):
    B, S, D = x.shape
    for l in range(DEPTH_2):
        mod = jax.nn.silu(c) @ ada_w[l] + ada_b[l]
        sh1, sc1, gt1, sh2, sc2, gt2 = [m[:, None, :] for m in jnp.split(mod, 6, axis=-1)]

        h = rms_norm(x, norm_mix_pre[l]) * (1.0 + sc1) + sh1
        proj = h @ w_in[l]
        attn_part = proj[..., :ATTN_QKV_WIDTH]
        rwkv_part = token_shift(proj[..., ATTN_QKV_WIDTH:ATTN_QKV_WIDTH + SHIFT_WIDTH], shift_mu[l])
        gate_part = proj[..., ATTN_QKV_WIDTH + SHIFT_WIDTH:]
        q, k, v = [t.reshape(B, S, ATTN_HEADS, HEAD_DIM_2) for t in jnp.split(attn_part, 3, axis=-1)]
        cuts = np.cumsum([RWKV_WIDTH, RWKV_WIDTH, RWKV_WIDTH, DECAY_LORA, ICLR_LORA])
        r_r, r_k_, r_v, dw, da, dg = jnp.split(rwkv_part, cuts, axis=-1)
        g_attn, g_rwkv = jnp.split(gate_part, 2, axis=-1)

        o_attn = dilated_attention_mixer(q, k, v, positions)
        o_rwkv = rwkv7_mixer(r_r, r_k_, r_v, dw, da, dg, decay_w0[l], decay_w2[l], iclr_a0[l],
                             iclr_a2[l], gate_g2[l], k_k[l], k_a[l], r_k[l], gn_w[l], gn_b[l])
        wb = w_branch[l]
        merged = (jax.nn.sigmoid(g_attn) * (o_attn @ wb[:ATTN_OUT_WIDTH])
                  + jax.nn.sigmoid(g_rwkv) * (o_rwkv @ wb[ATTN_OUT_WIDTH:]))
        mix_out = merged @ w_out[l]
        x = (x + gt1 * rms_norm(mix_out, norm_mix_post[l])).astype(x.dtype)

        h = rms_norm(x, norm_ffn_pre[l]) * (1.0 + sc2) + sh2
        f = jnp.square(jax.nn.relu(h @ w_ff1[l])) @ w_ff2[l]
        x = (x + gt2 * rms_norm(f, norm_ffn_post[l])).astype(x.dtype)
    return x


def setup_inputs(seed=0):
    out = dict(first_inputs(seed))
    for name, value in second_inputs(seed + 1).items():
        if name != "x":
            out[name + "_2"] = value
    return out


def reference(
    x, mem, ln_in_g, ln_in_b, mem_ln_g, mem_ln_b, w_in, b_forget, mla_q_norm_g, w_mla_q_up,
    mla_kv_norm_g, w_mla_kv_up, w_mem_kv, w_out, ln_g, ln_b, c_2, positions_2, ada_w_2, ada_b_2,
    norm_mix_pre_2, norm_mix_post_2, norm_ffn_pre_2, norm_ffn_post_2, w_in_2, shift_mu_2,
    decay_w0_2, decay_w2_2, iclr_a0_2, iclr_a2_2, gate_g2_2, k_k_2, k_a_2, r_k_2, gn_w_2,
    gn_b_2, w_branch_2, w_out_2, w_ff1_2, w_ff2_2,
):
    x = first_block(
        x, mem, ln_in_g, ln_in_b, mem_ln_g, mem_ln_b, w_in, b_forget, mla_q_norm_g, w_mla_q_up,
        mla_kv_norm_g, w_mla_kv_up, w_mem_kv, w_out, ln_g, ln_b,
    )
    return second_block(
        x, c_2, positions_2, ada_w_2, ada_b_2, norm_mix_pre_2, norm_mix_post_2, norm_ffn_pre_2,
        norm_ffn_post_2, w_in_2, shift_mu_2, decay_w0_2, decay_w2_2, iclr_a0_2, iclr_a2_2,
        gate_g2_2, k_k_2, k_a_2, r_k_2, gn_w_2, gn_b_2, w_branch_2, w_out_2, w_ff1_2, w_ff2_2,
    )


_drawn_inputs = setup_inputs


def setup_inputs(seed=0):
    import zlib

    import numpy as np

    out = dict(_drawn_inputs(seed))
    spreads = {}
    factors = {'mem': 3.482,
     'mem_ln_g': 8.0,
     'mem_ln_b': 8.0,
     'b_forget': 64.0,
     'mla_q_norm_g': 8.0,
     'w_mla_q_up': 3.08,
     'mla_kv_norm_g': 8.0,
     'w_mem_kv': 3.199,
     'norm_mix_post_2': 3.861,
     'norm_ffn_pre_2': 3.501,
     'norm_ffn_post_2': 4.11,
     'iclr_a0_2': 5.992,
     'k_k_2': 2.959,
     'k_a_2': 2.832,
     'gn_w_2': 3.976,
     'gn_b_2': 8.0}
    for name, (base, spread) in spreads.items():
        noise = np.random.default_rng([zlib.crc32(name.encode()), seed]).standard_normal(out[name].shape)
        drawn = base * np.exp(spread * noise) if base else spread * noise
        out[name] = __import__('jax').numpy.asarray(drawn.astype(out[name].dtype))
    for name, factor in factors.items():
        out[name] = (out[name] * factor).astype(out[name].dtype)
    return out
```

```python
from contextlib import ExitStack

import numpy as np

import concourse.bass as bass
from concourse import mybir

F32 = mybir.dt.float32
I32 = mybir.dt.int32
ALU = mybir.AluOpType
ACT = mybir.ActivationFunctionType
AX = mybir.AxisListType

P = 128
D = 1024
S = 1024
KT = D // P
NT = S // P
HALF = 512
MEM = 256
DEPTH = 2
LN_EPS = 1e-5
RMS_EPS = 1e-6
GN_EPS = 64e-5
MASKED = -1e30
ALPHA = (2 * DEPTH) ** 0.25
E_HALF = float(np.exp(-0.5))


class Stage:

    def __init__(self, k, name):
        self.k, self.name, self.sems, self.scope = k, name, [], ExitStack()
        if len(k.stages) > 1:
            k.stages.pop(0).scope.close()
        self.before = k.stages[-1].sems if k.stages else []
        k.stages.append(self)

    def sem(self, what):
        s = self.scope.enter_context(self.k.nc.semaphore(f"{self.name}_{what}"))
        self.sems.append(s)
        return s

    def clear_now(self, sp):
        for s in self.sems:
            sp.sem_clear(s)

    def clear_previous(self, sp):
        for s in self.before:
            sp.sem_clear(s)


def loop_edge(k, weights=()):
    with k.nc.Block() as block:
        @block.sync
        def _(sp):
            if k.stages:
                k.stages[-1].clear_now(sp)
            for w in weights:
                w.clear(sp)
    while k.stages:
        k.stages.pop(0).scope.close()


class Kernel:
    def __init__(self, nc, ctx):
        self.nc, self.ctx = nc, ctx
        self.psum = ctx.enter_context(nc.psum_tensor("banks", [P, 8, HALF], F32))
        self.stages = []
        ctx.enter_context(nc.allow_non_contiguous_dma(reason="vectors of gains are laid on the partitions"))

    def sem(self, name):
        return self.ctx.enter_context(self.nc.semaphore(name))

    def sb(self, name, shape, dt=F32, ctx=None):
        return (ctx or self.ctx).enter_context(self.nc.sbuf_tensor(name, shape, dt))

    def bank(self, b, n=HALF, p0=0, p1=P):
        return self.psum[p0:p1, b, 0:n]

    def banks2(self, b):
        return self.psum[:, b:b + 2, :].rearrange("p b n -> p (b n)")


def value_views(tensor, pairs):
    view = tensor[:].rearrange("p (t q w c) -> p t q w c", q=pairs, w=3, c=64)
    flat = tensor[:].rearrange("p (t c) -> p t c", c=pairs * 192)

    def both(t, q0, q1):
        return view[:, t, q0:q1, 0:3:2, :]

    def beside(h, t):
        at = h // 2 * 192 + 64 * (h % 2)
        return flat[:, t, at:at + P]

    def own(h, t):
        at = h // 2 * 192 + P * (h % 2)
        return flat[:, t, at:at + 64]
    return both, beside, own, view[:, :, :, 1, :]


def moving_values(nc, who, dst):
    move = nc.vector.tensor_copy if who == "dve" else nc.scalar.copy
    return lambda ps: move(dst, ps.rearrange("p (q w c) -> p q w c", w=2, c=64))


def gemm(nc, out, pairs):
    for i, (lhs, rhs) in enumerate(pairs):
        mm = nc.tensor.matmul(out, lhs, rhs, start=(i == 0), stop=(i == len(pairs) - 1))
    return mm


class Weights:

    def __init__(self, k, buffers, prefix, sources):
        self.k, self.buf, self.src = k, buffers, sources
        self.loaded = [k.sem(f"{prefix}_loaded_{c}") for c in range(len(sources))]

    def load(self, eng, c):
        src = self.src[c]
        eng.dma_start(self.view(c)[:, 0:src.shape[1], :], src).then_inc(self.loaded[c], 16)

    def view(self, c):
        n = self.src[c].shape[-1]
        return self.buf[c % 2][:, 0:KT, 0:n]

    def clear(self, sp):
        for s in self.loaded:
            sp.sem_clear(s)


def project_stage(k, name, groups, w=None, loads=(), prefetch=(), tail=None, nbanks=8, first=0, tail_act=None,
                  tail_pool=None, then_wait=()):
    nc = k.nc
    st = Stage(k, name)
    products = st.sem("products_done")
    evac = {"dve": st.sem("dve_evacuated"), "act": st.sem("act_evacuated")}
    last_of = {}
    order = {"dve": [], "act": []}
    for g, (c, shape, pairs, who, _) in enumerate(groups):
        last_of[c] = g
        order[who].append(g)

    def region(g):
        p0, p1, n = groups[g][1]
        return k.psum[p0:p1, first + g % nbanks, 0:n]

    with nc.Block() as block:
        @block.sync
        def _(sp):
            st.clear_previous(sp)
            for c in loads:
                if c - 2 in last_of:
                    sp.wait_ge(products, last_of[c - 2] + 1)
                w.load(sp, c)
            for c in prefetch:
                if c - 2 in last_of:
                    sp.wait_ge(products, last_of[c - 2] + 1)
                w.load(sp, c)
            for s, n in then_wait:
                sp.wait_ge(s, n)

        @block.tensor
        def _(pe):
            seen = set()
            for g, (c, shape, pairs, who, _) in enumerate(groups):
                if c is not None and c not in seen:
                    seen.add(c)
                    pe.wait_ge(w.loaded[c], 16)
                if g >= nbanks:
                    former = groups[g - nbanks][3]
                    pe.wait_ge(evac[former], order[former].index(g - nbanks) + 1)
                gemm(nc, region(g), pairs).then_inc(products, 1)

        @block.vector
        def _(dve):
            for g in order["dve"]:
                dve.wait_ge(products, g + 1)
                groups[g][4](region(g)).then_inc(evac["dve"], 1)
            if tail:
                tail(dve, evac["dve"], len(order["dve"]), evac["act"], len(order["act"]), st)

        @block.scalar
        def _(act):
            for g in order["act"]:
                act.wait_ge(products, g + 1)
                groups[g][4](region(g)).then_inc(evac["act"], 1)
            if tail_act:
                tail_act(act, evac["dve"], len(order["dve"]), evac["act"], len(order["act"]), st)

        @block.gpsimd
        def _(pool):
            if tail_pool:
                tail_pool(pool, evac["dve"], len(order["dve"]), evac["act"], len(order["act"]), st)


def moving(nc, who, dst, scale=None):
    if scale is None:
        return (lambda ps: nc.vector.tensor_copy(dst, ps)) if who == "dve" else (lambda ps: nc.scalar.copy(dst, ps))
    if who == "dve":
        return lambda ps: nc.vector.tensor_scalar_mul(dst, ps, scale)
    return lambda ps: nc.scalar.mul(dst, ps, scale)


def transpose_stage(k, name, src, dst, channel_tiles, scale=None, shift=None, prefetch=(), w=None):
    nc = k.nc
    st = Stage(k, name)
    turned = st.sem("turned")
    evac = {"dve": st.sem("dve_evacuated"), "act": st.sem("act_evacuated")}
    n = 2 * channel_tiles

    with nc.Block() as block:
        @block.sync
        def _(sp):
            st.clear_previous(sp)
            for c in prefetch:
                w.load(sp, c)

        @block.tensor
        def _(pe):
            for g in range(n):
                c, half = g // 2, g % 2
                if g >= 8:
                    pe.wait_ge(evac["dve" if g % 2 else "act"], (g - 8) // 2 + 1)
                for i in range(4):
                    t = 4 * half + i
                    mm = nc.tensor.transpose(k.psum[:, g % 8, i * P:(i + 1) * P], src(t)[:, c * P:(c + 1) * P], k.ident[:])
                mm.then_inc(turned, 1)

        @block.vector
        def _(dve):
            for g in range(1, n, 2):
                c = g // 2
                out = dst[:, c, HALF:S]
                dve.wait_ge(turned, g + 1)
                if scale is None:
                    nc.vector.tensor_copy(out, k.bank(g % 8)).then_inc(evac["dve"], 1)
                else:
                    nc.vector.tensor_scalar(out, k.bank(g % 8), scale[:, c:c + 1],
                                            shift[:, c:c + 1] if shift is not None else 0.0,
                                            ALU.mult, ALU.add).then_inc(evac["dve"], 1)

        @block.scalar
        def _(act):
            for g in range(0, n, 2):
                c = g // 2
                out = dst[:, c, 0:HALF]
                act.wait_ge(turned, g + 1)
                if scale is None:
                    nc.scalar.copy(out, k.bank(g % 8)).then_inc(evac["act"], 1)
                else:
                    nc.scalar.activation(out, k.bank(g % 8), ACT.Identity, scale=scale[:, c:c + 1],
                                         bias=shift[:, c:c + 1] if shift is not None else 0.0).then_inc(evac["act"], 1)


def layer_norm_stage(k, name, x, tiles, gain, bias, loads=()):
    nc = k.nc
    st = Stage(k, name)
    arrived, stats, rooted, scaled, step = (st.sem(n) for n in ("arrived", "stats_ready", "root_ready", "scaled", "dve_step"))
    with nc.Block() as block:
        @block.sync
        def _(sp):
            st.clear_previous(sp)
            for dst, src in loads:
                sp.dma_start(dst, src).then_inc(arrived, 16)

        @block.vector
        def _(dve):
            for t in range(tiles):
                if t == 0 and loads:
                    dve.wait_ge(arrived, 16 * len(loads))
                for h in range(2):
                    last = nc.vector.bn_stats(k.stats[:, t, h, :], x[:, t, h * HALF:(h + 1) * HALF])
            last.then_inc(step, 1)
            dve.wait_ge(step, 1)
            for t in range(tiles):
                last = nc.vector.bn_aggr(k.moments[:, t, :], k.stats[:, t, :, :])
            last.then_inc(step, 1)
            dve.wait_ge(step, 2)
            nc.vector.tensor_scalar_add(k.root[:, 0:tiles], k.moments[:, 0:tiles, 1], LN_EPS).then_inc(stats, 1)
            dve.wait_ge(rooted, 1)
            nc.vector.reciprocal(k.root[:, 0:tiles], k.root[:, 0:tiles]).then_inc(step, 1)
            dve.wait_ge(step, 3)
            for t in range(tiles):
                nc.vector.tensor_scalar(x[:, t, :], x[:, t, :], k.moments[:, t, 0:1], k.root[:, t:t + 1],
                                        ALU.subtract, ALU.mult).then_inc(step, 1)
                dve.wait_ge(step, 4 + t)
                nc.vector.tensor_tensor(x[:, t, :], x[:, t, :], gain, ALU.mult).then_inc(scaled, 1)

        @block.scalar
        def _(act):
            act.wait_ge(stats, 1)
            nc.scalar.activation(k.root[:, 0:tiles], k.root[:, 0:tiles], ACT.Sqrt).then_inc(rooted, 1)

        @block.gpsimd
        def _(pool):
            if loads:
                pool.wait_ge(arrived, 16 * len(loads))
            for t in range(tiles):
                pool.wait_ge(scaled, t + 1)
                nc.gpsimd.tensor_tensor(x[:, t, :], x[:, t, :], bias, ALU.add)


def attention_stage(k, name, buf, q, key, v, out, heads, plan, masks, scale, sticks=False, prefetch=(), w=None, tiles=NT):
    nc = k.nc
    st = Stage(k, name)
    units = [(h, t) for h in range(heads) for t in range(tiles)]
    N = len(units)
    wide = max(sum(r[2] for r in plan(t)) for t in range(tiles)) * P
    slots = 2 if wide <= 1024 else 1
    span = 2 if slots == 2 else 4
    names = ("scores_done", "max_ready", "exp_done", "turned", "dve_moved", "act_moved", "summed", "normalised",
             "dve_step", "clamped", "softplus_ready", "weights_log_ready")
    (scores_done, max_ready, exp_done, turned, dve_moved, act_moved, summed, normalised,
     step, clamped, softplus_ready, log_ready) = (st.sem(n) for n in names)
    steps = [0]

    def cols(u):
        return P * sum(r[2] for r in plan(units[u][1]))

    def scores(u, a=0, b=None):
        s = u % slots
        flat = k.psum[:, span * s:span * s + span, :].rearrange("p b n -> p (b n)")
        return flat[:, a:cols(u) if b is None else b]

    def blocks(u):
        h, t = units[u]
        return [(g, b) for g, b0, n in plan(t) for b in range(b0, b0 + n)]

    def chain(dve, ins):
        steps[0] += 1
        ins.then_inc(step, 1)
        dve.wait_ge(step, steps[0])

    def moved_counts(u):
        dve_n = act_n = 0
        for i in range(u + 1):
            n = -(-len(blocks(i)) // 4)
            act_n += (n + 1) // 2
            dve_n += n // 2
        return dve_n, act_n

    piece_no = {}
    total = 0
    for u in range(N):
        for j in range(-(-len(blocks(u)) // 4)):
            piece_no[u, j] = total
            total += 1
    turn_banks = 2

    with nc.Block() as block:
        @block.sync
        def _(sp):
            st.clear_previous(sp)
            for c in prefetch:
                w.load(sp, c)

        @block.tensor
        def _(pe):
            def do_scores(u):
                h, t = units[u]
                if u >= slots:
                    pe.wait_ge(log_ready if sticks else exp_done, u - slots + 1)
                at = 0
                for g, b0, n in plan(t):
                    a, left = b0 * P, n * P
                    while left:
                        size = min(left, HALF - at % HALF)
                        mm = nc.tensor.matmul(scores(u, at, at + size), q(h, g, t), key(h, g, a, a + size), start=True, stop=True)
                        at, a, left = at + size, a + size, left - size
                mm.then_inc(scores_done, 1)

            def do_turn(u):
                pe.wait_ge(exp_done, u + 1)
                n = len(blocks(u))
                for j in range(-(-n // 4)):
                    p = piece_no[u, j]
                    if p >= turn_banks:
                        pu, pj = next(key_ for key_, val in piece_no.items() if val == p - turn_banks)
                        d, a = moved_counts(pu - 1) if pu else (0, 0)
                        pe.wait_ge(dve_moved if pj % 2 else act_moved, (d if pj % 2 else a) + pj // 2 + 1)
                    for i in range(4 * j, min(4 * j + 4, n)):
                        mm = nc.tensor.transpose(k.psum[:, 4 + p % turn_banks, (i % 4) * P:(i % 4 + 1) * P],
                                                 buf.weights[u % buf.nw][:, i * P:(i + 1) * P], k.ident[:])
                    mm.then_inc(turned, 1)

            def do_sum(u):
                h, t = units[u]
                d, a = moved_counts(u)
                if d:
                    pe.wait_ge(dve_moved, d)
                pe.wait_ge(act_moved, a)
                if u >= 2:
                    pe.wait_ge(normalised, u - 1)
                bl = blocks(u)
                gemm(nc, k.psum[0:64 if sticks else P, 6 + u % 2, 0:P],
                     [(v(h, g, b), buf.turned[u % 2][:, i * P:(i + 1) * P]) for i, (g, b) in enumerate(bl)]).then_inc(summed, 1)

            for u in range(min(slots, N)):
                do_scores(u)
            for u in range(N):
                do_turn(u)
                if u + slots < N:
                    do_scores(u + slots)
                if u >= 1:
                    do_sum(u - 1)
            do_sum(N - 1)

        @block.vector
        def _(dve):
            def row_max(u):
                dve.wait_ge(scores_done, u + 1)
                t = units[u][1]
                if len(masks(t)) == 1 and masks(t)[0][1] == cols(u):
                    chain(dve, nc.vector.tensor_tensor_reduce(scores(u), scores(u), masks(t)[0][2], 1.0, -3e38, ALU.add, ALU.max,
                                                              k.rowmax[:, u:u + 1]))
                    nc.vector.tensor_scalar_mul(k.negmax[:, u:u + 1], k.rowmax[:, u:u + 1], -scale).then_inc(max_ready, 1)
                    return
                for a, n, m in masks(t):
                    last = nc.vector.tensor_tensor(scores(u, a, a + n), scores(u, a, a + n), m, ALU.add)
                if masks(t):
                    chain(dve, last)
                chain(dve, nc.vector.reduce_max(k.rowmax[:, u:u + 1], scores(u), AX.X))
                nc.vector.tensor_scalar_mul(k.negmax[:, u:u + 1], k.rowmax[:, u:u + 1], -scale).then_inc(max_ready, 1)

            def clamp(u):
                dve.wait_ge(scores_done, u + 1)
                if u >= 2:
                    dve.wait_ge(turned, piece_no[u - 1, 0])
                nc.vector.tensor_scalar_min(buf.weights[u % 2][:, 0:cols(u)], scores(u), 40.0).then_inc(clamped, 1)

            def stick_logs(u):
                z, n = buf.weights[u % 2], cols(u)
                dve.wait_ge(softplus_ready, u + 1)
                chain(dve, nc.vector.tensor_tensor(z[:, 0:n], scores(u), z[:, 0:n], ALU.max))
                chain(dve, nc.vector.tensor_tensor(z[:, n - P:n], z[:, n - P:n], k.before01[:], ALU.mult))
                chain(dve, nc.vector.tensor_tensor_scan(buf.cum[:, 0:n][:, ::-1], k.one[:, 0:1].broadcast_to([P, n]),
                                                        z[:, 0:n][:, ::-1], 0.0, ALU.mult, ALU.add))
                chain(dve, nc.vector.tensor_tensor(z[:, 0:n], scores(u), buf.cum[:, 0:n], ALU.subtract))
                nc.vector.tensor_tensor(z[:, n - P:n], z[:, n - P:n], k.before_add[:], ALU.add).then_inc(log_ready, 1)

            def move(u):
                n = len(blocks(u))
                if u >= 2:
                    dve.wait_ge(summed, u - 1)
                for j in range(1, -(-n // 4), 2):
                    dve.wait_ge(turned, piece_no[u, j] + 1)
                    c = min(4, n - 4 * j) * P
                    nc.vector.tensor_copy(buf.turned[u % 2][:, j * HALF:j * HALF + c],
                                          k.bank(4 + piece_no[u, j] % turn_banks, c)).then_inc(dve_moved, 1)

            def normalise(u):
                h, t = units[u]
                dve.wait_ge(summed, u + 1)
                if sticks:
                    nc.vector.tensor_copy(out(h, t), k.psum[0:64, 6 + u % 2, 0:P]).then_inc(normalised, 1)
                else:
                    mine, other = slice(64 * (h % 2), 64 * (h % 2) + 64), slice(64 * (1 - h % 2), 64 * (1 - h % 2) + 64)
                    chain(dve, nc.vector.reciprocal(k.inverse_sum[mine, :], k.psum[other, 6 + u % 2, 0:P]))
                    nc.vector.tensor_tensor(out(h, t), k.psum[mine, 6 + u % 2, 0:P], k.inverse_sum[mine, :],
                                            ALU.mult).then_inc(normalised, 1)
                    dve.wait_ge(normalised, u + 1)

            if sticks:
                clamp(0)
                for u in range(N):
                    if u + 1 < N:
                        clamp(u + 1)
                    stick_logs(u)
                    if u >= 1:
                        move(u - 1)
                    if u >= 2:
                        normalise(u - 2)
                move(N - 1)
                normalise(N - 2)
                normalise(N - 1)
            else:
                for u in range(min(slots, N)):
                    row_max(u)
                for u in range(N):
                    move(u)
                    if u + slots < N:
                        row_max(u + slots)
                    if u >= 1:
                        normalise(u - 1)
                normalise(N - 1)

        @block.scalar
        def _(act):
            def exponent(u):
                dst = buf.weights[u % buf.nw][:, 0:cols(u)]
                if sticks:
                    act.wait_ge(log_ready, u + 1)
                    nc.scalar.activation(dst, dst, ACT.Exp).then_inc(exp_done, 1)
                else:
                    act.wait_ge(max_ready, u + 1)
                    if u >= buf.nw:
                        act.wait_ge(turned, piece_no[u - buf.nw + 1, 0])
                    nc.scalar.activation(dst, scores(u), ACT.Exp, bias=k.negmax[:, u:u + 1], scale=scale).then_inc(exp_done, 1)

            def softplus_log(u):
                z = buf.weights[u % 2][:, 0:cols(u)]
                act.wait_ge(clamped, u + 1)
                nc.scalar.activation(z, z, ACT.Exp).then_inc(act_step, 1)
                act.wait_ge(act_step, u + 1)
                nc.scalar.activation(z, z, ACT.Ln, bias=1.0).then_inc(softplus_ready, 1)

            def move(u):
                n = len(blocks(u))
                if u >= 2:
                    act.wait_ge(summed, u - 1)
                for j in range(0, -(-n // 4), 2):
                    act.wait_ge(turned, piece_no[u, j] + 1)
                    c = min(4, n - 4 * j) * P
                    nc.scalar.copy(buf.turned[u % 2][:, j * HALF:j * HALF + c],
                                   k.bank(4 + piece_no[u, j] % turn_banks, c)).then_inc(act_moved, 1)

            act_step = st.sem("act_step")
            nc.scalar.preload_act_table_set("natural_log_exp_and_others")
            if sticks:
                softplus_log(0)
                for u in range(N):
                    if u + 1 < N:
                        softplus_log(u + 1)
                    exponent(u)
                    move(u)
            else:
                ahead = 1 if slots == 2 else 0
                if ahead:
                    exponent(0)
                for u in range(N):
                    if ahead and u + 1 < N:
                        exponent(u + 1)
                    if not ahead:
                        exponent(u)
                    move(u)



def rope_tables():
    half = 16
    freq = (10000.0 ** (-np.arange(half, dtype=np.float32) / half)).astype(np.float32)
    angle = np.arange(S, dtype=np.float32)[None, :] * np.concatenate([freq, freq])[:, None]
    return np.stack([np.cos(angle), np.sin(angle)], 1).astype(np.float32)


def rotation(n, starts, half):
    r = np.zeros((n, n), np.float32)
    for s in starts:
        for i in range(half):
            r[s + i, s + i + half] = -1.0
            r[s + i + half, s + i] = 1.0
    return np.ascontiguousarray(r.T)


def constants_one():
    q, key = np.arange(P)[:, None], np.arange(P)[None, :]
    parts = [np.eye(P), np.where(key <= q, 0.0, MASKED), np.where(key < q, 1.0, 0.0), np.where(key < q, 0.0, MASKED)]
    return np.concatenate(parts, 1).astype(np.float32)



O_FQ, O_FK, O_FV, O_FL, O_SQ, O_SK, O_SV, O_CQ, O_CKV, O_KR, O_MQ, O_GATE = (
    0, 256, 512, 768, 772, 1028, 1284, 1540, 1796, 1924, 1956, 2212)
RANKS = 384
HEAD_SCALE = 0.125
MLA_SCALE = 96 ** -0.5


class Buffers:
    pass


def common_tensors(k):
    nc = k.nc
    k.x = k.sb("x_residual", [P, NT, D])
    k.ht = k.sb("h_channel_major", [P, KT, S])
    k.consts = k.sb("masks_and_identity", [P, 4 * P])
    k.ident = k.consts[:, 0:P]
    k.causal_add = k.consts[:, P:2 * P]
    k.before01 = k.consts[:, 2 * P:3 * P]
    k.before_add = k.consts[:, 3 * P:4 * P]
    k.one = k.sb("one", [P, 1])
    k.stats = k.sb("norm_stats", [P, NT, 2, 6])
    k.moments = k.sb("norm_moments", [P, NT, 2])
    k.root = k.sb("norm_root", [P, NT])
    k.rowmax = k.sb("row_max", [P, 32])
    k.negmax = k.sb("row_max_negated", [P, 32])
    k.inverse_sum = k.sb("inverse_sum", [P, P])


def first_block(k, a):
    nc = k.nc
    with ExitStack() as own:
        memt = k.sb("mem_channel_major", [P, KT, MEM], ctx=own)
        buf = Buffers()
        wbuf = [k.sb(f"weights_{i}", [P, KT, HALF], ctx=own) for i in range(2)]
        mixed = k.sb("mixed_channel_major", [P, KT, S], ctx=own)
        qt = k.sb("queries", [P, 4, S], ctx=own)
        kt = k.sb("keys", [P, 4, S], ctx=own)
        values = value_views(k.sb("values", [P, NT * 2 * 192], ctx=own), 2)
        scratch = k.sb("attention_scratch", [P, 5, S], ctx=own)
        small = k.sb("small_columns", [P, 16], ctx=own)
        buf.weights = [scratch[:, i, :] for i in range(2)]
        buf.turned = [scratch[:, 2 + i, :] for i in range(2)]
        buf.cum = scratch[:, 4, :]
        buf.nw = 2
        gains = mixed[:, 0:4, :]
        mem_x = qt[:, 0:2, :]

        st = Stage(k, "start")
        ready = st.sem("arrived")
        with nc.Block() as block:
            @block.sync
            def _(sp):
                loads = [(k.consts[:], nc.inline_tensor(constants_one(), "constants_one").ap()),
                         (k.x[:], a["x"][0].rearrange("(t p) d -> p t d", p=P)),
                         (mem_x, a["mem"][0].rearrange("(t p) d -> p t d", p=P))]
                for i, name in enumerate(("ln_in_g", "ln_in_b", "mem_ln_g", "mem_ln_b")):
                    loads.append((gains[:, i, :], a[name].partition_broadcast(P)))
                for dst, src in loads:
                    sp.dma_start(dst, src).then_inc(ready, 16)
                sp.wait_ge(ready, 16 * len(loads))

            @block.vector
            def _(dve):
                nc.vector.memset(values[3], 1.0)
                nc.vector.memset(k.one[:], 1.0).then_inc(st.sem("one_set"), 1)
        layer_norm_stage(k, "norm_x", k.x, NT, gains[:, 0, :], gains[:, 1, :])
        layer_norm_stage(k, "norm_mem", mem_x, 2, gains[:, 2, :], gains[:, 3, :])

        st = Stage(k, "mem_turn")
        turned, moved = st.sem("turned"), st.sem("moved")
        with nc.Block() as block:
            @block.sync
            def _(sp):
                st.clear_previous(sp)

            @block.tensor
            def _(pe):
                for c in range(KT):
                    for t in range(2):
                        mm = nc.tensor.transpose(k.psum[:, c, t * P:(t + 1) * P], mem_x[:, t, c * P:(c + 1) * P], k.ident)
                    mm.then_inc(turned, 1)

            @block.vector
            def _(dve):
                for c in range(KT):
                    dve.wait_ge(turned, c + 1)
                    nc.vector.tensor_copy(memt[:, c, :], k.bank(c, MEM)).then_inc(moved, 1)
        loop_edge(k)
        with nc.Fori(0, DEPTH) as layer:
            first_layer(k, a, layer, Holder(memt, buf, wbuf, mixed, qt, kt, scratch, small, values))


class Holder:
    def __init__(self, memt, buf, wbuf, mixed, qt, kt, scratch, small, values):
        self.values = values
        self.memt, self.buf, self.wbuf, self.mixed = memt, buf, wbuf, mixed
        self.qt, self.kt, self.scratch, self.small = qt, kt, scratch, small


def first_layer(k, a, layer, b):
    nc = k.nc
    ht, mixed, qt, kt = k.ht, b.mixed, b.qt, b.kt
    place, beside, own, _ = b.values

    def rows(name, c0, c1):
        w = a[name]
        return w[bass.ds(layer, 1)].rearrange("l (kt p) c -> p (l kt) c", p=P)[:, :, c0:c1]

    W = Weights(k, b.wbuf, "layer_w", [
        rows("w_in", 0, 512), rows("w_in", 512, 772), rows("w_in", 772, 1284), rows("w_in", 1284, 1540),
        rows("w_in", 1540, 1956), rows("w_in", 1956, 2212), rows("w_mem_kv", 0, 512),
        rows("w_in", 2212, 2724), rows("w_in", 2724, 3236), rows("w_out", 0, 512), rows("w_out", 512, 1024)])
    (C_FQK, C_FVL, C_SQK, C_SV, C_LOW, C_MQ, C_MKV, C_GATE, _, C_OUT, _) = range(11)

    def over_tokens(c, col, width, half):
        return [(W.view(c)[:, i, col:col + width], ht[:, i, half * HALF:(half + 1) * HALF]) for i in range(KT)]

    def over_columns(c, t, col, width, src=None):
        return [((src or ht)[:, i, t * P:(t + 1) * P], W.view(c)[:, i, col:col + width]) for i in range(KT)]

    def halves(dst_rows, tile, half):
        return dst_rows[tile][:, half * HALF:(half + 1) * HALF]

    transpose_stage(k, "turn_x", lambda t: k.x[:, t, :], ht, KT, prefetch=(C_FQK, C_FVL), w=W)

    groups = []
    logits = b.scratch[0:4, 0, :]
    work = b.scratch[0:4, 1, :]
    cum = b.scratch[0:4, 2, :]
    negcum = b.scratch[0:4, 3, :]
    bias = b.small[0:4, 0:1]
    for tile in range(4):
        dst = qt if tile < 2 else kt
        for half in range(2):
            def split(ps, dst=dst, tile=tile, half=half):
                h = 2 * (tile % 2)
                cols = slice(half * HALF, (half + 1) * HALF)
                nc.vector.tensor_copy(dst[0:64, h, cols], ps[0:64, :])
                return nc.vector.tensor_copy(dst[0:64, h + 1, cols], ps[64:128, :])

            def split_act(ps, dst=dst, tile=tile, half=half):
                h = 2 * (tile % 2)
                cols = slice(half * HALF, (half + 1) * HALF)
                nc.scalar.copy(dst[0:64, h, cols], ps[0:64, :])
                return nc.scalar.copy(dst[0:64, h + 1, cols], ps[64:128, :])
            groups.append((C_FQK, (0, P, HALF), over_tokens(C_FQK, tile * P, P, half), "dve" if half else "act",
                           split if half else split_act))
    for half in range(2):
        groups.append((C_FVL, (0, 4, HALF), over_tokens(C_FVL, 256, 4, half), "act",
                       moving(nc, "act", logits[:, half * HALF:(half + 1) * HALF])))
    for t in range(NT):
        who = "dve" if t % 2 else "act"
        groups.append((C_FVL, (0, P, 256), over_columns(C_FVL, t, 0, 256), who, moving_values(nc, who, place(t, 0, 2))))

    def forget_tail(dve, dve_sem, dve_n, act_sem, act_n, st):
        s = st.sem("forget_step")
        zeroed = st.sem("rows_zeroed")
        nc.vector.memset(qt[64:P, :, :], 0.0)
        nc.vector.memset(kt[64:P, :, :], 0.0).then_inc(zeroed, 1)
        dve.wait_ge(zeroed, 1)
        nc.vector.memset(qt[64:66, :, :], 1.0)
        nc.vector.memset(kt[64:66, :, :], 1.0)
        dve.wait_ge(act_sem, act_n)
        dve.wait_ge(k.bias_arrived, 16)
        nc.vector.tensor_scalar(logits, logits, bias, None, ALU.add).then_inc(s, 1)
        dve.wait_ge(s, 1)
        nc.vector.tensor_scalar(work, logits, -1.0, None, ALU.mult).then_inc(s, 1)
        dve.wait_ge(s, 2)
        nc.vector.tensor_tensor(work, work, logits, ALU.min).then_inc(k.forget_abs, 1)
        dve.wait_ge(k.forget_ln, 1)
        nc.vector.tensor_scalar(logits, logits, 0.0, None, ALU.min).then_inc(s, 1)
        dve.wait_ge(s, 3)
        nc.vector.tensor_tensor(logits, logits, work, ALU.subtract).then_inc(s, 1)
        dve.wait_ge(s, 4)
        nc.vector.tensor_tensor_scan(cum, k.one[0:4, 0:1].broadcast_to([4, S]), logits, 0.0, ALU.mult, ALU.add).then_inc(s, 1)
        dve.wait_ge(s, 5)
        nc.vector.tensor_scalar(negcum, cum, -8.0, None, ALU.mult).then_inc(s, 1)
        dve.wait_ge(s, 6)
        nc.vector.tensor_scalar(cum, cum, 8.0, None, ALU.mult).then_inc(s, 1)
        dve.wait_ge(s, 7)

    def forget_act(act, dve_sem, dve_n, act_sem, act_n, st):
        s = st.sem("forget_exp")
        act.dma_start(bias, a["b_forget"][bass.ds(layer, 1)].rearrange("l h -> h l")).then_inc(k.bias_arrived, 16)
        act.wait_ge(k.forget_abs, 1)
        nc.scalar.activation(work, work, ACT.Exp).then_inc(s, 1)
        act.wait_ge(s, 1)
        nc.scalar.activation(work, work, ACT.Ln, bias=1.0).then_inc(k.forget_ln, 1)

    k.bias_arrived, k.forget_abs, k.forget_ln = (k.sem(f"forget_{n}") for n in ("bias_arrived", "abs_ready", "ln_ready"))
    project_stage(k, "fox_project", groups, W, prefetch=(C_SQK, C_SV), tail=forget_tail, tail_act=forget_act)

    st = Stage(k, "forget_rows")
    placed = st.sem("rows_placed")
    with nc.Block() as block:
        @block.sync
        def _(sp):
            st.clear_previous(sp)
            for s in (k.bias_arrived, k.forget_abs, k.forget_ln):
                sp.sem_clear(s)
            sp.dma_start(qt[64:65, :, :], cum).then_inc(placed, 16)
            sp.dma_start(kt[65:66, :, :], negcum).then_inc(placed, 16)
            sp.wait_ge(placed, 32)

    def mixed_rows(kind):
        return lambda h, t: mixed[64 * (h % 2):64 * (h % 2) + 64, 2 * kind + h // 2, t * P:(t + 1) * P]

    def with_ones(h, g, kb):
        return beside(h, kb)

    def full(t):
        return [(0, 0, t + 1)]

    def diagonal(mask):
        return lambda t: [(t * P, P, mask)]

    attention_stage(k, "fox", b.buf, lambda h, g, t: qt[:, h, t * P:(t + 1) * P],
                    lambda h, g, c0, c1: kt[:, h, c0:c1], with_ones,
                    mixed_rows(0), 4, full, diagonal(k.causal_add), HEAD_SCALE)

    def paired(dst, c, first_tile, scale=None):
        out = []
        for tile in range(2):
            for half in range(2):
                who = "dve" if half else "act"
                out.append((c, (0, P, HALF), over_tokens(c, first_tile * P + tile * P, P, half), who,
                            moving(nc, who, dst[:, tile, half * HALF:(half + 1) * HALF], scale)))
        return out

    def padded(c, scale):
        out = []
        for tile in range(2):
            for half in range(2):
                cols = slice(half * HALF, (half + 1) * HALF)

                def split_dve(ps, tile=tile, cols=cols):
                    nc.vector.tensor_scalar_mul(qt[0:64, 2 * tile, cols], ps[0:64, :], scale)
                    return nc.vector.tensor_scalar_mul(qt[64:P, 2 * tile + 1, cols], ps[64:P, :], scale)

                def split_act(ps, tile=tile, cols=cols):
                    nc.scalar.mul(qt[0:64, 2 * tile, cols], ps[0:64, :], scale)
                    return nc.scalar.mul(qt[64:P, 2 * tile + 1, cols], ps[64:P, :], scale)
                out.append((c, (0, P, HALF), over_tokens(c, tile * P, P, half), "dve" if half else "act",
                            split_dve if half else split_act))
        return out

    def zero_halves(pool, dve_sem, dve_n, act_sem, act_n, st):
        for h in range(4):
            r = 64 * (1 - h % 2)
            nc.gpsimd.memset(qt[r:r + 64, h, :], 0.0)

    groups = padded(C_SQK, 0.125) + paired(kt, C_SQK, 2)
    for t in range(NT):
        who = "dve" if t % 2 else "act"
        groups.append((C_SV, (0, P, 256), over_columns(C_SV, t, 0, 256), who, moving_values(nc, who, place(t, 0, 2))))
    project_stage(k, "sb_project", groups, W, prefetch=(C_LOW,), tail_pool=zero_halves)

    def pair_q(h, g, t):
        return qt[:, h, t * P:(t + 1) * P]

    def pair_k(h, g, c0, c1):
        return kt[:, h // 2, c0:c1]

    attention_stage(k, "sb", b.buf, pair_q, pair_k, lambda h, g, kb: own(h, kb),
                    mixed_rows(1), 4, full, None, 1.0, sticks=True)

    low_rank_stages(k, a, layer, b, W, C_LOW, over_tokens, over_columns)
    attention_stage(k, "mla", b.buf, lambda h, g, t: qt[0:96, h, t * P:(t + 1) * P],
                    lambda h, g, c0, c1: kt[0:96, h, c0:c1], with_ones,
                    mixed_rows(2), 4, full, diagonal(k.causal_add), MLA_SCALE,
                    prefetch=(C_MQ, C_MKV), w=W)

    groups = padded(C_MQ, 1.0)
    for tile in range(2):
        groups.append((C_MKV, (0, P, MEM), [(W.view(C_MKV)[:, i, tile * P:(tile + 1) * P], b.memt[:, i, :]) for i in range(KT)],
                       "dve", moving(nc, "dve", kt[:, tile, 0:MEM])))
    for t in range(2):
        groups.append((C_MKV, (0, P, 256), over_columns(C_MKV, t, 256, 256, b.memt), "act", moving_values(nc, "act", place(t, 0, 2))))
    project_stage(k, "mem_project", groups, W, prefetch=(C_GATE, C_GATE + 1), tail_pool=zero_halves)
    attention_stage(k, "mem", b.buf, pair_q, pair_k, with_ones,
                    mixed_rows(3), 4, lambda t: [(0, 0, 2)],
                    lambda t: [], HEAD_SCALE)

    gate_stage(k, b, W, C_GATE, over_tokens)

    gains = mixed[:, 0:2, :]
    groups = []
    for n in range(2):
        for t in range(NT):
            def add(ps, n=n, t=t):
                part = k.x[:, t, n * HALF:(n + 1) * HALF]
                return nc.vector.scalar_tensor_tensor(part, part, ALPHA, ps, ALU.mult, ALU.add)
            groups.append((C_OUT + n, (0, P, HALF), over_columns(C_OUT + n, t, 0, HALF, mixed), "dve", add))
    project_stage(k, "out_project", groups, W)
    layer_norm_stage(k, "norm_out", k.x, NT, gains[:, 0, :], gains[:, 1, :],
                     loads=[(gains[:, i, :], a[n][bass.ds(layer, 1)].rearrange("l d -> (l d)").partition_broadcast(P))
                            for i, n in enumerate(("ln_g", "ln_b"))])
    loop_edge(k, [W])


def low_rank_stages(k, a, layer, b, W, C_LOW, over_tokens, over_columns):
    nc = k.nc
    qt, kt = b.qt, b.kt
    place = b.values[0]
    low = kt[:].rearrange("p a s -> p (a s)")[:, 0:NT * RANKS].rearrange("p (t r) -> p t r", t=NT)
    with ExitStack() as own:
        low_t = b.wbuf[1][:].rearrange("p a c -> p (a c)")[:, 0:3 * S].rearrange("p (a s) -> p a s", a=3)
        up_q = b.scratch[:, 0, 0:768].rearrange("p (a c) -> p a c", a=2)
        up_kv = b.scratch[:, 1, 0:512]
        trig = b.mixed[64:96, 6:8, :]
        turn = b.scratch[64:96, 1, 512:544]
        squares = qt[:].rearrange("p a s -> p (a s)")[:, 0:NT * RANKS].rearrange("p (t r) -> p t r", t=NT)
        sums = b.small[:, 0:16].rearrange("p (t two) -> p t two", two=2)
        gain = k.sb("latent_gains", [P, 3], ctx=own)
        kr = b.scratch[64:96, 2, :]

        st = Stage(k, "mla_loads")
        here = st.sem("arrived")
        with nc.Block() as block:
            @block.sync
            def _(sp):
                st.clear_previous(sp)
                loads = [(up_q, a["w_mla_q_up"][bass.ds(layer, 1)].rearrange("l (kt p) c -> p (l kt) c", p=P)),
                         (up_kv, a["w_mla_kv_up"][bass.ds(layer, 1)].rearrange("l p c -> p (l c)")),
                         (trig, nc.inline_tensor(rope_tables(), "rope_tables_one").ap()),
                         (turn, nc.inline_tensor(rotation(32, [0], 16), "rope_turn_one").ap()),
                         (gain[:, 0:2], a["mla_q_norm_g"][bass.ds(layer, 1)].rearrange("l (kt p) -> p (l kt)", p=P)),
                         (gain[:, 2:3], a["mla_kv_norm_g"][bass.ds(layer, 1)].rearrange("l p -> p l"))]
                for dst, src in loads:
                    sp.dma_start(dst, src).then_inc(here, 16)
                sp.wait_ge(here, 16 * len(loads))

        groups = []
        for t in range(NT):
            def keep(ps, t=t):
                nc.scalar.activation(squares[:, t, 0:256], ps[:, 0:256], ACT.Square, accum_out=sums[:, t, 0:1])
                nc.scalar.activation(squares[:, t, 256:384], ps[:, 256:384], ACT.Square, accum_out=sums[:, t, 1:2])
                return nc.scalar.copy(low[:, t, :], ps)
            groups.append((C_LOW, (0, P, RANKS), over_columns(C_LOW, t, 0, RANKS), "act", keep))
        for half in range(2):
            groups.append((C_LOW, (64, 96, HALF), over_tokens(C_LOW, 384, 32, half), "dve",
                           moving(nc, "dve", kr[:, half * HALF:(half + 1) * HALF])))
        project_stage(k, "latent_project", groups, W)

        st = Stage(k, "latent_norm")
        step, added, rooted = st.sem("dve_step"), st.sem("mean_ready"), st.sem("root_ready")
        with nc.Block() as block:
            @block.sync
            def _(sp):
                st.clear_previous(sp)

            @block.vector
            def _(dve):
                nc.vector.tensor_scalar(sums[:, :, 0], sums[:, :, 0], 1.0 / 256, RMS_EPS, ALU.mult, ALU.add)
                nc.vector.tensor_scalar(sums[:, :, 1], sums[:, :, 1], 1.0 / 128, RMS_EPS, ALU.mult, ALU.add).then_inc(added, 1)
                dve.wait_ge(rooted, 1)
                nc.vector.reciprocal(sums, sums).then_inc(step, 1)
                dve.wait_ge(step, 1)
                for t in range(NT):
                    nc.vector.tensor_scalar_mul(low[:, t, 0:256], low[:, t, 0:256], sums[:, t, 0:1])
                    last = nc.vector.tensor_scalar_mul(low[:, t, 256:384], low[:, t, 256:384], sums[:, t, 1:2])
                last.then_inc(step, 1)

            @block.scalar
            def _(act):
                act.wait_ge(added, 1)
                nc.scalar.activation(sums, sums, ACT.Sqrt).then_inc(rooted, 1)
        transpose_stage(k, "turn_latents", lambda t: low[:, t, :], low_t, 3, scale=gain)

        groups = []
        for h in range(4):
            for half in range(2):
                s = slice(half * HALF, (half + 1) * HALF)
                groups.append((None, (0, 96, HALF), [(up_q[:, i, 96 * h:96 * h + 96], low_t[:, i, s]) for i in range(2)],
                               "dve", moving(nc, "dve", qt[0:96, h, s])))
                groups.append((None, (0, 64, HALF), [(up_kv[:, 128 * h:128 * h + 64], low_t[:, 2, s])],
                               "act", moving(nc, "act", kt[0:64, h, s])))
        for t in range(NT):
            vals = up_kv.rearrange("p (h c) -> p h c", h=4)[:, :, 64:128]
            groups.append((None, (0, P, 256), [(low_t[:, 2, t * P:(t + 1) * P], vals)], "act", moving_values(nc, "act", place(t, 0, 2))))
        project_stage(k, "latent_up", groups)

        st = Stage(k, "mla_rope")
        products, step, shared, cos_done, freed = (st.sem(n) for n in ("turned_rows", "dve_step", "key_ready", "cos_done", "freed"))
        heads = [kr] + [qt[64:96, h, :] for h in range(4)]
        sine = b.scratch[64:96, 3, :]
        with nc.Block() as block:
            @block.sync
            def _(sp):
                st.clear_previous(sp)

            @block.tensor
            def _(pe):
                for i, rows_ in enumerate(heads):
                    for half in range(2):
                        s = slice(half * HALF, (half + 1) * HALF)
                        if i >= 3:
                            pe.wait_ge(freed, i - 2)
                        mm = nc.tensor.matmul(k.psum[64:96, 2 * (i % 3) + half, :], turn, rows_[:, s], start=True, stop=True)
                    mm.then_inc(products, 1)

            @block.vector
            def _(dve):
                for i, rows_ in enumerate(heads):
                    dve.wait_ge(products, i + 1)
                    banks = k.psum[64:96, 2 * (i % 3):2 * (i % 3) + 2, :].rearrange("p b n -> p (b n)")
                    nc.vector.tensor_tensor(sine, banks, trig[:, 1, :], ALU.mult).then_inc(freed, 1)
                    dve.wait_ge(freed, i + 1)
                    nc.vector.tensor_tensor(rows_, rows_, trig[:, 0, :], ALU.mult).then_inc(cos_done, 1)
                    dve.wait_ge(cos_done, i + 1)
                    nc.vector.tensor_tensor(rows_, rows_, sine, ALU.add).then_inc(step if i else shared, 1)
                    dve.wait_ge(step if i else shared, max(i, 1))

            @block.scalar
            def _(act):
                act.wait_ge(shared, 1)
                for h in range(4):
                    nc.scalar.copy(kt[64:96, h, :], kr)


def gate_stage(k, b, W, C_GATE, over_tokens):
    nc = k.nc
    mixed = b.mixed
    st = Stage(k, "gate")
    products, sigmoid, gated, step = (st.sem(n) for n in ("products_done", "sigmoid_ready", "gated", "dve_step"))
    sig = b.scratch
    n_groups = 2 * NT
    with nc.Block() as block:
        @block.sync
        def _(sp):
            st.clear_previous(sp)
            for n in range(2):
                sp.wait_ge(products, NT * (n + 1))
                W.load(sp, C_GATE + 2 + n)

        @block.tensor
        def _(pe):
            for g in range(n_groups):
                n, t = g // NT, g % NT
                if t == 0:
                    pe.wait_ge(W.loaded[C_GATE + n], 16)
                if g >= 4:
                    pe.wait_ge(gated, g - 3)
                gemm(nc, k.bank(g % 4), over_tokens(C_GATE + n, t // 2 * P, P, t % 2)).then_inc(products, 1)

        @block.scalar
        def _(act):
            for g in range(n_groups):
                act.wait_ge(products, g + 1)
                if g >= 4:
                    act.wait_ge(step, g - 3)
                nc.scalar.activation(sig[:, g % 4, 0:HALF], k.bank(g % 4), ACT.Sigmoid).then_inc(sigmoid, 1)

        @block.vector
        def _(dve):
            for g in range(n_groups):
                n, t = g // NT, g % NT
                s = sig[:, g % 4, 0:HALF]
                part = mixed[:, 4 * n + t // 2, t % 2 * HALF:(t % 2 + 1) * HALF]
                dve.wait_ge(sigmoid, g + 1)
                nc.vector.tensor_tensor(s, s, k.bank(g % 4), ALU.mult).then_inc(gated, 1)
                dve.wait_ge(gated, g + 1)
                nc.vector.tensor_tensor(part, part, s, ALU.mult).then_inc(step, 1)



CHUNK = 64
NCH = S // CHUNK
PAIRS = D // P
ATT = 768
O_RWKV = 3 * ATT
O_LOW = O_RWKV + 3 * D
O_GA = O_LOW + 256
O_GR = O_GA + D
LEVELS = (1, 2, 4, 8, 16, 32)
TWO_PI = 2 * np.pi
ROUND = 1.5 * 2.0 ** 23


def window_masks():
    q, key = np.arange(P)[:, None], np.arange(P)[None, :]

    def mask(ok):
        return np.where(ok, 0.0, MASKED)
    same16, same4 = (q - key) % 16 == 0, (q - key) % 4 == 0
    parts = [mask(same16)] * 7 + [mask(same16 & (key <= q)), mask(key >= q), mask(key <= q)]
    parts += [mask(same4)] * 3 + [mask(same4 & (key <= q)), mask(same4 & (key >= q))]
    return np.concatenate(parts, 1).astype(np.float32)


def constants_two():
    turn = rotation(P, [0, 64], 8)
    ones = np.kron(np.eye(2), np.ones((64, 64)))
    a, b = np.arange(64)[:, None], np.arange(64)[None, :]
    tri = np.concatenate([a < b, a <= b], 1)
    cols = [tri, np.eye(64)]
    for m in LEVELS:
        cols.append((a // (2 * m) == b // (2 * m)) & ((a // m) % 2 == 1) & ((b // m) % 2 == 0))
    cols = np.tile(np.concatenate([c.astype(np.float32) for c in cols], 1), (2, 1))
    freq = (500000.0 ** (-np.arange(8, dtype=np.float32) * 2.0 / 16)).astype(np.float32)
    column = np.tile(np.concatenate([freq, freq, np.zeros(48, np.float32)]), 2)[:, None]
    return np.concatenate([turn, ones, cols, column], 1).astype(np.float32)


class Chain:

    def __init__(self, st, eng, name):
        self.sem, self.eng, self.n = st.sem(name), eng, 0

    def __call__(self, ins):
        self.n += 1
        ins.then_inc(self.sem, 1)
        self.eng.wait_ge(self.sem, self.n)


def rms_scale_stage(k, name, src, junk, eps, then):
    nc = k.nc
    st = Stage(k, name)
    summed, added, rooted = st.sem("squares_summed"), st.sem("mean_ready"), st.sem("root_ready")
    with nc.Block() as block:
        @block.sync
        def _(sp):
            st.clear_previous(sp)

        @block.scalar
        def _(act):
            for t in range(NT):
                last = nc.scalar.activation(junk[:, t, :], src[:, t, :], ACT.Square, accum_out=k.root[:, t:t + 1])
            last.then_inc(summed, 1)
            act.wait_ge(added, 1)
            nc.scalar.activation(k.root[:], k.root[:], ACT.Sqrt).then_inc(rooted, 1)

        @block.vector
        def _(dve):
            chain = Chain(st, dve, "dve_step")
            dve.wait_ge(summed, 1)
            nc.vector.tensor_scalar(k.root[:], k.root[:], 1.0 / D, eps, ALU.mult, ALU.add).then_inc(added, 1)
            dve.wait_ge(rooted, 1)
            chain(nc.vector.reciprocal(k.root[:], k.root[:]))
            for t in range(NT):
                then(t, chain)


def second_block(k, a, out):
    nc = k.nc
    w_in = a["w_in_2"][0].rearrange("(kt p) c -> p kt c", p=P)
    with ExitStack() as own:
        k.c2 = k.sb("tables_two", [P, 128 + 128 + 128 + 64 + 6 * 64 + 1], ctx=own)
        k.turn, k.head_ones = k.c2[:, 0:128], k.c2[:, 128:256]
        k.tri = k.c2[:, 256:384]
        k.eye64 = k.c2[:, 384:448]
        k.level = [k.c2[:, 448 + 64 * i:512 + 64 * i] for i in range(6)]
        k.freq = k.c2[:, 832:833]
        vec = k.sb("vectors_by_channel", [P, 98], ctx=own)
        k.x_home = nc.dram_tensor("x_waiting", (P, NT, D), F32, kind="Internal").ap()
        k.x_away, k.x_back = k.sem("x_stored"), k.sem("x_loaded")
        mod = k.sb("modulation_by_channel", [P, 4, 8], ctx=own)
        post = k.sb("post_norm_rows", [P, 2, D], ctx=own)
        modulation_stages(k, a, vec, mod, post)

        with ExitStack() as merged_scope:
            oat = k.sb("attention_out_channel_major", [P, 2, S], ctx=merged_scope)
            with ExitStack() as att_scope:
                windows(k, a, w_in, mod, oat, att_scope)
            ort = k.sb("rwkv_out_channel_major", [P, PAIRS, S], ctx=merged_scope)
            with ExitStack() as rwkv_scope:
                rwkv(k, a, w_in, vec, ort, rwkv_scope)
            merged = k.sb("merged", [P, NT, D], ctx=merged_scope)
            with ExitStack() as scope:
                branches(k, a, w_in, oat, ort, merged, scope)
            transpose_stage(k, "turn_merged", lambda t: merged[:, t, :], k.ht, KT)
            wbuf = [ort[:, 4 * i:4 * i + 4, :].rearrange("p a s -> p (a s)").rearrange("p (a s) -> p a s", a=8) for i in range(2)]
            post_project(k, a["w_out_2"][0], wbuf, merged, post[:, 0, :])
        feed_forward(k, a, mod, post)

        st = Stage(k, "store")
        stored = st.sem("stored")
        with nc.Block() as block:
            @block.sync
            def _(sp):
                st.clear_previous(sp)
                sp.dma_start(out[0].rearrange("(t p) d -> p t d", p=P), k.x[:]).then_inc(stored, 16)
                sp.wait_ge(stored, 16)


def modulation_stages(k, a, vec, mod, post):
    nc = k.nc
    with ExitStack() as own:
        rows_a = k.sb("vector_rows", [98, P], ctx=own)
        rows_b = k.sb("condition_rows", [56, P], ctx=own)
        cond = k.sb("condition_by_channel", [P, 56], ctx=own)
        spread = k.sb("condition_spread", [P, KT, P], ctx=own)
        sig = k.sb("condition_sigmoid", [P, KT], ctx=own)
        gate_bias = k.sb("gate_bias_rows", [P, 4, D], ctx=own)
        wbuf = [k.sb(f"ada_weights_{i}", [P, KT, HALF], ctx=own) for i in range(2)]
        ada = a["ada_w_2"][0].rearrange("(kt p) c -> p kt c", p=P)
        W = Weights(k, wbuf, "ada", [ada[:, :, i * HALF:(i + 1) * HALF] for i in range(12)])

        st = Stage(k, "vectors")
        here, turned, moved, silu = (st.sem(n) for n in ("arrived", "turned", "moved", "sigmoid_ready"))
        with nc.Block() as block:
            @block.sync
            def _(sp):
                st.clear_previous(sp)
                loads = [(k.c2[:], nc.inline_tensor(constants_two(), "constants_two").ap())]
                mu = a["shift_mu_2"][0].rearrange("(r c) -> r c", c=P)
                names = ("norm_mix_pre_2", "norm_ffn_pre_2", None, "decay_w0_2", "iclr_a0_2", "k_k_2", "k_a_2", None,
                         "gn_w_2", "gn_b_2")
                row = 0
                for name in names:
                    if name is None and row == 16:
                        loads.append((rows_a[16:40, :], mu[0:24, :]))
                        row = 40
                        continue
                    src = a[name][0].rearrange("(r c) -> r c", c=P) if name else \
                        a["r_k_2"][0].rearrange("(r two) c -> r (two c)", two=2)
                    loads.append((rows_a[row:row + 8, :], src))
                    row += 8
                loads.append((rows_a[96:98, :], mu[24:26, :]))
                loads.append((rows_b[0:48, :], a["ada_b_2"][0].rearrange("(r c) -> r c", c=P)))
                loads.append((rows_b[48:56, :], a["c_2"][0].rearrange("(r c) -> r c", c=P)))
                for i, part in enumerate((2, 5)):
                    loads.append((gate_bias[:, i, :], a["ada_b_2"][0, part * D:(part + 1) * D].partition_broadcast(P)))
                for i, name in enumerate(("norm_mix_post_2", "norm_ffn_post_2")):
                    loads.append((gate_bias[:, 2 + i, :], a[name][0].partition_broadcast(P)))
                for dst, src in loads:
                    sp.dma_start(dst, src).then_inc(here, 16)
                W.load(sp, 0)
                W.load(sp, 1)
                sp.dma_start(k.x_home, k.x[:]).then_inc(k.x_away, 16)
                st.loads = len(loads)
                sp.wait_ge(here, 16 * len(loads))

            @block.tensor
            def _(pe):
                pe.wait_ge(here, 16 * st.loads)
                nc.tensor.transpose(k.psum[:, 0, 0:98], rows_a[:], k.ident[0:98, 0:98]).then_inc(turned, 1)
                nc.tensor.transpose(k.psum[:, 1, 0:56], rows_b[:], k.ident[0:56, 0:56]).then_inc(turned, 1)

            @block.vector
            def _(dve):
                dve.wait_ge(turned, 2)
                nc.vector.tensor_copy(vec[:], k.psum[:, 0, 0:98])
                nc.vector.tensor_copy(cond[:], k.psum[:, 1, 0:56]).then_inc(moved, 1)
                dve.wait_ge(silu, 1)
                chain = Chain(st, dve, "dve_step")
                chain(nc.vector.tensor_tensor(sig[:], sig[:], cond[:, 48:56], ALU.mult))
                nc.vector.tensor_copy(spread[:], sig[:].unsqueeze(2).broadcast_to([P, KT, P]))

            @block.scalar
            def _(act):
                act.wait_ge(moved, 1)
                nc.scalar.activation(sig[:], cond[:, 48:56], ACT.Sigmoid).then_inc(silu, 1)

        st = Stage(k, "modulation")
        products, evacuated = st.sem("products_done"), st.sem("evacuated")
        with nc.Block() as block:
            @block.sync
            def _(sp):
                st.clear_previous(sp)
                for c in range(2, 12):
                    sp.wait_ge(products, c - 1)
                    W.load(sp, c)

            @block.tensor
            def _(pe):
                for c in range(12):
                    pe.wait_ge(W.loaded[c], 16)
                    if c >= 4:
                        pe.wait_ge(evacuated, c - 3)
                    if c // 2 in (2, 5):
                        gemm(nc, k.bank(c % 4), [(spread[:, i, :], W.view(c)[:, i, :]) for i in range(KT)]).then_inc(products, 1)
                    else:
                        for j in range(4):
                            mm = gemm(nc, k.psum[:, c % 4, j:j + 1],
                                      [(W.view(c)[:, i, j * P:(j + 1) * P], sig[:, i:i + 1]) for i in range(KT)])
                        mm.then_inc(products, 1)

            @block.vector
            def _(dve):
                chain = Chain(st, dve, "dve_step")
                slot = {0: 0, 1: 1, 3: 2, 4: 3}
                for c in range(12):
                    part, half = c // 2, c % 2
                    dve.wait_ge(products, c + 1)
                    if part in (2, 5):
                        i = 0 if part == 2 else 1
                        s = slice(half * HALF, (half + 1) * HALF)
                        ins = nc.vector.tensor_tensor(post[:, i, s], k.bank(c % 4), gate_bias[:, i, s], ALU.add)
                    else:
                        ins = nc.vector.tensor_tensor(mod[:, slot[part], 4 * half:4 * half + 4], k.psum[:, c % 4, 0:4],
                                                      cond[:, 8 * part + 4 * half:8 * part + 4 * half + 4], ALU.add)
                    ins.then_inc(evacuated, 1)
                dve.wait_ge(evacuated, 12)
                for i in range(2):
                    nc.vector.tensor_tensor(post[:, i, :], post[:, i, :], gate_bias[:, 2 + i, :], ALU.mult)
                    last = nc.vector.scalar_tensor_tensor(mod[:, 2 * i + 1, :], mod[:, 2 * i + 1, :], 1.0,
                                                          vec[:, 8 * i:8 * i + 8], ALU.add, ALU.mult)
                chain(last)
    loop_edge(k, [W])


def windows(k, a, w_in, mod, oat, scope):
    nc = k.nc
    qk = k.sb("window_queries_keys", [P, 12, S], ctx=scope)
    place, beside, _, ones = value_views(k.sb("window_values", [P, NT * 6 * 192], ctx=scope), 6)
    trig = k.x[:, 6:8, :]
    wbuf = [k.sb(f"window_weights_{i}", [P, KT, HALF], ctx=scope) for i in range(2)]
    W = Weights(k, wbuf, "window_w", [w_in[:, :, c:min(c + HALF, 3 * ATT)] for c in range(0, 3 * ATT, HALF)])

    scaled = qk[:, 0:8, :]
    rms_scale_stage(k, "norm_mix", k.x, scaled, 1e-6,
                    lambda t, chain: nc.vector.tensor_scalar_mul(scaled[:, t, :], k.x[:, t, :], k.root[:, t:t + 1]))
    transpose_stage(k, "turn_mix", lambda t: scaled[:, t, :], k.ht, KT, scale=mod[:, 1, :], shift=mod[:, 0, :])

    raw = qk[:, 0, :]
    angle, turns, t2 = qk[:, 1, :], qk[:, 2, :], qk[:, 3, :]
    st = Stage(k, "window_trig")
    here, sin_in, cos_in, cast = st.sem("arrived"), st.sem("sine_argument"), st.sem("cosine_argument"), st.sem("cast")
    parts = [6.28125, 0.00193500518798828125]
    parts.append(TWO_PI - sum(parts))
    with nc.Block() as block:
        @block.sync
        def _(sp):
            st.clear_previous(sp)
            sp.dma_start(raw.bitcast(I32), a["positions_2"][0].partition_broadcast(P)).then_inc(here, 16)
            W.load(sp, 0)
            W.load(sp, 1)

        @block.vector
        def _(dve):
            chain = Chain(st, dve, "dve_step")
            nc.vector.memset(ones, 1.0)
            dve.wait_ge(k.x_away, 16)
            dve.wait_ge(here, 16)
            chain(nc.vector.tensor_copy(t2, raw.bitcast(I32)))
            chain(nc.vector.tensor_scalar(angle, t2, k.freq, None, ALU.mult))
            chain(nc.vector.tensor_scalar(turns, angle, 1 / TWO_PI, ROUND, ALU.mult, ALU.add))
            chain(nc.vector.tensor_scalar(turns, turns, -ROUND, None, ALU.add))
            for c in parts:
                chain(nc.vector.scalar_tensor_tensor(angle, turns, -c, angle, ALU.mult, ALU.add))
            chain(nc.vector.tensor_scalar(angle, angle, 3.1415925, -3.1415925, ALU.min, ALU.max))
            nc.vector.tensor_copy(trig[:, 1, :], angle).then_inc(sin_in, 1)
            chain(nc.vector.tensor_scalar(t2, angle, float(np.pi / 2), None, ALU.add))
            chain(nc.vector.tensor_scalar(turns, t2, float(np.pi), -TWO_PI, ALU.is_gt, ALU.mult))
            chain(nc.vector.tensor_tensor(t2, t2, turns, ALU.add))
            nc.vector.tensor_scalar(trig[:, 0, :], t2, 3.1415925, -3.1415925, ALU.min, ALU.max).then_inc(cos_in, 1)

        @block.scalar
        def _(act):
            act.wait_ge(sin_in, 1)
            nc.scalar.activation(trig[:, 1, :], trig[:, 1, :], ACT.Sin)
            act.wait_ge(cos_in, 1)
            nc.scalar.activation(trig[:, 0, :], trig[:, 0, :], ACT.Sin)

    groups = []
    for tile in range(12):
        for half in range(2):
            who = "dve" if half else "act"
            s = slice(half * HALF, (half + 1) * HALF)
            c = tile // 4
            groups.append((c, (0, P, HALF), [(W.view(c)[:, i, tile % 4 * P:(tile % 4 + 1) * P], k.ht[:, i, s]) for i in range(KT)],
                           who, moving(nc, who, qk[:, tile, s])))
    for c, col, n in ((3, 0, 512), (4, 512, 256)):
        for t in range(NT):
            who = "dve" if t % 2 else "act"
            groups.append((c, (0, P, n), [(k.ht[:, i, t * P:(t + 1) * P], W.view(c)[:, i, 0:n]) for i in range(KT)],
                           who, moving_values(nc, who, place(t, col // P, (col + n) // P))))
    project_stage(k, "window_project", groups, W, loads=(2, 3, 4))

    st = Stage(k, "window_rope")
    products, read, cosined, step = (st.sem(n) for n in ("turned_rows", "sine_part_ready", "cosine_part_ready", "dve_step"))
    part = [wbuf[0][:, 2 * i:2 * i + 2, :].rearrange("p a s -> p (a s)") for i in range(2)]
    with nc.Block() as block:
        @block.sync
        def _(sp):
            st.clear_previous(sp)
            sp.sem_clear(k.x_away)

        @block.tensor
        def _(pe):
            for i in range(12):
                if i >= 3:
                    pe.wait_ge(read, i - 2)
                for half in range(2):
                    mm = nc.tensor.matmul(k.psum[:, 2 * (i % 3) + half, :], k.turn, qk[:, i, half * HALF:(half + 1) * HALF],
                                          start=True, stop=True)
                mm.then_inc(products, 1)

        @block.gpsimd
        def _(pool):
            nc.gpsimd.memset(k.x[0:64, 0:6, :], 0.0)
            for i in range(12):
                pool.wait_ge(products, i + 1)
                nc.gpsimd.tensor_tensor(qk[:, i, :], qk[:, i, :], trig[:, 0, :], ALU.mult).then_inc(cosined, 1)
            pool.wait_ge(cosined, 12)
            for i in range(6):
                pool.wait_ge(step, i + 1)
                nc.gpsimd.memset(qk[64:P, i, :], 0.0)

        @block.vector
        def _(dve):
            for i in range(12):
                dve.wait_ge(products, i + 1)
                if i >= 2:
                    dve.wait_ge(step, i - 1)
                nc.vector.tensor_tensor(part[i % 2], k.banks2(2 * (i % 3)), trig[:, 1, :], ALU.mult).then_inc(read, 1)
                dve.wait_ge(read, i + 1)
                dve.wait_ge(cosined, i + 1)
                if i < 6:
                    nc.vector.tensor_tensor(qk[0:64, i, :], qk[0:64, i, :], part[i % 2][0:64, :], ALU.add)
                    nc.vector.tensor_tensor(k.x[64:P, i, :], qk[64:P, i, :], part[i % 2][64:P, :], ALU.add).then_inc(step, 1)
                else:
                    nc.vector.tensor_tensor(qk[:, i, :], qk[:, i, :], part[i % 2], ALU.add).then_inc(step, 1)

    masks_row = trig.rearrange("p a s -> p (a s)")[:, 0:15 * P]
    st = Stage(k, "window_masks")
    here = st.sem("arrived")
    with nc.Block() as block:
        @block.sync
        def _(sp):
            st.clear_previous(sp)
            sp.dma_start(masks_row, nc.inline_tensor(window_masks(), "window_masks").ap()).then_inc(here, 16)
            sp.wait_ge(here, 16)

    def plan(t):
        runs = [(2, 0, t + 1), (0, max(t - 1, 0), min(t, 1) + 1), (1, max(t - 3, 0), min(t, 3) + 1)]
        return runs + ([(1, t - 4, 1)] if t >= 4 else [])

    def masks(t):
        wide = (t + 1) * P
        near = (min(t, 1) + 1) * P
        mid = (min(t, 3) + 1 + (t >= 4)) * P
        out = [(0, wide, masks_row[:, (7 - t) * P:8 * P]),
               (wide, near, masks_row[:, (8 if t else 9) * P:10 * P]),
               (wide + near, mid, masks_row[:, (13 - min(t, 3)) * P:(14 + (t >= 4)) * P])]
        if t >= 4:
            return [(0, wide + near + mid, masks_row[:, (7 - t) * P:15 * P])]
        return out

    buf = Buffers()
    buf.weights = [wbuf[0][:].rearrange("p a s -> p (a s)")[:, i * 2048:(i + 1) * 2048] for i in range(2)]
    buf.turned = [wbuf[1][:].rearrange("p a s -> p (a s)")[:, i * 2048:(i + 1) * 2048] for i in range(2)]
    buf.nw = 2

    def query(h, g, t):
        head = 4 * g + h
        return (k.x if head % 2 else qk)[:, head // 2, t * P:(t + 1) * P]

    attention_stage(k, "window", buf, query,
                    lambda h, g, c0, c1: qk[:, 6 + (4 * g + h) // 2, c0:c1],
                    lambda h, g, b: beside(4 * g + h, b),
                    lambda h, t: oat[64 * (h % 2):64 * (h % 2) + 64, h // 2, t * P:(t + 1) * P], 4, plan, masks, 0.125)
    loop_edge(k, [W])


def rwkv(k, a, w_in, vec, ort, scope):
    nc = k.nc
    low = k.sb("low_rank", [P, 2, S], ctx=scope)
    wr = k.sb("pair_weights", [P, 3, KT, P], ctx=scope)
    wl = k.sb("pair_low_weights", [P, 2, P], ctx=scope)
    raw = k.sb("unshifted", [P, 4 + S], ctx=scope)
    pv = k.sb("pair_vectors", [P, 16], ctx=scope)
    tiles = k.sb("pair_tiles", [P, 11, S], ctx=scope)
    b = [tiles[:, i, :] for i in range(11)]
    ar = k.sb("decayed_a_and_r", [P, NCH, 2, CHUNK], ctx=scope)
    lb = k.sb("a_and_r_by_b", [P, NCH, 2, CHUNK], ctx=scope)
    lk = tiles[:, 9:11, :].rearrange("p q (n a c) -> p (q n) a c", a=2, c=CHUNK)
    state = k.sb("state", [P, 2, CHUNK], ctx=scope)
    small = k.sb("x_and_u", [P, 2, CHUNK], ctx=scope)
    k_loaded = k.sem("pair_weights_loaded")

    def by_chunk(t):
        return t.rearrange("p (n c) -> p n c", c=CHUNK)

    def load_pair(sp, p):
        for j in range(3):
            sp.dma_start(wr[:, j, :, :], w_in[:, :, bass.ds(p * P + (O_RWKV + j * D), P)]).then_inc(k_loaded, 16)

    lw = lb[:].rearrange("p n a c -> p (n a c)").rearrange("p (kt c) -> p kt c", c=256)
    st = Stage(k, "low_rank")
    here, products, kept, mixed, act_step = (st.sem(n) for n in ("arrived", "products_done", "raw_kept", "shifted", "act_step"))
    with nc.Block() as block:
        @block.sync
        def _(sp):
            st.clear_previous(sp)
            sp.dma_start(lw, w_in[:, :, O_LOW:O_LOW + 256]).then_inc(here, 16)
            load_pair(sp, 0)

        @block.tensor
        def _(pe):
            pe.wait_ge(here, 16)
            for j in range(2):
                for half in range(2):
                    mm = gemm(nc, k.bank(2 * j + half), [(lw[:, i, j * P:(j + 1) * P], k.ht[:, i, half * HALF:(half + 1) * HALF])
                                                        for i in range(KT)])
                mm.then_inc(products, 1)

        @block.scalar
        def _(act):
            for j in range(2):
                act.wait_ge(products, j + 1)
                if j:
                    act.wait_ge(mixed, 1)
                nc.scalar.copy(raw[:, 4:4 + S], k.banks2(2 * j)).then_inc(kept, 1)
            act.wait_ge(mixed, 2)
            nc.scalar.activation(low[0:64, 0, :], low[0:64, 0, :], ACT.Tanh)
            nc.scalar.activation(low[:, 1, :], low[:, 1, :], ACT.Sigmoid)

        @block.vector
        def _(dve):
            chain = Chain(st, dve, "dve_step")
            nc.vector.memset(raw[:, 0:4], 0.0)
            for j in range(2):
                mu = vec[:, 96 + j:97 + j]
                chain(nc.vector.tensor_scalar(pv[:, 15:16], mu, -1.0, 1.0, ALU.mult, ALU.add))
                dve.wait_ge(kept, j + 1)
                chain(nc.vector.tensor_scalar_mul(low[:, j, :], raw[:, 4:4 + S], pv[:, 15:16]))
                nc.vector.scalar_tensor_tensor(low[:, j, :], raw[:, 3:3 + S], mu, low[:, j, :], ALU.mult, ALU.add).then_inc(mixed, 1)
                dve.wait_ge(mixed, j + 1)
    loop_edge(k)

    with nc.Fori(0, PAIRS) as p:
        pair_body(k, a, p, dict(low=low, wr=wr, wl=wl, raw=raw, pv=pv, b=b, ar=ar, lb=lb, lk=lk, state=state,
                                small=small, loaded=k_loaded, load=load_pair, by_chunk=by_chunk, vec=vec, ort=ort))
    st = Stage(k, "pair_end")
    with nc.Block() as block:
        @block.sync
        def _(sp):
            sp.wait_ge(k_loaded, 48)
            sp.sem_clear(k_loaded)


def pair_body(k, a, p, t):
    nc = k.nc
    low, wr, wl, raw, pv, b = t["low"], t["wr"], t["wl"], t["raw"], t["pv"], t["b"]
    ar, lb, lk, state, small = t["ar"], t["lb"], t["lk"], t["state"], t["small"]
    by_chunk = t["by_chunk"]
    (MU_R, MU_K, MU_V, W0, A0, KK, KA, RK, GW, GB, KEEP_R, KEEP_K, KEEP_V) = (pv[:, i:i + 1] for i in range(13))
    vec = t["vec"]

    st = Stage(k, "pair_project")
    products, kept, part, shifted, vectors, here = (
        st.sem(n) for n in ("products_done", "raw_kept", "kept_part_ready", "shifted", "vectors_ready", "arrived"))
    first, second = (0, 2, 4), (6, 0)
    with nc.Block() as block:
        @block.sync
        def _(sp):
            sp.dma_start(wl[0:64, 0, :], a["decay_w2_2"][0][:, bass.ds(p * P, P)]).then_inc(here, 16)
            sp.dma_start(wl[64:128, 0, :], a["iclr_a2_2"][0][:, bass.ds(p * P, P)]).then_inc(here, 16)
            sp.dma_start(wl[:, 1, :], a["gate_g2_2"][0][:, bass.ds(p * P, P)]).then_inc(here, 16)
            sp.wait_ge(here, 48)

        @block.tensor
        def _(pe):
            pe.wait_ge(t["loaded"], 48)
            for j in range(3):
                for half in range(2):
                    mm = gemm(nc, k.bank(first[j] + half), [(wr[:, j, i, :], k.ht[:, i, half * HALF:(half + 1) * HALF])
                                                           for i in range(KT)])
                mm.then_inc(products, 1)
            pe.wait_ge(here, 48)
            for j in range(2):
                if j:
                    pe.wait_ge(kept, 1)
                    pe.wait_ge(part, 1)
                r0 = 64 * j
                for half in range(2):
                    mm = nc.tensor.matmul(k.bank(second[j] + half), wl[r0:r0 + 64, 0, :],
                                          low[r0:r0 + 64, 0, half * HALF:(half + 1) * HALF], start=True, stop=True)
                mm.then_inc(products, 1)

        @block.vector
        def _(dve):
            chain = Chain(st, dve, "dve_step")
            table = vec[:, 16:96].rearrange("p (j q) -> p j q", q=8)
            chain(nc.vector.tensor_copy(pv[:, 0:10].unsqueeze(2), table[:, :, bass.ds(p, 1)]))
            nc.vector.tensor_scalar(pv[:, 10:13], pv[:, 0:3], -1.0, 1.0, ALU.mult, ALU.add).then_inc(vectors, 1)
            dve.wait_ge(vectors, 1)
            for j in range(3):
                dve.wait_ge(products, j + 1)
                nc.vector.tensor_scalar_mul(b[j], k.banks2(first[j]), (KEEP_R, KEEP_K, KEEP_V)[j]).then_inc(part, 1)
                dve.wait_ge(part, j + 1)
                dve.wait_ge(kept, j + 1)
                nc.vector.scalar_tensor_tensor(b[j], raw[:, 3:3 + S], (MU_R, MU_K, MU_V)[j], b[j],
                                               ALU.mult, ALU.add).then_inc(shifted, 1)

        @block.scalar
        def _(act):
            for j in range(3):
                act.wait_ge(products, j + 1)
                act.wait_ge(part, j + 1)
                if j:
                    act.wait_ge(shifted, j)
                nc.scalar.copy(raw[:, 4:4 + S], k.banks2(first[j])).then_inc(kept, 1)
            for j in range(2):
                act.wait_ge(products, 4 + j)
                nc.scalar.activation(b[3 + j], k.banks2(second[j]), ACT.Sigmoid, bias=(W0, A0)[j])

    st = Stage(k, "pair_prepare")
    names = ("logs_ready", "decays_ready", "squares_ready", "norms_done", "bonus_ready", "bonus_done", "clamped", "root_ready")
    logs, decays, squares, norms, bonus_in, bonus_done, clamped, rooted = (st.sem(n) for n in names)
    last_decay = by_chunk(b[6])[:, :, 63:64].broadcast_to([P, NCH, CHUNK])
    with nc.Block() as block:
        @block.sync
        def _(sp):
            st.clear_previous(sp)
            sp.sem_clear(t["loaded"])

        @block.scalar
        def _(act):
            chain = Chain(st, act, "act_step")
            act.wait_ge(logs, 1)
            nc.scalar.activation(b[6], b[5], ACT.Exp, scale=-E_HALF)
            chain(nc.scalar.activation(b[9], b[9], ACT.Exp, scale=-E_HALF))
            nc.scalar.activation(b[5], b[5], ACT.Exp, scale=E_HALF).then_inc(decays, 1)
            act.wait_ge(clamped, 1)
            nc.scalar.activation(b[10], b[10], ACT.Sqrt).then_inc(rooted, 1)

        @block.tensor
        def _(pe):
            for i, (ready, done, src) in enumerate(((squares, norms, b[10]), (bonus_in, bonus_done, b[8]))):
                pe.wait_ge(ready, 1)
                for half in range(2):
                    mm = nc.tensor.matmul(k.bank(2 * i + half), k.head_ones, src[:, half * HALF:(half + 1) * HALF],
                                          start=True, stop=True)
                mm.then_inc(done, 1)

        @block.vector
        def _(dve):
            chain = Chain(st, dve, "dve_step")
            one = k.one[:, 0:1].broadcast_to([P, CHUNK])
            for n in range(NCH):
                s = slice(n * CHUNK, (n + 1) * CHUNK)
                last = nc.vector.tensor_tensor_scan(b[5][:, s], one, b[3][:, s], 0.0, ALU.mult, ALU.add)
            chain(last)
            nc.vector.tensor_tensor(b[9], b[5], b[3], ALU.subtract).then_inc(logs, 1)
            chain(nc.vector.tensor_scalar_mul(b[7], b[1], KK))
            nc.vector.tensor_tensor(b[10], b[7], b[7], ALU.mult).then_inc(squares, 1)
            chain(nc.vector.tensor_scalar(b[8], b[4], -1.0, KA, ALU.add, ALU.mult))
            chain(nc.vector.scalar_tensor_tensor(b[1], b[8], 1.0, b[1], ALU.add, ALU.mult))
            nc.vector.scalar_tensor_tensor(b[8], b[0], RK, b[1], ALU.mult, ALU.mult).then_inc(bonus_in, 1)
            dve.wait_ge(norms, 1)
            nc.vector.tensor_scalar_max(b[10], k.banks2(0), 1e-24).then_inc(clamped, 1)
            dve.wait_ge(bonus_done, 1)
            nc.vector.tensor_tensor(b[8], k.banks2(2), b[2], ALU.mult)
            dve.wait_ge(decays, 1)
            nc.vector.tensor_tensor(ar[:, :, 1, :], by_chunk(b[0]), by_chunk(b[6]), ALU.mult)
            dve.wait_ge(logs, 1)
            chain(nc.vector.tensor_tensor(b[3], b[1], b[5], ALU.mult))
            dve.wait_ge(rooted, 1)
            chain(nc.vector.reciprocal(b[10], b[10]))
            chain(nc.vector.tensor_tensor(b[7], b[7], b[10], ALU.mult))
            chain(nc.vector.scalar_tensor_tensor(ar[:, :, 0, :], by_chunk(b[7]), -1.0, by_chunk(b[9]), ALU.mult, ALU.mult))
            chain(nc.vector.tensor_tensor(b[7], b[7], b[4], ALU.mult))
            chain(nc.vector.tensor_tensor(b[4], b[7], b[5], ALU.mult))
            nc.vector.tensor_tensor(by_chunk(b[9]), by_chunk(b[4]), last_decay, ALU.mult)
            nc.vector.tensor_tensor(by_chunk(b[10]), by_chunk(b[3]), last_decay, ALU.mult)

    ends = raw[:, 4:4 + NCH]
    st = Stage(k, "pair_turn")
    turned, used = st.sem("turned"), st.sem("copied")
    sources = (b[2], b[9], b[10])
    dests = (b[0], b[1], b[5])
    with nc.Block() as block:
        @block.sync
        def _(sp):
            st.clear_previous(sp)
            t["load"](sp, p + 1)

        @block.tensor
        def _(pe):
            for j in range(3):
                for m in range(8):
                    mm = nc.tensor.transpose(k.psum[:, 2 * j + m // 4, (m % 4) * P:(m % 4 + 1) * P],
                                             sources[j][:, m * P:(m + 1) * P], k.ident)
                mm.then_inc(turned, 1)

        def quadrants(j):
            banks = k.psum[:, 2 * j:2 * j + 2, :].rearrange("p b (m c) -> p (b m) c", c=P)
            for parity in range(2):
                for h in range(2):
                    dst = dests[j][64 * h:64 * h + 64, :].rearrange("p (m q c) -> p m q c", q=2, c=CHUNK)[:, :, parity, :]
                    yield dst, banks[64 * parity:64 * parity + 64, :, 64 * h:64 * h + 64]

        @block.vector
        def _(dve):
            nc.vector.tensor_copy(ends, by_chunk(b[6])[:, :, 63])
            for j in (0, 2):
                dve.wait_ge(turned, j + 1)
                for i, (dst, src) in enumerate(quadrants(j)):
                    if j == 0 or i < 2:
                        last = nc.vector.tensor_copy(dst, src)
            last.then_inc(used, 1)

        @block.scalar
        def _(act):
            for j in (1, 2):
                act.wait_ge(turned, j + 1)
                if j == 2:
                    act.wait_ge(used, 1)
                for i, (dst, src) in enumerate(quadrants(j)):
                    if j == 1 or i >= 2:
                        nc.scalar.copy(dst, src)

    st = Stage(k, "pair_products")
    done = st.sem("products_done")
    with nc.Block() as block:
        @block.sync
        def _(sp):
            st.clear_previous(sp)

        @block.tensor
        def _(pe):
            for i, src in enumerate((b[4], b[3])):
                for n in range(NCH):
                    for h in range(2):
                        r = slice(64 * h, 64 * h + 64)
                        mm = nc.tensor.matmul(k.psum[r, 4 * i + n // 4, (n % 4) * P:(n % 4 + 1) * P],
                                              src[r, n * CHUNK:(n + 1) * CHUNK], ar[r, n, :, :].rearrange("p a c -> p (a c)"),
                                              start=True, stop=True)
                    if n % 4 == 3:
                        mm.then_inc(done, 1)

        @block.vector
        def _(dve):
            for i, dst in enumerate((lb, lk)):
                for q in range(4):
                    dve.wait_ge(done, 4 * i + q + 1)
                    nc.vector.tensor_tensor(dst[:, 4 * q:4 * q + 4, :, :].rearrange("p n a c -> p n (a c)"),
                                            k.bank(4 * i + q).rearrange("p (n c) -> p n c", c=P),
                                            k.tri.unsqueeze(1).broadcast_to([P, 4, P]), ALU.mult)

    st = Stage(k, "pair_inverse")
    zdone, zready, tdone, tadded, turned, moved, masked = (
        st.sem(n) for n in ("z_products_done", "z_ready", "t_products_done", "t_added", "turned", "moved", "z_masked"))
    inv, inv_t, z = b[6], b[7], b[2]
    LAST = 5

    def side(x, q):
        return x[:, HALF * q:HALF * (q + 1)].rearrange("p (m i c) -> p m i c", i=2, c=CHUNK)

    def psum_side(first, q):
        return (k.psum[:, first + 2 * q:first + 2 * q + 2, 0:4 * CHUNK]
                .rearrange("p i (m c) -> p m i c", c=CHUNK))

    order = [(i + j, j ^ h) for i in range(0, 8, 2) for h in range(2) for j in range(2)]
    with nc.Block() as block:
        @block.sync
        def _(sp):
            st.clear_previous(sp)

        @block.tensor
        def _(pe):
            def systems(q):
                for i, h in order:
                    n = 8 * q + i
                    at = ((n // 2) * 2 + h) * CHUNK
                    yield (slice(64 * h, 64 * h + 64), slice(64 * (n % 2), 64 * (n % 2) + 64), n,
                           slice(n * CHUNK, (n + 1) * CHUNK), slice(at, at + CHUNK))

            def tile(half, first, second, n, q):
                at = n % 8 // 2 * CHUNK
                return k.psum[half, first + 2 * q + second, at:at + CHUNK]

            def do_z(lev, q):
                if lev:
                    pe.wait_ge(tadded, 2 * (lev - 1) + q + 1)
                for hh, ch, n, cols, tcols in systems(q):
                    if lev:
                        mm = nc.tensor.matmul(tile(ch, 0, hh.start // 64, n, q), lb[hh, n, 0, :], inv[hh, cols],
                                              start=True, stop=True)
                    else:
                        mm = nc.tensor.matmul(tile(hh, 4, n % 2, n, q), lb[hh, n, 0, :], k.eye64[hh, :],
                                              start=True, stop=True)
                mm.then_inc(zdone, 1)

            def do_t(lev, q):
                pe.wait_ge(zready, 2 * (lev - 1) + q + 1)
                pe.wait_ge(moved, 2 * (lev - 1) + q + 1)
                for hh, ch, n, cols, tcols in systems(q):
                    out = tile(hh, 4, n % 2, n, q)
                    lhs, rhs = (inv_t, z) if lev < LAST else (z, inv_t)
                    mm = nc.tensor.matmul(out, lhs[ch, tcols], rhs[ch, tcols], start=True, stop=True)
                mm.then_inc(tdone, 1)

            def do_turn(lev, q):
                pe.wait_ge(tadded, 2 * lev + q + 1)
                for i in range(4):
                    mm = nc.tensor.transpose(k.psum[:, 4 + 2 * q, i * P:(i + 1) * P],
                                             inv[:, HALF * q + i * P:HALF * q + (i + 1) * P], k.ident)
                mm.then_inc(turned, 1)

            for q in range(2):
                do_z(0, q)
            for lev in range(LAST):
                for q in range(2):
                    do_turn(lev, q)
                    do_z(lev + 1, q)
                for q in range(2):
                    do_t(lev + 1, q)

        @block.vector
        def _(dve):
            eye = k.eye64.unsqueeze(1).unsqueeze(1).broadcast_to([P, 4, 2, CHUNK])
            for lev in range(LAST + 1):
                mask = k.level[lev].unsqueeze(1).unsqueeze(1).broadcast_to([P, 4, 2, CHUNK])
                for q in range(2):
                    dve.wait_ge(zdone, 2 * lev + q + 1)
                    if lev == 0:
                        nc.vector.tensor_tensor(side(inv, q), psum_side(4, q), mask, ALU.mult).then_inc(masked, 1)
                        dve.wait_ge(masked, q + 1)
                        nc.vector.tensor_tensor(side(inv, q), side(inv, q), eye, ALU.add).then_inc(tadded, 1)
                    elif lev < LAST:
                        nc.vector.tensor_tensor(side(z, q), psum_side(0, q), mask, ALU.mult).then_inc(zready, 1)
                    else:
                        nc.vector.tensor_tensor(side(z, q), psum_side(0, q), mask, ALU.mult).then_inc(masked, 1)
                        dve.wait_ge(masked, 2 + q + 1)
                        nc.vector.tensor_tensor(side(z, q), side(z, q), eye, ALU.add).then_inc(zready, 1)
                if 0 < lev < LAST:
                    for q in range(2):
                        dve.wait_ge(tdone, 2 * (lev - 1) + q + 1)
                        nc.vector.tensor_tensor(side(inv, q), side(inv, q), psum_side(4, q), ALU.add).then_inc(tadded, 1)

        @block.scalar
        def _(act):
            for lev in range(LAST):
                for q in range(2):
                    act.wait_ge(turned, 2 * lev + q + 1)
                    nc.scalar.copy(inv_t[:, HALF * q:HALF * (q + 1)], k.bank(4 + 2 * q)).then_inc(moved, 1)
            for q in range(2):
                act.wait_ge(tdone, 2 * (LAST - 1) + q + 1)
                nc.scalar.copy(side(inv, q), psum_side(4, q))

    st = Stage(k, "pair_scan")
    names = ("x_done", "x_ready", "u_done", "u_ready", "update_done", "state_ready", "y_done", "y_moved")
    xdone, xready, udone, uready, mdone, mready, ydone, ymoved = (st.sem(n) for n in names)
    vt, bt, kt, inv_t = b[0], b[1], b[5], b[6]
    y = b[3]
    xs, us = small[:, 0, :], small[:, 1, :]
    heads = (slice(0, 64), slice(64, 128))
    with nc.Block() as block:
        @block.sync
        def _(sp):
            st.clear_previous(sp)

        @block.tensor
        def _(pe):
            def product(n, bank, lhs, rhs, at=0, start=False, stop=False):
                for r in heads:
                    mm = nc.tensor.matmul(k.psum[r, bank, at:at + 64], lhs(r), rhs(r), start=start, stop=stop,
                                          skip_group_check=True)
                return mm

            def of(x, n):
                return lambda r: x[r, n * CHUNK:(n + 1) * CHUNK]

            def first_of_x(n):
                product(n, 0, lambda r: lk[r, n, 0, :], of(vt, n), start=True)

            first_of_x(0)
            for n in range(NCH):
                m = lambda r: state[r, n % 2, :]
                out = dict(bank=3 + n // 8, at=(n % 8) * 64)
                pe.wait_ge(mready, n + 1)
                product(n, 0, lambda r: ar[r, n, 0, :], m, stop=True).then_inc(xdone, 1)
                product(n, lhs=m, rhs=lambda r: ar[r, n, 1, :], start=True, **out)
                product(n, lhs=of(vt, n), rhs=lambda r: lk[r, n, 1, :], **out)
                product(n, 2, of(kt, n), of(vt, n), start=True)
                pe.wait_ge(xready, n + 1)
                product(n, 1, of(inv_t, n), lambda r: xs[r, :], start=True, stop=True).then_inc(udone, 1)
                if n + 1 < NCH:
                    first_of_x(n + 1)
                pe.wait_ge(uready, n + 1)
                product(n, 2, of(bt, n), lambda r: us[r, :], stop=True).then_inc(mdone, 1)
                product(n, lhs=lambda r: us[r, :], rhs=lambda r: lb[r, n, 1, :], stop=True, **out).then_inc(ydone, 1)

        @block.vector
        def _(dve):
            nc.vector.memset(state[:, 0, :], 0.0).then_inc(mready, 1)
            for n in range(NCH):
                dve.wait_ge(xdone, n + 1)
                nc.vector.tensor_copy(xs, k.psum[:, 0, 0:64]).then_inc(xready, 1)
                dve.wait_ge(udone, n + 1)
                if n:
                    dve.wait_ge(ydone, n)
                nc.vector.tensor_copy(us, k.psum[:, 1, 0:64]).then_inc(uready, 1)
                dve.wait_ge(mdone, n + 1)
                dve.wait_ge(mready, n + 1)
                nc.vector.scalar_tensor_tensor(state[:, (n + 1) % 2, :], state[:, n % 2, :], ends[:, n:n + 1],
                                               k.psum[:, 2, 0:64], ALU.mult, ALU.add).then_inc(mready, 1)

        @block.scalar
        def _(act):
            for i in range(2):
                act.wait_ge(ydone, 8 * (i + 1))
                nc.scalar.copy(y[:, i * HALF:(i + 1) * HALF], k.bank(3 + i))

    st = Stage(k, "pair_out")
    names = ("means_done", "centred", "squares_ready", "variances_done", "variance_ready", "root_ready", "gate_done")
    means, centred, squares, variances, vready, rooted, gated = (st.sem(n) for n in names)
    ones = k.head_ones
    with nc.Block() as block:
        @block.sync
        def _(sp):
            st.clear_previous(sp)

        @block.tensor
        def _(pe):
            for half in range(2):
                mm = nc.tensor.matmul(k.bank(half), ones, y[:, half * HALF:(half + 1) * HALF], start=True, stop=True)
            mm.then_inc(means, 1)
            for half in range(2):
                mm = nc.tensor.matmul(k.bank(4 + half), wl[:, 1, :], low[:, 1, half * HALF:(half + 1) * HALF], start=True, stop=True)
            mm.then_inc(gated, 1)
            pe.wait_ge(squares, 1)
            for half in range(2):
                mm = nc.tensor.matmul(k.bank(2 + half), ones, b[7][:, half * HALF:(half + 1) * HALF], start=True, stop=True)
            mm.then_inc(variances, 1)

        @block.scalar
        def _(act):
            act.wait_ge(centred, 1)
            nc.scalar.activation(b[7], b[9], ACT.Square).then_inc(squares, 1)
            act.wait_ge(vready, 1)
            nc.scalar.activation(b[6], b[6], ACT.Sqrt).then_inc(rooted, 1)

        @block.vector
        def _(dve):
            chain = Chain(st, dve, "dve_step")
            dve.wait_ge(means, 1)
            nc.vector.scalar_tensor_tensor(b[9], k.banks2(0), -1.0 / 64, y, ALU.mult, ALU.add).then_inc(centred, 1)
            dve.wait_ge(variances, 1)
            nc.vector.tensor_scalar(b[6], k.banks2(2), 1.0 / 64, GN_EPS, ALU.mult, ALU.add).then_inc(vready, 1)
            dve.wait_ge(rooted, 1)
            chain(nc.vector.reciprocal(b[6], b[6]))
            dve.wait_ge(centred, 1)
            chain(nc.vector.tensor_tensor(b[9], b[9], b[6], ALU.mult))
            chain(nc.vector.tensor_scalar(b[9], b[9], GW, GB, ALU.mult, ALU.add))
            chain(nc.vector.tensor_tensor(b[9], b[9], b[8], ALU.add))
            dve.wait_ge(gated, 1)
            nc.vector.tensor_tensor(t["ort"][:, bass.ds(p, 1), :].rearrange("p o s -> p (o s)"), b[9], k.banks2(4), ALU.mult)
    loop_edge(k)


def branches(k, a, w_in, oat, ort, merged, scope):
    nc = k.nc
    C = 256
    wg = [k.sb(f"gate_weights_{i}", [P, KT, 2, C], ctx=scope) for i in range(2)]
    wb = [k.sb(f"branch_weights_{i}", [P, 10, C], ctx=scope) for i in range(2)]
    wbr = a["w_branch_2"][0].rearrange("(kt p) c -> p kt c", p=P)
    st = Stage(k, "branches")
    loaded = [st.sem(f"loaded_{i}") for i in range(4)]
    products, sigmoid, joined, added = (st.sem(n) for n in ("products_done", "sigmoid_ready", "joined", "added"))
    sig = k.sb("branch_sigmoids", [P, 2, 512], ctx=scope)
    N = 4 * NT
    with nc.Block() as block:
        @block.sync
        def _(sp):
            st.clear_previous(sp)
            for c in range(4):
                if c >= 2:
                    sp.wait_ge(products, NT * (c - 1))
                if c == 2:
                    sp.dma_start(k.x[:], k.x_home).then_inc(k.x_back, 16)
                i = c % 2
                sp.dma_start(wg[i][:, :, 0, :], w_in[:, :, O_GA + c * C:O_GA + (c + 1) * C]).then_inc(loaded[c], 16)
                sp.dma_start(wg[i][:, :, 1, :], w_in[:, :, O_GR + c * C:O_GR + (c + 1) * C]).then_inc(loaded[c], 16)
                sp.dma_start(wb[i][:], wbr[:, :, c * C:(c + 1) * C]).then_inc(loaded[c], 16)

        @block.tensor
        def _(pe):
            for g in range(N):
                c, t = g // NT, g % NT
                i = c % 2
                tok = slice(t * P, (t + 1) * P)
                if t == 0:
                    pe.wait_ge(loaded[c], 48)
                if g >= 4:
                    pe.wait_ge(joined, g - 3)
                gemm(nc, k.bank(2 * (g % 4)), [(k.ht[:, j, tok], wg[i][:, j, :, :].rearrange("p a c -> p (a c)")) for j in range(KT)])
                gemm(nc, k.psum[:, 2 * (g % 4) + 1, 0:C], [(oat[:, j, tok], wb[i][:, j, :]) for j in range(2)])
                gemm(nc, k.psum[:, 2 * (g % 4) + 1, C:2 * C],
                     [(ort[:, j, tok], wb[i][:, 2 + j, :]) for j in range(KT)]).then_inc(products, 1)

        @block.scalar
        def _(act):
            for g in range(N):
                act.wait_ge(products, g + 1)
                if g >= 2:
                    act.wait_ge(added, g - 1)
                nc.scalar.activation(sig[:, g % 2, :], k.bank(2 * (g % 4)), ACT.Sigmoid).then_inc(sigmoid, 1)

        @block.vector
        def _(dve):
            for g in range(N):
                c, t = g // NT, g % NT
                s = sig[:, g % 2, :]
                dve.wait_ge(sigmoid, g + 1)
                nc.vector.tensor_tensor(s, s, k.bank(2 * (g % 4) + 1), ALU.mult).then_inc(joined, 1)
                dve.wait_ge(joined, g + 1)
                nc.vector.tensor_tensor(merged[:, t, c * C:(c + 1) * C], s[:, 0:C], s[:, C:2 * C], ALU.add).then_inc(added, 1)


def post_project(k, w, wbuf, y, post):
    nc = k.nc
    src = w.rearrange("(kt p) c -> p kt c", p=P)
    W = Weights(k, wbuf, "mix_out", [src[:, :, i * HALF:(i + 1) * HALF] for i in range(2)])
    groups = []
    for n in range(2):
        for t in range(NT):
            who = "dve" if t % 2 else "act"
            groups.append((n, (0, P, HALF), [(k.ht[:, i, t * P:(t + 1) * P], W.view(n)[:, i, :]) for i in range(KT)],
                           who, moving(nc, who, y[:, t, n * HALF:(n + 1) * HALF])))
    project_stage(k, "mix_out_project", groups, W, loads=(0, 1), then_wait=[(k.x_back, 16)])
    add_normed(k, "norm_mix_post", y, post)
    loop_edge(k, [W])


def add_normed(k, name, y, post):
    nc = k.nc

    def then(t, chain):
        chain(nc.vector.scalar_tensor_tensor(y[:, t, :], y[:, t, :], k.root[:, t:t + 1], post, ALU.mult, ALU.mult))
        nc.vector.tensor_tensor(k.x[:, t, :], k.x[:, t, :], y[:, t, :], ALU.add)
    rms_scale_stage(k, name, y, k.ht, 1e-6, then)


def feed_forward(k, a, mod, post):
    nc = k.nc
    HID = 4 * D // 2
    with ExitStack() as own:
        f = k.sb("ffn_out", [P, NT, D], ctx=own)
        hid = k.sb("hidden", [P, HID // P, S], ctx=own)
        wbuf = [k.sb(f"ffn_weights_{i}", [P, KT, HALF], ctx=own) for i in range(2)]
        rms_scale_stage(k, "norm_ffn", k.x, f, 1e-6,
                        lambda t, chain: nc.vector.tensor_scalar_mul(f[:, t, :], k.x[:, t, :], k.root[:, t:t + 1]))
        transpose_stage(k, "turn_ffn", lambda t: f[:, t, :], k.ht, KT, scale=mod[:, 3, :], shift=mod[:, 2, :])
        st = Stage(k, "ffn_zero")
        with nc.Block() as block:
            @block.vector
            def _(dve):
                nc.vector.memset(f[:], 0.0)

            @block.sync
            def _(sp):
                st.clear_previous(sp)
        w1 = a["w_ff1_2"][0].rearrange("(kt p) c -> p kt c", p=P)
        w2 = a["w_ff2_2"][0].rearrange("(kt p) c -> p kt c", p=P)
        loop_edge(k)
        with nc.Fori(0, 2) as part:
            up = [w1[:, :, bass.ds(part * HID + c * HALF, HALF)] for c in range(4)]
            down = [w2[:, bass.ds(part * (HID // P) + r * KT, KT), n * HALF:(n + 1) * HALF] for n in range(2) for r in range(2)]
            W = Weights(k, wbuf, "ffn_w", up + down)
            groups = []
            for tile in range(HID // P):
                c = tile // 4
                for half in range(2):
                    s = slice(half * HALF, (half + 1) * HALF)

                    def relu(ps, tile=tile, s=s):
                        return nc.scalar.activation(hid[:, tile, s], ps, ACT.Relu)
                    groups.append((c, (0, P, HALF), [(W.view(c)[:, i, tile % 4 * P:(tile % 4 + 1) * P], k.ht[:, i, s])
                                                     for i in range(KT)], "act", relu))

            def square_tail(dve, dve_sem, dve_n, act_sem, act_n, st):
                for g in range(act_n):
                    s = slice((g % 2) * HALF, (g % 2 + 1) * HALF)
                    dve.wait_ge(act_sem, g + 1)
                    nc.vector.tensor_tensor(hid[:, g // 2, s], hid[:, g // 2, s], hid[:, g // 2, s], ALU.mult)
            project_stage(k, "ffn_up", groups, W, loads=(0, 1, 2, 3), prefetch=(4, 5), tail=square_tail)

            st = Stage(k, "ffn_down")
            products, added = st.sem("products_done"), st.sem("added")
            with nc.Block() as block:
                @block.sync
                def _(sp):
                    st.clear_previous(sp)
                    for c in (6, 7):
                        sp.wait_ge(products, NT * (c - 5))
                        W.load(sp, c)

                @block.tensor
                def _(pe):
                    for n in range(2):
                        for r in range(2):
                            pe.wait_ge(W.loaded[4 + 2 * n + r], 16)
                            for t in range(NT):
                                if n and not r:
                                    pe.wait_ge(added, t + 1)
                                for i in range(KT):
                                    mm = nc.tensor.matmul(k.bank(t), hid[:, r * KT + i, t * P:(t + 1) * P],
                                                          W.view(4 + 2 * n + r)[:, i, :], start=(r == 0 and i == 0),
                                                          stop=(r == 1 and i == KT - 1))
                                mm.then_inc(products, 1)

                @block.vector
                def _(dve):
                    for n in range(2):
                        for t in range(NT):
                            dve.wait_ge(products, NT * (2 * n + 1) + t + 1)
                            s = f[:, t, n * HALF:(n + 1) * HALF]
                            nc.vector.tensor_tensor(s, s, k.bank(t), ALU.add).then_inc(added, 1)
            loop_edge(k, [W])
        add_normed(k, "norm_ffn_post", f, post[:, 1, :])


def program(nc, a, out):
    with ExitStack() as ctx:
        k = Kernel(nc, ctx)
        common_tensors(k)
        first_block(k, a)
        second_block(k, a, out)



def kernel(**inputs):
    import numpy as _np
    import concourse.bacc as _bacc
    from concourse import mybir as _mybir
    from concourse.bass_utils import run_bass_kernel_spmd as _run

    nc = _bacc.Bacc("TRN2", target_bir_lowering=False, num_devices=1)
    arrays, args = {}, {}
    for name, value in inputs.items():
        value = _np.ascontiguousarray(value)
        arrays[f"in_{name}_dram"] = value
        args[name] = nc.dram_tensor(f"in_{name}_dram", value.shape, _mybir.dt.from_np(value.dtype), kind="ExternalInput").ap()
    out = nc.dram_tensor("out_dram", (1, S, D), _mybir.dt.float32, kind="ExternalOutput").ap()
    program(nc, args, out)
    r = _run(nc, [arrays], core_ids=[0])
    return r.results[0]["out_dram"]
```

```python
from contextlib import ExitStack

import numpy as np

import concourse.bass as bass
from concourse import mybir

F32 = mybir.dt.float32
F32R = mybir.dt.float32r
I32 = mybir.dt.int32
ALU = mybir.AluOpType
ACT = mybir.ActivationFunctionType
AX = mybir.AxisListType

P = 128
D = 1024
S = 1024
KT = D // P
NT = S // P
HALF = 512
MEM = 256
DEPTH = 2
LN_EPS = 1e-5
RMS_EPS = 1e-6
GN_EPS = 64e-5
MASKED = -1e30
ALPHA = (2 * DEPTH) ** 0.25
E_HALF = float(np.exp(-0.5))


class Stage:

    def __init__(self, k, name):
        self.k, self.name, self.sems, self.scope = k, name, [], ExitStack()
        if len(k.stages) > 1:
            k.stages.pop(0).scope.close()
        self.before = k.stages[-1].sems if k.stages else []
        k.stages.append(self)

    def sem(self, what):
        s = self.scope.enter_context(self.k.nc.semaphore(f"{self.name}_{what}"))
        self.sems.append(s)
        return s

    def clear_now(self, sp):
        for s in self.sems:
            sp.sem_clear(s)

    def clear_previous(self, sp):
        for s in self.before:
            sp.sem_clear(s)


def loop_edge(k, weights=()):
    with k.nc.Block() as block:
        @block.sync
        def _(sp):
            if k.stages:
                k.stages[-1].clear_now(sp)
            for w in weights:
                w.clear(sp)
    while k.stages:
        k.stages.pop(0).scope.close()


class Kernel:
    def __init__(self, nc, ctx):
        self.nc, self.ctx = nc, ctx
        self.psum = ctx.enter_context(nc.psum_tensor("banks", [P, 8, HALF], F32))
        self.stages = []
        ctx.enter_context(nc.allow_non_contiguous_dma(reason="vectors of gains are laid on the partitions"))

    def sem(self, name):
        return self.ctx.enter_context(self.nc.semaphore(name))

    def sb(self, name, shape, dt=F32, ctx=None):
        return (ctx or self.ctx).enter_context(self.nc.sbuf_tensor(name, shape, dt))

    def next_place(self):
        return -(-self.nc.sbuf_base // 32) * 32

    def over(self, name, shape, at, dt=F32R):
        return self.nc.alloc_sbuf_tensor_at(name, shape, dt, offset=at)

    def twofold(self, name, shape, ctx):
        at = self.next_place()
        value = self.sb(f"{name}_value", shape, ctx=ctx)
        return value, self.over(f"{name}_low", shape, at)

    def bank(self, b, n=HALF, p0=0, p1=P):
        return self.psum[p0:p1, b, 0:n]

    def banks2(self, b):
        return self.psum[:, b:b + 2, :].rearrange("p b n -> p (b n)")


def value_views(tensor, pairs):
    view = tensor[:].rearrange("p (t q w c) -> p t q w c", q=pairs, w=3, c=64)
    flat = tensor[:].rearrange("p (t c) -> p t c", c=pairs * 192)

    def both(t, q0, q1):
        return view[:, t, q0:q1, 0:3:2, :]

    def beside(h, t):
        at = h // 2 * 192 + 64 * (h % 2)
        return flat[:, t, at:at + P]

    def own(h, t):
        at = h // 2 * 192 + P * (h % 2)
        return flat[:, t, at:at + 64]
    return both, beside, own, view[:, :, :, 1, :]


def moving_values(nc, who, dst):
    move = nc.vector.tensor_copy if who == "dve" else nc.scalar.copy
    return lambda ps: move(dst, ps.rearrange("p (q w c) -> p q w c", w=2, c=64))


def gemm(nc, out, pairs):
    if isinstance(pairs[0][0], tuple):
        return split_gemm(nc, out, pairs)
    for i, (lhs, rhs) in enumerate(pairs):
        mm = nc.tensor.matmul(out, lhs, rhs, start=(i == 0), stop=(i == len(pairs) - 1))
    return mm


class SemaphoreGroup:
    def __init__(self, sems):
        self.sems = sems

    def clear(self, sp):
        for s in self.sems:
            sp.sem_clear(s)


class Weights:

    def __init__(self, k, buffers, prefix, sources):
        self.k, self.buf, self.src = k, buffers, sources
        self.loaded = [k.sem(f"{prefix}_loaded_{c}") for c in range(len(sources))]

    def load(self, eng, c):
        src = self.src[c]
        eng.dma_start(self.view(c)[:, 0:src.shape[1], :], src).then_inc(self.loaded[c], 16)

    def view(self, c):
        n = self.src[c].shape[-1]
        return self.buf[c % 2][:, 0:KT, 0:n]

    def clear(self, sp):
        for s in self.loaded:
            sp.sem_clear(s)


class SplitWeights:

    def __init__(self, k, high, two, prefix, sources):
        self.k, self.high, self.two, self.src = k, high, two, sources
        self.loaded = [k.sem(f"{prefix}_loaded_{c}") for c in range(len(sources))]

    def load(self, eng, c):
        eng.dma_start(self.value(c), self.src[c]).then_inc(self.loaded[c], 16)

    def width(self, c):
        return self.src[c].shape[-1]

    def value(self, c):
        return self.two[c % 2][0][:, :, 0:self.width(c)]

    def parts(self, c, i, c0, c1):
        return self.high[c % 2][:, i, c0:c1], self.two[c % 2][1][:, i, c0:c1]

    def split(self, pool, chunks, rounded, done, used=None):
        nc = self.k.nc
        for n, c in enumerate(chunks):
            w = self.width(c)
            high, value, low = self.high[c % 2][:, :, 0:w], self.value(c), self.two[c % 2][1][:, :, 0:w]
            pool.wait_ge(self.loaded[c], 16)
            if used:
                used(c - 2)
            nc.gpsimd.tensor_copy(high, value).then_inc(rounded, 1)
            pool.wait_ge(rounded, n + 1)
            nc.gpsimd.tensor_tensor(low, value, high, ALU.subtract).then_inc(done, 1)

    def clear(self, sp):
        for s in self.loaded:
            sp.sem_clear(s)


def split_gemm(nc, out, pairs, first=True, last=True):
    n = len(pairs)
    for i, (lhs, rhs) in enumerate(pairs):
        for j, (x, y) in enumerate(((lhs[0], rhs[0]), (lhs[0], rhs[1]), (lhs[1], rhs[0]))):
            mm = nc.tensor.matmul(out, x, y, start=(first and i == 0 and j == 0),
                                  stop=(last and i == n - 1 and j == 2))
    return mm


def split_transpose_stage(k, name, src, high, low, scale=None, shift=None, store=None, prefetch=(), splits=(), w=None):
    value, low = low
    nc = k.nc
    st = Stage(k, name)
    turned, scaled, rounded, split = (st.sem(n) for n in ("turned", "scaled", "rounded", "split"))

    def place(x, g):
        return x[:, g // 2, (g % 2) * HALF:(g % 2 + 1) * HALF]

    with nc.Block() as block:
        @block.sync
        def _(sp):
            st.clear_previous(sp)
            for c in prefetch:
                w.load(sp, c)
            if store:
                sp.dma_start(store[0], store[1]).then_inc(store[2], 16)
                sp.wait_ge(store[2], 16)

        @block.tensor
        def _(pe):
            for g in range(2 * KT):
                c = g // 2
                if g >= 8:
                    pe.wait_ge(scaled, g - 7)
                for i in range(4):
                    t = 4 * (g % 2) + i
                    mm = nc.tensor.transpose(k.psum[:, g % 8, i * P:(i + 1) * P], src(t)[:, c * P:(c + 1) * P], k.ident[:])
                mm.then_inc(turned, 1)

        @block.scalar
        def _(act):
            for g in range(2 * KT):
                c = g // 2
                act.wait_ge(turned, g + 1)
                if scale is None:
                    nc.scalar.copy(place(value, g), k.bank(g % 8)).then_inc(scaled, 1)
                else:
                    nc.scalar.activation(place(value, g), k.bank(g % 8), ACT.Identity, scale=scale[:, c:c + 1],
                                         bias=shift[:, c:c + 1]).then_inc(scaled, 1)

        @block.gpsimd
        def _(pool):
            if splits:
                w.split(pool, splits, st.sem("weights_rounded"), st.sem("weights_split"))

        @block.vector
        def _(dve):
            for g in range(2 * KT):
                dve.wait_ge(scaled, g + 1)
                nc.vector.tensor_copy(place(high, g), place(value, g)).then_inc(rounded, 1)
                dve.wait_ge(rounded, g + 1)
                nc.vector.tensor_tensor(place(low, g), place(value, g), place(high, g), ALU.subtract).then_inc(split, 1)


def project_stage(k, name, groups, w=None, loads=(), prefetch=(), tail=None, nbanks=8, first=0, tail_act=None,
                  tail_pool=None, then_wait=(), splits=(), reload=None, first_dve=None,
                  tails_after=None, lead_pool=None):
    nc = k.nc
    st = Stage(k, name)
    products, rounded, split = (st.sem(n) for n in ("products_done", "weights_rounded", "weights_split"))
    evac = {"dve": st.sem("dve_evacuated"), "act": st.sem("act_evacuated")}
    last_of = {}
    order = {"dve": [], "act": []}
    for g, (c, shape, pairs, who, _) in enumerate(groups):
        last_of[c] = g
        order[who].append(g)

    def region(g):
        p0, p1, n = groups[g][1]
        return k.psum[p0:p1, first + g % nbanks, 0:n]

    with nc.Block() as block:
        @block.sync
        def _(sp):
            st.clear_previous(sp)
            if reload:
                sp.dma_start(reload[0], reload[1]).then_inc(reload[2], 16)
            for c in loads:
                if c - 2 in last_of:
                    sp.wait_ge(products, last_of[c - 2] + 1)
                w.load(sp, c)
            for c in prefetch:
                if c - 2 in last_of:
                    sp.wait_ge(products, last_of[c - 2] + 1)
                w.load(sp, c)
            for s, n in then_wait:
                sp.wait_ge(s, n)

        @block.tensor
        def _(pe):
            seen = set()
            for g, (c, shape, pairs, who, _) in enumerate(groups):
                if c is not None and c not in seen:
                    seen.add(c)
                    if c in splits:
                        pe.wait_ge(split, splits.index(c) + 1)
                    else:
                        pe.wait_ge(w.loaded[c], 16)
                if g >= nbanks:
                    former = groups[g - nbanks][3]
                    pe.wait_ge(evac[former], order[former].index(g - nbanks) + 1)
                gemm(nc, region(g), pairs).then_inc(products, 1)

        @block.vector
        def _(dve):
            if first_dve:
                dve.wait_ge(*first_dve)
            for i, g in enumerate(order["dve"]):
                if tails_after and i == tails_after[0]:
                    tail(dve, evac["dve"], i, evac["act"], tails_after[1], st)
                dve.wait_ge(products, g + 1)
                groups[g][4](region(g)).then_inc(evac["dve"], 1)
            if tail and not tails_after:
                tail(dve, evac["dve"], len(order["dve"]), evac["act"], len(order["act"]), st)

        @block.scalar
        def _(act):
            for i, g in enumerate(order["act"]):
                if tails_after and i == tails_after[1]:
                    tail_act(act, evac["dve"], tails_after[0], evac["act"], i, st)
                act.wait_ge(products, g + 1)
                groups[g][4](region(g)).then_inc(evac["act"], 1)
            if tail_act and not tails_after:
                tail_act(act, evac["dve"], len(order["dve"]), evac["act"], len(order["act"]), st)

        @block.gpsimd
        def _(pool):
            if lead_pool:
                lead_pool(pool, st)
            if splits:
                def used(c):
                    if c in last_of:
                        pool.wait_ge(products, last_of[c] + 1)
                w.split(pool, splits, rounded, split, used)
                pool.wait_ge(split, len(splits))
            if tail_pool:
                tail_pool(pool, evac["dve"], len(order["dve"]), evac["act"], len(order["act"]), st)


def moving(nc, who, dst, scale=None):
    if scale is None:
        return (lambda ps: nc.vector.tensor_copy(dst, ps)) if who == "dve" else (lambda ps: nc.scalar.copy(dst, ps))
    if who == "dve":
        return lambda ps: nc.vector.tensor_scalar_mul(dst, ps, scale)
    return lambda ps: nc.scalar.mul(dst, ps, scale)


def transpose_stage(k, name, src, dst, channel_tiles, scale=None, shift=None, prefetch=(), w=None):
    nc = k.nc
    st = Stage(k, name)
    turned = st.sem("turned")
    evac = {"dve": st.sem("dve_evacuated"), "act": st.sem("act_evacuated")}
    n = 2 * channel_tiles

    with nc.Block() as block:
        @block.sync
        def _(sp):
            st.clear_previous(sp)
            for c in prefetch:
                w.load(sp, c)

        @block.tensor
        def _(pe):
            for g in range(n):
                c, half = g // 2, g % 2
                if g >= 8:
                    pe.wait_ge(evac["dve" if g % 2 else "act"], (g - 8) // 2 + 1)
                for i in range(4):
                    t = 4 * half + i
                    mm = nc.tensor.transpose(k.psum[:, g % 8, i * P:(i + 1) * P], src(t)[:, c * P:(c + 1) * P], k.ident[:])
                mm.then_inc(turned, 1)

        @block.vector
        def _(dve):
            for g in range(1, n, 2):
                c = g // 2
                out = dst[:, c, HALF:S]
                dve.wait_ge(turned, g + 1)
                if scale is None:
                    nc.vector.tensor_copy(out, k.bank(g % 8)).then_inc(evac["dve"], 1)
                else:
                    nc.vector.tensor_scalar(out, k.bank(g % 8), scale[:, c:c + 1],
                                            shift[:, c:c + 1] if shift is not None else 0.0,
                                            ALU.mult, ALU.add).then_inc(evac["dve"], 1)

        @block.scalar
        def _(act):
            for g in range(0, n, 2):
                c = g // 2
                out = dst[:, c, 0:HALF]
                act.wait_ge(turned, g + 1)
                if scale is None:
                    nc.scalar.copy(out, k.bank(g % 8)).then_inc(evac["act"], 1)
                else:
                    nc.scalar.activation(out, k.bank(g % 8), ACT.Identity, scale=scale[:, c:c + 1],
                                         bias=shift[:, c:c + 1] if shift is not None else 0.0).then_inc(evac["act"], 1)


def layer_norm_stage(k, name, x, tiles, gain, bias, loads=(), dst=None):
    nc = k.nc
    dst = x if dst is None else dst
    st = Stage(k, name)
    arrived, stats, rooted, scaled, step, offsets, centred = (
        st.sem(n) for n in ("arrived", "stats_ready", "root_ready", "scaled", "dve_step", "offsets_ready", "centred"))
    offset = k.rowmax[:, 0:tiles]
    with nc.Block() as block:
        @block.sync
        def _(sp):
            st.clear_previous(sp)
            for to, src in loads:
                sp.dma_start(to, src).then_inc(arrived, 16)

        @block.vector
        def _(dve):
            for t in range(tiles):
                if t == 0 and loads:
                    dve.wait_ge(arrived, 16 * len(loads))
                for h in range(2):
                    last = nc.vector.bn_stats(k.stats[:, t, h, :], x[:, t, h * HALF:(h + 1) * HALF])
            last.then_inc(step, 1)
            dve.wait_ge(step, 1)
            for t in range(tiles):
                last = nc.vector.bn_aggr(k.moments[:, t, :], k.stats[:, t, :, :])
            last.then_inc(step, 1)
            dve.wait_ge(step, 2)
            nc.vector.tensor_scalar_add(k.root[:, 0:tiles], k.moments[:, 0:tiles, 1], LN_EPS).then_inc(stats, 1)
            dve.wait_ge(rooted, 1)
            nc.vector.reciprocal(k.root[:, 0:tiles], k.root[:, 0:tiles]).then_inc(step, 1)
            dve.wait_ge(step, 3)
            nc.vector.scalar_tensor_tensor(offset, k.moments[:, 0:tiles, 0], -1.0, k.root[:, 0:tiles], ALU.mult,
                                           ALU.mult).then_inc(offsets, 1)
            for t in range(tiles):
                dve.wait_ge(centred, t + 1)
                nc.vector.tensor_tensor(dst[:, t, :], dst[:, t, :], gain, ALU.mult).then_inc(scaled, 1)
                if t % 2:
                    dve.wait_ge(scaled, t + 1)
                    nc.vector.tensor_tensor(dst[:, t, :], dst[:, t, :], bias, ALU.add)

        @block.scalar
        def _(act):
            act.wait_ge(stats, 1)
            nc.scalar.activation(k.root[:, 0:tiles], k.root[:, 0:tiles], ACT.Sqrt).then_inc(rooted, 1)
            act.wait_ge(offsets, 1)
            for t in range(tiles):
                nc.scalar.activation(dst[:, t, :], x[:, t, :], ACT.Identity, scale=k.root[:, t:t + 1],
                                     bias=offset[:, t:t + 1]).then_inc(centred, 1)

        @block.gpsimd
        def _(pool):
            if loads:
                pool.wait_ge(arrived, 16 * len(loads))
            for t in range(0, tiles, 2):
                pool.wait_ge(scaled, t + 1)
                nc.gpsimd.tensor_tensor(dst[:, t, :], dst[:, t, :], bias, ALU.add)


def attention_stage(k, name, buf, q, key, v, out, heads, plan, masks, scale, sticks=False, prefetch=(), w=None, tiles=NT, spare=None, splits=()):
    nc = k.nc
    st = Stage(k, name)
    units = [(h, t) for h in range(heads) for t in range(tiles)]
    N = len(units)
    wide = max(sum(r[2] for r in plan(t)) for t in range(tiles)) * P
    slots = 2 if wide <= 1024 else 1
    span = 2 if slots == 2 else 4
    names = ("scores_done", "max_ready", "exp_done", "turned", "dve_moved", "act_moved", "summed", "normalised",
             "dve_step", "softplus_ready", "weights_log_ready", "inverted")
    (scores_done, max_ready, exp_done, turned, dve_moved, act_moved, summed, normalised,
     step, softplus_ready, log_ready, inverted) = (st.sem(n) for n in names)
    steps = [0]
    weights = buf.weights + ([spare] if spare is not None else [])
    NW = len(weights)

    def cols(u):
        return P * sum(r[2] for r in plan(units[u][1]))

    def scores(u, a=0, b=None):
        s = u % slots
        flat = k.psum[:, span * s:span * s + span, :].rearrange("p b n -> p (b n)")
        return flat[:, a:cols(u) if b is None else b]

    def blocks(u):
        h, t = units[u]
        return [(g, b) for g, b0, n in plan(t) for b in range(b0, b0 + n)]

    def chain(dve, ins):
        steps[0] += 1
        ins.then_inc(step, 1)
        dve.wait_ge(step, steps[0])

    def moved_counts(u):
        dve_n = act_n = 0
        for i in range(u + 1):
            n = -(-len(blocks(i)) // 4)
            dve_n += len(dve_pieces(n))
            act_n += len(act_pieces(n))
        return dve_n, act_n

    def dve_pieces(n):
        return range(1, n, 2) if slots == 2 else range(0)

    def act_pieces(n):
        return range(0, n, 2) if slots == 2 else range(n)

    piece_no = {}
    total = 0
    for u in range(N):
        for j in range(-(-len(blocks(u)) // 4)):
            piece_no[u, j] = total
            total += 1
    turn_banks = 2

    with nc.Block() as block:
        @block.sync
        def _(sp):
            st.clear_previous(sp)
            for c in prefetch:
                w.load(sp, c)

        @block.tensor
        def _(pe):
            def do_scores(u):
                h, t = units[u]
                if u >= slots:
                    pe.wait_ge(log_ready if sticks else exp_done, u - slots + 1)
                at = 0
                for g, b0, n in plan(t):
                    a, left = b0 * P, n * P
                    while left:
                        size = min(left, HALF - at % HALF)
                        mm = nc.tensor.matmul(scores(u, at, at + size), q(h, g, t), key(h, g, a, a + size), start=True, stop=True)
                        at, a, left = at + size, a + size, left - size
                mm.then_inc(scores_done, 1)

            def do_turn(u):
                pe.wait_ge(exp_done, u + 1)
                n = len(blocks(u))
                for j in range(-(-n // 4)):
                    p = piece_no[u, j]
                    if p >= turn_banks:
                        pu, pj = next(key_ for key_, val in piece_no.items() if val == p - turn_banks)
                        d, a = moved_counts(pu - 1) if pu else (0, 0)
                        pieces = -(-len(blocks(pu)) // 4)
                        if pj in dve_pieces(pieces):
                            pe.wait_ge(dve_moved, d + dve_pieces(pieces).index(pj) + 1)
                        else:
                            pe.wait_ge(act_moved, a + act_pieces(pieces).index(pj) + 1)
                    for i in range(4 * j, min(4 * j + 4, n)):
                        mm = nc.tensor.transpose(k.psum[:, 4 + p % turn_banks, (i % 4) * P:(i % 4 + 1) * P],
                                                 weights[u % NW][:, i * P:(i + 1) * P], k.ident[:])
                    mm.then_inc(turned, 1)

            def do_sum(u):
                h, t = units[u]
                d, a = moved_counts(u)
                if d:
                    pe.wait_ge(dve_moved, d)
                pe.wait_ge(act_moved, a)
                if u >= 2:
                    pe.wait_ge(normalised, u - 1)
                bl = blocks(u)
                gemm(nc, k.psum[0:64 if sticks else P, 6 + u % 2, 0:P],
                     [(v(h, g, b), buf.turned[u % 2][:, i * P:(i + 1) * P]) for i, (g, b) in enumerate(bl)]).then_inc(summed, 1)

            for u in range(min(slots, N)):
                do_scores(u)
            for u in range(N):
                scores_first = sticks or slots == 1
                if scores_first and u + slots < N:
                    do_scores(u + slots)
                do_turn(u)
                if not scores_first and u + slots < N:
                    do_scores(u + slots)
                if u >= 1:
                    do_sum(u - 1)
            do_sum(N - 1)

        @block.vector
        def _(dve):
            def row_max(u):
                dve.wait_ge(scores_done, u + 1)
                t = units[u][1]
                if len(masks(t)) == 1 and masks(t)[0][1] == cols(u):
                    chain(dve, nc.vector.tensor_tensor_reduce(scores(u), scores(u), masks(t)[0][2], 1.0, -3e38, ALU.add, ALU.max,
                                                              k.rowmax[:, u:u + 1]))
                    nc.vector.tensor_scalar_mul(k.negmax[:, u:u + 1], k.rowmax[:, u:u + 1], -scale).then_inc(max_ready, 1)
                    return
                for a, n, m in masks(t):
                    last = nc.vector.tensor_tensor(scores(u, a, a + n), scores(u, a, a + n), m, ALU.add)
                if masks(t):
                    chain(dve, last)
                chain(dve, nc.vector.reduce_max(k.rowmax[:, u:u + 1], scores(u), AX.X))
                nc.vector.tensor_scalar_mul(k.negmax[:, u:u + 1], k.rowmax[:, u:u + 1], -scale).then_inc(max_ready, 1)

            def stick_logs(u):
                z, n = weights[u % NW], cols(u)
                dve.wait_ge(softplus_ready, u + 1)
                chain(dve, nc.vector.scalar_tensor_tensor(z[:, 0:n], scores(u), 0.0, z[:, 0:n], ALU.max, ALU.add))
                chain(dve, nc.vector.tensor_tensor(z[:, n - P:n], z[:, n - P:n], k.before01[:], ALU.mult))
                chain(dve, nc.vector.tensor_tensor_scan(buf.cum[:, 0:n][:, ::-1], k.one[:, 0:1].broadcast_to([P, n]),
                                                        z[:, 0:n][:, ::-1], 0.0, ALU.mult, ALU.add))
                chain(dve, nc.vector.tensor_tensor(z[:, 0:n], scores(u), buf.cum[:, 0:n], ALU.subtract))
                nc.vector.tensor_tensor(z[:, n - P:n], z[:, n - P:n], k.before_add[:], ALU.add).then_inc(log_ready, 1)

            def move(u):
                n = len(blocks(u))
                if u >= 2:
                    dve.wait_ge(summed, u - 1)
                for j in dve_pieces(-(-n // 4)):
                    dve.wait_ge(turned, piece_no[u, j] + 1)
                    c = min(4, n - 4 * j) * P
                    nc.vector.tensor_copy(buf.turned[u % 2][:, j * HALF:j * HALF + c],
                                          k.bank(4 + piece_no[u, j] % turn_banks, c)).then_inc(dve_moved, 1)

            def normalise(u):
                h, t = units[u]
                dve.wait_ge(summed, u + 1)
                if sticks:
                    nc.vector.tensor_copy(out(h, t), k.psum[0:64, 6 + u % 2, 0:P]).then_inc(normalised, 1)
                else:
                    mine = slice(64 * (h % 2), 64 * (h % 2) + 64)
                    dve.wait_ge(inverted, u + 1)
                    nc.vector.tensor_tensor(out(h, t), k.psum[mine, 6 + u % 2, 0:P], k.inverse_sum[mine, u % 2, :],
                                            ALU.mult).then_inc(normalised, 1)

            if sticks:
                for u in range(N):
                    stick_logs(u)
                    if u >= 1:
                        move(u - 1)
                    if u >= 2:
                        normalise(u - 2)
                move(N - 1)
                normalise(N - 2)
                normalise(N - 1)
            else:
                lag = 1
                for u in range(min(slots, N)):
                    row_max(u)
                for u in range(N):
                    if slots == 1 and u + 1 < N:
                        row_max(u + 1)
                    move(u)
                    if slots == 2 and u + 2 < N:
                        row_max(u + 2)
                    if u >= lag:
                        normalise(u - lag)
                for u in range(N - lag, N):
                    normalise(u)

        @block.gpsimd
        def _(pool):
            if splits:
                w.split(pool, splits, st.sem("weights_rounded"), st.sem("weights_split"))

        @block.scalar
        def _(act):
            def exponent(u):
                dst = weights[u % NW][:, 0:cols(u)]
                if sticks:
                    act.wait_ge(log_ready, u + 1)
                    nc.scalar.activation(dst, dst, ACT.Exp).then_inc(exp_done, 1)
                else:
                    act.wait_ge(max_ready, u + 1)
                    if u >= NW:
                        act.wait_ge(turned, piece_no[u - NW + 1, 0])
                    nc.scalar.activation(dst, scores(u), ACT.Exp, bias=k.negmax[:, u:u + 1], scale=scale).then_inc(exp_done, 1)

            def softplus_log(u):
                z = weights[u % NW][:, 0:cols(u)]
                act.wait_ge(scores_done, u + 1)
                if u >= NW:
                    act.wait_ge(turned, piece_no[u - NW + 1, 0])
                nc.scalar.activation(z, scores(u), ACT.Abs).then_inc(act_step, 1)
                act.wait_ge(act_step, 2 * u + 1)
                nc.scalar.activation(z, z, ACT.Exp, scale=-1.0).then_inc(act_step, 1)
                act.wait_ge(act_step, 2 * u + 2)
                nc.scalar.activation(z, z, ACT.Ln, bias=1.0).then_inc(softplus_ready, 1)

            def move(u):
                n = len(blocks(u))
                if u >= 2:
                    act.wait_ge(summed, u - 1)
                for j in act_pieces(-(-n // 4)):
                    act.wait_ge(turned, piece_no[u, j] + 1)
                    c = min(4, n - 4 * j) * P
                    nc.scalar.copy(buf.turned[u % 2][:, j * HALF:j * HALF + c],
                                   k.bank(4 + piece_no[u, j] % turn_banks, c)).then_inc(act_moved, 1)

            def invert(u):
                mine = slice(64 * (units[u][0] % 2), 64 * (units[u][0] % 2) + 64)
                other = slice(64 - mine.start, 128 - mine.start)
                inverse = k.inverse_sum[mine, u % 2, :]
                act.wait_ge(summed, u + 1)
                if u >= 2:
                    act.wait_ge(normalised, u - 1)
                nc.scalar.activation(inverse, k.psum[other, 6 + u % 2, 0:P], ACT.Ln).then_inc(act_step, 1)
                act.wait_ge(act_step, u + 1)
                nc.scalar.activation(inverse, inverse, ACT.Exp, scale=-1.0).then_inc(inverted, 1)

            act_step = st.sem("act_step")
            nc.scalar.preload_act_table_set("natural_log_exp_and_others")
            if sticks:
                softplus_log(0)
                for u in range(N):
                    if u + 1 < N:
                        softplus_log(u + 1)
                    exponent(u)
                    move(u)
            else:
                exponent(0)
                for u in range(N):
                    if slots == 2 and u + 1 < N:
                        exponent(u + 1)
                    move(u)
                    if u >= 1:
                        invert(u - 1)
                    if slots == 1 and u + 1 < N:
                        exponent(u + 1)
                invert(N - 1)



def rope_tables():
    half = 16
    freq = (10000.0 ** (-np.arange(half, dtype=np.float32) / half)).astype(np.float32)
    angle = np.arange(S, dtype=np.float32)[None, :] * np.concatenate([freq, freq])[:, None]
    return np.stack([np.cos(angle), np.sin(angle)], 1).astype(np.float32)


def rotation(n, starts, half):
    r = np.zeros((n, n), np.float32)
    for s in starts:
        for i in range(half):
            r[s + i, s + i + half] = -1.0
            r[s + i + half, s + i] = 1.0
    return np.ascontiguousarray(r.T)


def constants_one():
    q, key = np.arange(P)[:, None], np.arange(P)[None, :]
    parts = [np.eye(P), np.where(key <= q, 0.0, MASKED), np.where(key < q, 1.0, 0.0), np.where(key < q, 0.0, MASKED)]
    return np.concatenate(parts, 1).astype(np.float32)



O_FQ, O_FK, O_FV, O_FL, O_SQ, O_SK, O_SV, O_CQ, O_CKV, O_KR, O_MQ, O_GATE = (
    0, 256, 512, 768, 772, 1028, 1284, 1540, 1796, 1924, 1956, 2212)
RANKS = 384
HEAD_SCALE = 0.125
MLA_SCALE = 96 ** -0.5


class Buffers:
    pass


def common_tensors(k):
    nc = k.nc
    k.x_at = k.next_place()
    k.x = k.sb("x_residual", [P, NT, D])
    k.ht_at = k.next_place()
    k.ht = k.sb("h_channel_major", [P, KT, S])
    k.consts = k.sb("masks_and_identity", [P, 4 * P])
    k.ident = k.consts[:, 0:P]
    k.causal_add = k.consts[:, P:2 * P]
    k.before01 = k.consts[:, 2 * P:3 * P]
    k.before_add = k.consts[:, 3 * P:4 * P]
    k.one = k.sb("one", [P, 1])
    k.stats = k.sb("norm_stats", [P, NT, 2, 6])
    k.moments = k.sb("norm_moments", [P, NT, 2])
    k.root = k.sb("norm_root", [P, NT])
    k.rowmax = k.sb("row_max", [P, 32])
    k.negmax = k.sb("row_max_negated", [P, 32])
    k.inverse_sum = k.sb("inverse_sum", [P, 2, P])


def first_block(k, a):
    nc = k.nc
    with ExitStack() as own:
        memt = k.sb("mem_channel_major", [P, KT, MEM], ctx=own)
        buf = Buffers()
        w_high, w_two = [], []
        for i in range(2):
            slot_at = k.next_place()
            w_high.append(k.sb(f"weights_high_{i}", [P, KT, 256], F32R, ctx=own))
            w_two.append(k.twofold(f"weights_{i}", [P, KT, 256], own))
        mixed = k.over("mixed_channel_major", [P, KT, S], k.x_at, F32)
        mixed_low = k.over("mixed_low", [P, KT, S], k.x_at)
        h_high = k.over("h_high", [P, KT, S], k.ht_at)
        h_value, h_low = k.twofold("h", [P, KT, S], own)
        heads_at = k.next_place()
        qt = k.sb("queries", [P, 4, S], ctx=own)
        kt = k.sb("keys", [P, 4, S], ctx=own)
        mixed_high = k.over("mixed_high", [P, KT, S], heads_at)
        low_t = k.over("latents_channel_major", [P, 3, S], slot_at, F32)
        k.x_home = nc.dram_tensor("x_waiting", (P, NT, D), F32, kind="Internal").ap()
        k.x_stored, k.x_loaded = k.sem("layer_x_stored"), k.sem("layer_x_loaded")
        values = value_views(k.sb("values", [P, NT * 2 * 192], ctx=own), 2)
        scratch = k.sb("attention_scratch", [P, 5, S], ctx=own)
        small = k.sb("small_columns", [P, 16], ctx=own)
        buf.weights = [scratch[:, i, :] for i in range(2)]
        buf.turned = [scratch[:, 2 + i, :] for i in range(2)]
        buf.cum = scratch[:, 4, :]
        gains = h_value[:, 0:4, :]
        mem_x = qt[:, 0:2, :]

        st = Stage(k, "start")
        ready = st.sem("arrived")
        with nc.Block() as block:
            @block.sync
            def _(sp):
                loads = [(k.consts[:], nc.inline_tensor(constants_one(), "constants_one").ap()),
                         (k.x[:], a["x"][0].rearrange("(t p) d -> p t d", p=P)),
                         (mem_x, a["mem"][0].rearrange("(t p) d -> p t d", p=P))]
                for i, name in enumerate(("ln_in_g", "ln_in_b", "mem_ln_g", "mem_ln_b")):
                    loads.append((gains[:, i, :], a[name].partition_broadcast(P)))
                for dst, src in loads:
                    sp.dma_start(dst, src).then_inc(ready, 16)
                sp.wait_ge(ready, 16 * len(loads))

            @block.vector
            def _(dve):
                nc.vector.memset(values[3], 1.0)
                nc.vector.memset(k.one[:], 1.0).then_inc(st.sem("one_set"), 1)
        layer_norm_stage(k, "norm_x", k.x, NT, gains[:, 0, :], gains[:, 1, :])
        layer_norm_stage(k, "norm_mem", mem_x, 2, gains[:, 2, :], gains[:, 3, :])

        st = Stage(k, "mem_turn")
        turned, moved = st.sem("turned"), st.sem("moved")
        with nc.Block() as block:
            @block.sync
            def _(sp):
                st.clear_previous(sp)

            @block.tensor
            def _(pe):
                for c in range(KT):
                    for t in range(2):
                        mm = nc.tensor.transpose(k.psum[:, c, t * P:(t + 1) * P], mem_x[:, t, c * P:(c + 1) * P], k.ident)
                    mm.then_inc(turned, 1)

            @block.vector
            def _(dve):
                for c in range(KT):
                    dve.wait_ge(turned, c + 1)
                    nc.vector.tensor_copy(memt[:, c, :], k.bank(c, MEM)).then_inc(moved, 1)
        loop_edge(k)
        with nc.Fori(0, DEPTH) as layer:
            first_layer(k, a, layer, Holder(memt=memt, buf=buf, w_high=w_high, w_two=w_two, mixed=mixed, mixed_low=mixed_low,
                                            mixed_high=mixed_high, h_high=h_high, h_value=h_value, h_low=h_low, qt=qt,
                                            kt=kt, scratch=scratch, small=small, values=values, low_t=low_t))


class Holder:
    def __init__(self, memt, buf, w_high, w_two, mixed, mixed_low, mixed_high, h_high, h_value, h_low, qt, kt, scratch,
                 small, values, low_t):
        self.memt, self.buf, self.w_high, self.w_two = memt, buf, w_high, w_two
        self.mixed, self.mixed_low, self.mixed_high = mixed, mixed_low, mixed_high
        self.h_high, self.h_value, self.h_low = h_high, h_value, h_low
        self.qt, self.kt, self.scratch, self.small, self.values, self.low_t = qt, kt, scratch, small, values, low_t


def first_layer(k, a, layer, b):
    nc = k.nc
    mixed, qt, kt = b.mixed, b.qt, b.kt
    place, beside, own, _ = b.values

    def rows(name, c0, c1):
        w = a[name]
        return w[bass.ds(layer, 1)].rearrange("l (kt p) c -> p (l kt) c", p=P)[:, :, c0:c1]

    def columns(name, start, count):
        return [rows(name, start + 256 * i, start + 256 * (i + 1)) for i in range(count)]

    W = SplitWeights(k, b.w_high, b.w_two, "layer_w",
                     [rows("w_in", O_FL, O_FL + P)] + columns("w_in", O_FQ, 3) + columns("w_in", O_SQ, 3)
                     + columns("w_in", O_CQ, 1) + columns("w_in", O_CKV, 1) + columns("w_in", O_MQ, 1) + columns("w_mem_kv", 0, 2) + columns("w_in", O_GATE, 4)
                     + columns("w_out", 0, 4))
    (C_FL, C_FQ, C_FK, C_FV, C_SQ, C_SK, C_SV, C_CQ, C_CKV, C_MQ, C_MK, C_MV, C_GATE, _, _, _, C_OUT, _, _, _) = range(20)

    def over_tokens(c, col, width, half):
        s = slice(half * HALF, (half + 1) * HALF)
        return [(W.parts(c, i, col, col + width), (b.h_high[:, i, s], b.h_low[:, i, s])) for i in range(KT)]

    def over_columns(c, t, col, width, high=b.h_high, low=b.h_low):
        tok = slice(t * P, (t + 1) * P)
        return [((high[:, i, tok], low[:, i, tok]), W.parts(c, i, col, col + width)) for i in range(KT)]

    def halves(dst_rows, tile, half):
        return dst_rows[tile][:, half * HALF:(half + 1) * HALF]

    split_transpose_stage(k, "turn_x", lambda t: k.x[:, t, :], b.h_high, (b.h_value, b.h_low), prefetch=(C_FL, C_FQ),
                          splits=(C_FL, C_FQ), w=W, store=(k.x_home, k.x[:], k.x_stored))

    groups = []
    logits = b.scratch[0:4, 0, :]
    work = b.scratch[0:4, 1, :]
    cum = b.scratch[0:4, 2, :]
    negcum = b.scratch[0:4, 3, :]
    bias = b.small[0:4, 0:1]
    for half in range(2):
        def logit_rows(ps, half=half):
            return nc.scalar.copy(logits[:, half * HALF:(half + 1) * HALF], ps[0:4, :])
        groups.append((C_FL, (0, P, HALF), over_tokens(C_FL, 0, P, half), "act", logit_rows))
    for tile in range(4):
        dst = qt if tile < 2 else kt
        for half in range(2):
            def split(ps, dst=dst, tile=tile, half=half):
                h = 2 * (tile % 2)
                cols = slice(half * HALF, (half + 1) * HALF)
                nc.vector.tensor_copy(dst[0:64, h, cols], ps[0:64, :])
                return nc.vector.tensor_copy(dst[0:64, h + 1, cols], ps[64:128, :])

            def split_act(ps, dst=dst, tile=tile, half=half):
                h = 2 * (tile % 2)
                cols = slice(half * HALF, (half + 1) * HALF)
                nc.scalar.copy(dst[0:64, h, cols], ps[0:64, :])
                return nc.scalar.copy(dst[0:64, h + 1, cols], ps[64:128, :])
            c = (C_FQ, C_FK)[tile // 2]
            groups.append((c, (0, P, HALF), over_tokens(c, tile % 2 * P, P, half), "dve" if half else "act",
                           split if half else split_act))
    for t in range(NT):
        who = "dve" if t % 2 else "act"
        groups.append((C_FV, (0, P, 256), over_columns(C_FV, t, 0, 256), who, moving_values(nc, who, place(t, 0, 2))))
    def fill_rows(pool, st):
        filled = st.sem("rows_filled")
        for n, (rows_, value) in enumerate(((slice(64, P), 0.0), (slice(64, 66), 1.0))):
            nc.gpsimd.memset(qt[rows_, :, :], value).then_inc(filled, 1)
            pool.wait_ge(filled, 2 * n + 1)
            nc.gpsimd.memset(kt[rows_, :, :], value).then_inc(filled, 1)
            pool.wait_ge(filled, 2 * n + 2)

    def forget_tail(dve, dve_sem, dve_n, act_sem, act_n, st):
        s = st.sem("forget_step")
        dve.wait_ge(act_sem, act_n)
        dve.wait_ge(k.bias_arrived, 16)
        nc.vector.tensor_scalar(logits, logits, bias, None, ALU.add).then_inc(s, 1)
        dve.wait_ge(s, 1)
        nc.vector.tensor_scalar(work, logits, -1.0, None, ALU.mult).then_inc(s, 1)
        dve.wait_ge(s, 2)
        nc.vector.tensor_tensor(work, work, logits, ALU.min).then_inc(k.forget_abs, 1)
        dve.wait_ge(k.forget_ln, 1)
        nc.vector.tensor_scalar(logits, logits, 0.0, None, ALU.min).then_inc(s, 1)
        dve.wait_ge(s, 3)
        nc.vector.tensor_tensor(logits, logits, work, ALU.subtract).then_inc(s, 1)
        dve.wait_ge(s, 4)
        nc.vector.tensor_tensor_scan(cum, k.one[0:4, 0:1].broadcast_to([4, S]), logits, 0.0, ALU.mult, ALU.add).then_inc(s, 1)
        dve.wait_ge(s, 5)
        nc.vector.tensor_scalar(negcum, cum, -8.0, None, ALU.mult).then_inc(s, 1)
        dve.wait_ge(s, 6)
        nc.vector.tensor_scalar(cum, cum, 8.0, None, ALU.mult).then_inc(s, 1)
        dve.wait_ge(s, 7)

    def forget_act(act, dve_sem, dve_n, act_sem, act_n, st):
        s = st.sem("forget_exp")
        act.dma_start(bias, a["b_forget"][bass.ds(layer, 1)].rearrange("l h -> h l")).then_inc(k.bias_arrived, 16)
        act.wait_ge(k.forget_abs, 1)
        nc.scalar.activation(work, work, ACT.Exp).then_inc(s, 1)
        act.wait_ge(s, 1)
        nc.scalar.activation(work, work, ACT.Ln, bias=1.0).then_inc(k.forget_ln, 1)

    k.bias_arrived, k.forget_abs, k.forget_ln = (k.sem(f"forget_{n}") for n in ("bias_arrived", "abs_ready", "ln_ready"))
    project_stage(k, "fox_project", groups, W, loads=(C_FK, C_FV), splits=(C_FK, C_FV), prefetch=(C_SQ, C_SK),
                  tails_after=(0, 2), lead_pool=fill_rows, tail=forget_tail, tail_act=forget_act)

    st = Stage(k, "forget_rows")
    placed = st.sem("rows_placed")
    with nc.Block() as block:
        @block.sync
        def _(sp):
            st.clear_previous(sp)
            for s in (k.bias_arrived, k.forget_abs, k.forget_ln):
                sp.sem_clear(s)
            sp.dma_start(qt[64:65, :, :], cum).then_inc(placed, 16)
            sp.dma_start(kt[65:66, :, :], negcum).then_inc(placed, 16)
            sp.wait_ge(placed, 32)

    def mixed_rows(kind):
        return lambda h, t: mixed[64 * (h % 2):64 * (h % 2) + 64, 2 * kind + h // 2, t * P:(t + 1) * P]

    def with_ones(h, g, kb):
        return beside(h, kb)

    def full(t):
        return [(0, 0, t + 1)]

    def diagonal(mask):
        return lambda t: [(t * P, P, mask)]

    attention_stage(k, "fox", b.buf, lambda h, g, t: qt[:, h, t * P:(t + 1) * P],
                    lambda h, g, c0, c1: kt[:, h, c0:c1], with_ones,
                    mixed_rows(0), 4, full, diagonal(k.causal_add), HEAD_SCALE, spare=mixed[:, 6, :],
                    splits=(C_SQ, C_SK), w=W)

    def paired(dst, c, first_tile, scale=None):
        out = []
        for tile in range(2):
            for half in range(2):
                who = "dve" if half else "act"
                out.append((c, (0, P, HALF), over_tokens(c, first_tile * P + tile * P, P, half), who,
                            moving(nc, who, dst[:, tile, half * HALF:(half + 1) * HALF], scale)))
        return out

    def padded(c, scale):
        out = []
        for tile in range(2):
            for half in range(2):
                cols = slice(half * HALF, (half + 1) * HALF)

                def split_dve(ps, tile=tile, cols=cols):
                    nc.vector.tensor_scalar_mul(qt[0:64, 2 * tile, cols], ps[0:64, :], scale)
                    return nc.vector.tensor_scalar_mul(qt[64:P, 2 * tile + 1, cols], ps[64:P, :], scale)

                def split_act(ps, tile=tile, cols=cols):
                    nc.scalar.mul(qt[0:64, 2 * tile, cols], ps[0:64, :], scale)
                    return nc.scalar.mul(qt[64:P, 2 * tile + 1, cols], ps[64:P, :], scale)
                out.append((c, (0, P, HALF), over_tokens(c, tile * P, P, half), "dve" if half else "act",
                            split_dve if half else split_act))
        return out

    def zero_halves(pool, dve_sem, dve_n, act_sem, act_n, st):
        for h in range(4):
            r = 64 * (1 - h % 2)
            nc.gpsimd.memset(qt[r:r + 64, h, :], 0.0)

    groups = padded(C_SQ, 0.125) + paired(kt, C_SK, 0)
    for t in range(NT):
        who = "dve" if t % 2 else "act"
        groups.append((C_SV, (0, P, 256), over_columns(C_SV, t, 0, 256), who, moving_values(nc, who, place(t, 0, 2))))
    project_stage(k, "sb_project", groups, W, loads=(C_SV,), splits=(C_SV,), prefetch=(C_CQ, C_CKV), tail_pool=zero_halves)

    def pair_q(h, g, t):
        return qt[:, h, t * P:(t + 1) * P]

    def pair_k(h, g, c0, c1):
        return kt[:, h // 2, c0:c1]

    attention_stage(k, "sb", b.buf, pair_q, pair_k, lambda h, g, kb: own(h, kb),
                    mixed_rows(1), 4, full, None, 1.0, sticks=True, spare=mixed[:, 6, :],
                    splits=(C_CQ, C_CKV), w=W)

    low_rank_stages(k, a, layer, b, W, (C_CQ, C_CKV), over_tokens, over_columns)
    attention_stage(k, "mla", b.buf, lambda h, g, t: qt[0:96, h, t * P:(t + 1) * P],
                    lambda h, g, c0, c1: kt[0:96, h, c0:c1], with_ones,
                    mixed_rows(2), 4, full, diagonal(k.causal_add), MLA_SCALE,
                    prefetch=(C_MQ, C_MK), splits=(C_MQ,), w=W, spare=mixed[:, 6, :])

    groups = padded(C_MQ, 1.0)
    for tile in range(2):
        groups.append((C_MK, (0, P, MEM), [(W.value(C_MK)[:, i, tile * P:(tile + 1) * P], b.memt[:, i, :]) for i in range(KT)],
                       "dve", moving(nc, "dve", kt[:, tile, 0:MEM])))
    for t in range(2):
        groups.append((C_MV, (0, P, 256), [(b.memt[:, i, t * P:(t + 1) * P], W.value(C_MV)[:, i, :]) for i in range(KT)],
                       "act", moving_values(nc, "act", place(t, 0, 2))))
    project_stage(k, "mem_project", groups, W, loads=(C_MV,), prefetch=(C_GATE, C_GATE + 1), tail_pool=zero_halves)
    attention_stage(k, "mem", b.buf, pair_q, pair_k, with_ones,
                    mixed_rows(3), 4, lambda t: [(0, 0, 2)],
                    lambda t: [], HEAD_SCALE, splits=(C_GATE, C_GATE + 1), w=W)

    gate_stage(k, b, W, C_GATE, over_tokens)

    gains = k.ht[:, 0:2, :]
    groups = []
    for c in range(4):
        for t in range(NT):
            def add(ps, c=c, t=t):
                part = b.h_value[:, t, c * 256:(c + 1) * 256]
                return nc.vector.scalar_tensor_tensor(part, part, ALPHA, ps, ALU.mult, ALU.add)
            groups.append((C_OUT + c, (0, P, 256), over_columns(C_OUT + c, t, 0, 256, b.mixed_high, b.mixed_low), "dve", add))
    project_stage(k, "out_project", groups, W, loads=(C_OUT + 2, C_OUT + 3), splits=(C_OUT + 1, C_OUT + 2, C_OUT + 3),
                  reload=(b.h_value[:], k.x_home, k.x_loaded), first_dve=(k.x_loaded, 16))
    layer_norm_stage(k, "norm_out", b.h_value, NT, gains[:, 0, :], gains[:, 1, :], dst=k.x,
                     loads=[(gains[:, i, :], a[n][bass.ds(layer, 1)].rearrange("l d -> (l d)").partition_broadcast(P))
                            for i, n in enumerate(("ln_g", "ln_b"))])
    loop_edge(k, [W, SemaphoreGroup([k.x_stored, k.x_loaded])])


def low_rank_stages(k, a, layer, b, W, chunks, over_tokens, over_columns):
    nc = k.nc
    qt, kt = b.qt, b.kt
    place = b.values[0]
    low = kt[:].rearrange("p a s -> p (a s)")[:, 0:NT * RANKS].rearrange("p (t r) -> p t r", t=NT)
    with ExitStack() as own:
        C_CQ, C_CKV = chunks
        low_t = b.low_t
        up_q = b.scratch[:, 0, 0:768].rearrange("p (a c) -> p a c", a=2)
        up_kv = b.scratch[:, 1, 0:512]
        trig = b.mixed[64:96, 6:8, :]
        turn = b.scratch[64:96, 1, 512:544]
        squares = qt[:].rearrange("p a s -> p (a s)")[:, 0:NT * RANKS].rearrange("p (t r) -> p t r", t=NT)
        sums = b.small[:, 0:16].rearrange("p (t two) -> p t two", two=2)
        gain = k.sb("latent_gains", [P, 3], ctx=own)
        kr = b.scratch[64:96, 2, :]

        st = Stage(k, "mla_loads")
        here = st.sem("arrived")
        with nc.Block() as block:
            @block.sync
            def _(sp):
                st.clear_previous(sp)
                loads = [(up_q, a["w_mla_q_up"][bass.ds(layer, 1)].rearrange("l (kt p) c -> p (l kt) c", p=P)),
                         (up_kv, a["w_mla_kv_up"][bass.ds(layer, 1)].rearrange("l p c -> p (l c)")),
                         (trig, nc.inline_tensor(rope_tables(), "rope_tables_one").ap()),
                         (turn, nc.inline_tensor(rotation(32, [0], 16), "rope_turn_one").ap()),
                         (gain[:, 0:2], a["mla_q_norm_g"][bass.ds(layer, 1)].rearrange("l (kt p) -> p (l kt)", p=P)),
                         (gain[:, 2:3], a["mla_kv_norm_g"][bass.ds(layer, 1)].rearrange("l p -> p l"))]
                for dst, src in loads:
                    sp.dma_start(dst, src).then_inc(here, 16)
                sp.wait_ge(here, 16 * len(loads))

        groups = []
        for t in range(NT):
            def keep(ps, t=t):
                nc.scalar.activation(squares[:, t, 0:256], ps, ACT.Square, accum_out=sums[:, t, 0:1])
                return nc.scalar.copy(low[:, t, 0:256], ps)
            groups.append((C_CQ, (0, P, 256), over_columns(C_CQ, t, 0, 256), "act", keep))
        for t in range(NT):
            def keep_kv(ps, t=t):
                nc.scalar.activation(squares[:, t, 256:384], ps, ACT.Square, accum_out=sums[:, t, 1:2])
                return nc.scalar.copy(low[:, t, 256:384], ps)
            groups.append((C_CKV, (0, P, P), over_columns(C_CKV, t, 0, P), "act", keep_kv))
        for half in range(2):
            def key_rows(ps, half=half):
                return nc.vector.tensor_copy(kr[:, half * HALF:(half + 1) * HALF], ps[0:32, :])
            groups.append((C_CKV, (0, P, HALF), over_tokens(C_CKV, P, P, half), "dve", key_rows))
        project_stage(k, "latent_project", groups, W)

        st = Stage(k, "latent_norm")
        step, added, rooted = st.sem("dve_step"), st.sem("mean_ready"), st.sem("root_ready")
        with nc.Block() as block:
            @block.sync
            def _(sp):
                st.clear_previous(sp)

            @block.vector
            def _(dve):
                nc.vector.tensor_scalar(sums[:, :, 0], sums[:, :, 0], 1.0 / 256, RMS_EPS, ALU.mult, ALU.add)
                nc.vector.tensor_scalar(sums[:, :, 1], sums[:, :, 1], 1.0 / 128, RMS_EPS, ALU.mult, ALU.add).then_inc(added, 1)
                dve.wait_ge(rooted, 1)
                nc.vector.reciprocal(sums, sums).then_inc(step, 1)
                dve.wait_ge(step, 1)
                for t in range(NT):
                    nc.vector.tensor_scalar_mul(low[:, t, 0:256], low[:, t, 0:256], sums[:, t, 0:1])
                    last = nc.vector.tensor_scalar_mul(low[:, t, 256:384], low[:, t, 256:384], sums[:, t, 1:2])
                last.then_inc(step, 1)

            @block.scalar
            def _(act):
                act.wait_ge(added, 1)
                nc.scalar.activation(sums, sums, ACT.Sqrt).then_inc(rooted, 1)
        transpose_stage(k, "turn_latents", lambda t: low[:, t, :], low_t, 3, scale=gain)

        groups = []
        for h in range(4):
            for half in range(2):
                s = slice(half * HALF, (half + 1) * HALF)
                groups.append((None, (0, 96, HALF), [(up_q[:, i, 96 * h:96 * h + 96], low_t[:, i, s]) for i in range(2)],
                               "dve", moving(nc, "dve", qt[0:96, h, s])))
                groups.append((None, (0, 64, HALF), [(up_kv[:, 128 * h:128 * h + 64], low_t[:, 2, s])],
                               "act", moving(nc, "act", kt[0:64, h, s])))
        for t in range(NT):
            vals = up_kv.rearrange("p (h c) -> p h c", h=4)[:, :, 64:128]
            groups.append((None, (0, P, 256), [(low_t[:, 2, t * P:(t + 1) * P], vals)], "act", moving_values(nc, "act", place(t, 0, 2))))
        project_stage(k, "latent_up", groups)

        st = Stage(k, "mla_rope")
        products, step, shared, cos_done, freed = (st.sem(n) for n in ("turned_rows", "dve_step", "key_ready", "cos_done", "freed"))
        heads = [kr] + [qt[64:96, h, :] for h in range(4)]
        sine = b.scratch[64:96, 3, :]
        with nc.Block() as block:
            @block.sync
            def _(sp):
                st.clear_previous(sp)

            @block.tensor
            def _(pe):
                for i, rows_ in enumerate(heads):
                    for half in range(2):
                        s = slice(half * HALF, (half + 1) * HALF)
                        if i >= 3:
                            pe.wait_ge(freed, i - 2)
                        mm = nc.tensor.matmul(k.psum[64:96, 2 * (i % 3) + half, :], turn, rows_[:, s], start=True, stop=True)
                    mm.then_inc(products, 1)

            @block.vector
            def _(dve):
                for i, rows_ in enumerate(heads):
                    dve.wait_ge(products, i + 1)
                    banks = k.psum[64:96, 2 * (i % 3):2 * (i % 3) + 2, :].rearrange("p b n -> p (b n)")
                    nc.vector.tensor_tensor(sine, banks, trig[:, 1, :], ALU.mult).then_inc(freed, 1)
                    dve.wait_ge(freed, i + 1)
                    nc.vector.tensor_tensor(rows_, rows_, trig[:, 0, :], ALU.mult).then_inc(cos_done, 1)
                    dve.wait_ge(cos_done, i + 1)
                    nc.vector.tensor_tensor(rows_, rows_, sine, ALU.add).then_inc(step if i else shared, 1)
                    dve.wait_ge(step if i else shared, max(i, 1))

            @block.scalar
            def _(act):
                act.wait_ge(shared, 1)
                for h in range(4):
                    nc.scalar.copy(kt[64:96, h, :], kr)


def gate_stage(k, b, W, C_GATE, over_tokens):
    nc = k.nc
    mixed = b.mixed
    st = Stage(k, "gate")
    names = ("products_done", "sigmoid_ready", "gated", "dve_step", "weights_rounded", "weights_split", "mixed_rounded")
    products, sigmoid, gated, step, rounded, split, mixed_rounded = (st.sem(n) for n in names)
    sig = b.scratch
    n_groups = 2 * NT
    with nc.Block() as block:
        @block.sync
        def _(sp):
            st.clear_previous(sp)
            for n in range(4):
                sp.wait_ge(products, 4 * (n + 1))
                W.load(sp, C_GATE + 2 + n)

        @block.tensor
        def _(pe):
            for g in range(n_groups):
                c = g // 4
                if g % 4 == 0 and c >= 2:
                    pe.wait_ge(split, c - 1)
                if g >= 4:
                    pe.wait_ge(gated, g - 3)
                gemm(nc, k.bank(g % 4), over_tokens(C_GATE + c, g // 2 % 2 * P, P, g % 2)).then_inc(products, 1)

        @block.gpsimd
        def _(pool):
            def used(c):
                pool.wait_ge(products, 4 * (c - C_GATE + 1))
            W.split(pool, (C_GATE + 2, C_GATE + 3, C_GATE + 4), rounded, split, used)

        def part_of(x, g):
            return x[:, g // 2, g % 2 * HALF:(g % 2 + 1) * HALF]

        @block.scalar
        def _(act):
            def round_high(g):
                act.wait_ge(step, g + 1)
                nc.scalar.copy(part_of(b.mixed_high, g), part_of(mixed, g)).then_inc(mixed_rounded, 1)

            for g in range(n_groups):
                act.wait_ge(products, g + 1)
                if g >= 4:
                    act.wait_ge(step, g - 3)
                nc.scalar.activation(sig[:, g % 4, 0:HALF], k.bank(g % 4), ACT.Sigmoid).then_inc(sigmoid, 1)
                if g:
                    round_high(g - 1)
            round_high(n_groups - 1)

        @block.vector
        def _(dve):
            def subtract(g):
                dve.wait_ge(mixed_rounded, g + 1)
                nc.vector.tensor_tensor(part_of(b.mixed_low, g), part_of(mixed, g), part_of(b.mixed_high, g), ALU.subtract)

            for g in range(n_groups):
                s = sig[:, g % 4, 0:HALF]
                part = part_of(mixed, g)
                dve.wait_ge(sigmoid, g + 1)
                nc.vector.tensor_tensor(s, s, k.bank(g % 4), ALU.mult).then_inc(gated, 1)
                dve.wait_ge(gated, g + 1)
                nc.vector.tensor_tensor(part, part, s, ALU.mult).then_inc(step, 1)
                if g >= 2:
                    subtract(g - 2)
            subtract(n_groups - 2)
            subtract(n_groups - 1)



CHUNK = 64
NCH = S // CHUNK
PAIRS = D // P
ATT = 768
O_RWKV = 3 * ATT
O_LOW = O_RWKV + 3 * D
O_GA = O_LOW + 256
O_GR = O_GA + D
LEVELS = (1, 2, 4, 8, 16, 32)
TWO_PI = 2 * np.pi
ROUND = 1.5 * 2.0 ** 23


def window_masks():
    q, key = np.arange(P)[:, None], np.arange(P)[None, :]

    def mask(ok):
        return np.where(ok, 0.0, MASKED)
    same16, same4 = (q - key) % 16 == 0, (q - key) % 4 == 0
    parts = [mask(same16)] * 7 + [mask(same16 & (key <= q)), mask(key >= q), mask(key <= q)]
    parts += [mask(same4)] * 3 + [mask(same4 & (key <= q)), mask(same4 & (key >= q))]
    return np.concatenate(parts, 1).astype(np.float32)


def constants_two():
    turn = rotation(P, [0, 64], 8)
    ones = np.kron(np.eye(2), np.ones((64, 64)))
    a, b = np.arange(64)[:, None], np.arange(64)[None, :]
    tri = np.concatenate([a < b, a <= b], 1)
    cols = [tri, np.eye(64)]
    for m in LEVELS:
        cols.append((a // (2 * m) == b // (2 * m)) & ((a // m) % 2 == 1) & ((b // m) % 2 == 0))
    cols = np.tile(np.concatenate([c.astype(np.float32) for c in cols], 1), (2, 1))
    freq = (500000.0 ** (-np.arange(8, dtype=np.float32) * 2.0 / 16)).astype(np.float32)
    column = np.tile(np.concatenate([freq, freq, np.zeros(48, np.float32)]), 2)[:, None]
    return np.concatenate([turn, ones, cols, column], 1).astype(np.float32)


class Chain:

    def __init__(self, st, eng, name):
        self.sem, self.eng, self.n = st.sem(name), eng, 0

    def __call__(self, ins):
        self.n += 1
        ins.then_inc(self.sem, 1)
        self.eng.wait_ge(self.sem, self.n)


def rms_scale_stage(k, name, src, junk, eps, then, store=None, ready=None):
    nc = k.nc
    st = Stage(k, name)
    summed, added, rooted = st.sem("squares_summed"), st.sem("mean_ready"), st.sem("root_ready")
    with nc.Block() as block:
        @block.sync
        def _(sp):
            st.clear_previous(sp)
            if store:
                sp.dma_start(store[0], store[1]).then_inc(store[2], 16)
                sp.wait_ge(store[2], 16)

        @block.scalar
        def _(act):
            for t in range(NT):
                last = nc.scalar.activation(junk[:, t, :], src[:, t, :], ACT.Square, accum_out=k.root[:, t:t + 1])
            last.then_inc(summed, 1)
            act.wait_ge(added, 1)
            nc.scalar.activation(k.root[:], k.root[:], ACT.Sqrt).then_inc(rooted, 1)

        @block.vector
        def _(dve):
            chain = Chain(st, dve, "dve_step")
            dve.wait_ge(summed, 1)
            nc.vector.tensor_scalar(k.root[:], k.root[:], 1.0 / D, eps, ALU.mult, ALU.add).then_inc(added, 1)
            dve.wait_ge(rooted, 1)
            chain(nc.vector.reciprocal(k.root[:], k.root[:]))
            if ready:
                dve.wait_ge(*ready)
            for t in range(NT):
                then(t, chain)


def second_block(k, a, out):
    nc = k.nc
    w_in = a["w_in_2"][0].rearrange("(kt p) c -> p kt c", p=P)
    with ExitStack() as own:
        k.c2 = k.sb("tables_two", [P, 128 + 128 + 128 + 64 + 6 * 64 + 1], ctx=own)
        k.turn, k.head_ones = k.c2[:, 0:128], k.c2[:, 128:256]
        k.tri = k.c2[:, 256:384]
        k.eye64 = k.c2[:, 384:448]
        k.level = [k.c2[:, 448 + 64 * i:512 + 64 * i] for i in range(6)]
        k.freq = k.c2[:, 832:833]
        vec = k.sb("vectors_by_channel", [P, 98], ctx=own)
        k.x_home = nc.dram_tensor("x_waiting_two", (P, NT, D), F32, kind="Internal").ap()
        k.x_away, k.x_back = k.sem("x_stored"), k.sem("x_loaded")
        mod = k.sb("modulation_by_channel", [P, 4, 8], ctx=own)
        post = k.sb("post_norm_rows", [P, 2, D], ctx=own)
        modulation_stages(k, a, vec, mod, post)

        with ExitStack() as merged_scope:
            oat = k.sb("attention_out_channel_major", [P, 2, S], ctx=merged_scope)
            with ExitStack() as att_scope:
                windows(k, a, w_in, mod, oat, att_scope)
            ort = k.sb("rwkv_out_channel_major", [P, PAIRS, S], ctx=merged_scope)
            with ExitStack() as rwkv_scope:
                rwkv(k, a, w_in, vec, ort, rwkv_scope)
            merged = k.sb("merged", [P, NT, D], ctx=merged_scope)
            with ExitStack() as scope:
                branches(k, a, w_in, oat, ort, merged, scope)
            transpose_stage(k, "turn_merged", lambda t: merged[:, t, :], k.ht, KT)
            wbuf = [ort[:, 4 * i:4 * i + 4, :].rearrange("p a s -> p (a s)").rearrange("p (a s) -> p a s", a=8) for i in range(2)]
            post_project(k, a["w_out_2"][0], wbuf, merged, post[:, 0, :])
        feed_forward(k, a, mod, post)

        st = Stage(k, "store")
        stored = st.sem("stored")
        with nc.Block() as block:
            @block.sync
            def _(sp):
                st.clear_previous(sp)
                sp.dma_start(out[0].rearrange("(t p) d -> p t d", p=P), k.x[:]).then_inc(stored, 16)
                sp.wait_ge(stored, 16)


def modulation_stages(k, a, vec, mod, post):
    nc = k.nc
    with ExitStack() as own:
        rows_a = k.sb("vector_rows", [98, P], ctx=own)
        rows_b = k.sb("condition_rows", [56, P], ctx=own)
        cond = k.sb("condition_by_channel", [P, 56], ctx=own)
        spread = k.sb("condition_spread", [P, KT, P], ctx=own)
        sig = k.sb("condition_sigmoid", [P, KT], ctx=own)
        gate_bias = k.sb("gate_bias_rows", [P, 4, D], ctx=own)
        wbuf = [k.sb(f"ada_weights_{i}", [P, KT, HALF], ctx=own) for i in range(2)]
        ada = a["ada_w_2"][0].rearrange("(kt p) c -> p kt c", p=P)
        W = Weights(k, wbuf, "ada", [ada[:, :, i * HALF:(i + 1) * HALF] for i in range(12)])

        st = Stage(k, "vectors")
        here, turned, moved, silu = (st.sem(n) for n in ("arrived", "turned", "moved", "sigmoid_ready"))
        with nc.Block() as block:
            @block.sync
            def _(sp):
                st.clear_previous(sp)
                loads = [(k.c2[:], nc.inline_tensor(constants_two(), "constants_two").ap())]
                mu = a["shift_mu_2"][0].rearrange("(r c) -> r c", c=P)
                names = ("norm_mix_pre_2", "norm_ffn_pre_2", None, "decay_w0_2", "iclr_a0_2", "k_k_2", "k_a_2", None,
                         "gn_w_2", "gn_b_2")
                row = 0
                for name in names:
                    if name is None and row == 16:
                        loads.append((rows_a[16:40, :], mu[0:24, :]))
                        row = 40
                        continue
                    src = a[name][0].rearrange("(r c) -> r c", c=P) if name else \
                        a["r_k_2"][0].rearrange("(r two) c -> r (two c)", two=2)
                    loads.append((rows_a[row:row + 8, :], src))
                    row += 8
                loads.append((rows_a[96:98, :], mu[24:26, :]))
                loads.append((rows_b[0:48, :], a["ada_b_2"][0].rearrange("(r c) -> r c", c=P)))
                loads.append((rows_b[48:56, :], a["c_2"][0].rearrange("(r c) -> r c", c=P)))
                for i, part in enumerate((2, 5)):
                    loads.append((gate_bias[:, i, :], a["ada_b_2"][0, part * D:(part + 1) * D].partition_broadcast(P)))
                for i, name in enumerate(("norm_mix_post_2", "norm_ffn_post_2")):
                    loads.append((gate_bias[:, 2 + i, :], a[name][0].partition_broadcast(P)))
                for dst, src in loads:
                    sp.dma_start(dst, src).then_inc(here, 16)
                W.load(sp, 0)
                W.load(sp, 1)
                sp.dma_start(k.x_home, k.x[:]).then_inc(k.x_away, 16)
                st.loads = len(loads)
                sp.wait_ge(here, 16 * len(loads))

            @block.tensor
            def _(pe):
                pe.wait_ge(here, 16 * st.loads)
                nc.tensor.transpose(k.psum[:, 0, 0:98], rows_a[:], k.ident[0:98, 0:98]).then_inc(turned, 1)
                nc.tensor.transpose(k.psum[:, 1, 0:56], rows_b[:], k.ident[0:56, 0:56]).then_inc(turned, 1)

            @block.vector
            def _(dve):
                dve.wait_ge(turned, 2)
                nc.vector.tensor_copy(vec[:], k.psum[:, 0, 0:98])
                nc.vector.tensor_copy(cond[:], k.psum[:, 1, 0:56]).then_inc(moved, 1)
                dve.wait_ge(silu, 1)
                chain = Chain(st, dve, "dve_step")
                chain(nc.vector.tensor_tensor(sig[:], sig[:], cond[:, 48:56], ALU.mult))
                nc.vector.tensor_copy(spread[:], sig[:].unsqueeze(2).broadcast_to([P, KT, P]))

            @block.scalar
            def _(act):
                act.wait_ge(moved, 1)
                nc.scalar.activation(sig[:], cond[:, 48:56], ACT.Sigmoid).then_inc(silu, 1)

        st = Stage(k, "modulation")
        products, evacuated = st.sem("products_done"), st.sem("evacuated")
        with nc.Block() as block:
            @block.sync
            def _(sp):
                st.clear_previous(sp)
                for c in range(2, 12):
                    sp.wait_ge(products, c - 1)
                    W.load(sp, c)

            @block.tensor
            def _(pe):
                for c in range(12):
                    pe.wait_ge(W.loaded[c], 16)
                    if c >= 4:
                        pe.wait_ge(evacuated, c - 3)
                    if c // 2 in (2, 5):
                        gemm(nc, k.bank(c % 4), [(spread[:, i, :], W.view(c)[:, i, :]) for i in range(KT)]).then_inc(products, 1)
                    else:
                        for j in range(4):
                            mm = gemm(nc, k.psum[:, c % 4, j:j + 1],
                                      [(W.view(c)[:, i, j * P:(j + 1) * P], sig[:, i:i + 1]) for i in range(KT)])
                        mm.then_inc(products, 1)

            @block.vector
            def _(dve):
                chain = Chain(st, dve, "dve_step")
                slot = {0: 0, 1: 1, 3: 2, 4: 3}
                for c in range(12):
                    part, half = c // 2, c % 2
                    dve.wait_ge(products, c + 1)
                    if part in (2, 5):
                        i = 0 if part == 2 else 1
                        s = slice(half * HALF, (half + 1) * HALF)
                        ins = nc.vector.tensor_tensor(post[:, i, s], k.bank(c % 4), gate_bias[:, i, s], ALU.add)
                    else:
                        ins = nc.vector.tensor_tensor(mod[:, slot[part], 4 * half:4 * half + 4], k.psum[:, c % 4, 0:4],
                                                      cond[:, 8 * part + 4 * half:8 * part + 4 * half + 4], ALU.add)
                    ins.then_inc(evacuated, 1)
                dve.wait_ge(evacuated, 12)
                for i in range(2):
                    nc.vector.tensor_tensor(post[:, i, :], post[:, i, :], gate_bias[:, 2 + i, :], ALU.mult)
                    last = nc.vector.scalar_tensor_tensor(mod[:, 2 * i + 1, :], mod[:, 2 * i + 1, :], 1.0,
                                                          vec[:, 8 * i:8 * i + 8], ALU.add, ALU.mult)
                chain(last)
    loop_edge(k, [W])


def windows(k, a, w_in, mod, oat, scope):
    nc = k.nc
    qk = k.sb("window_queries_keys", [P, 12, S], ctx=scope)
    place, beside, _, ones = value_views(k.sb("window_values", [P, NT * 6 * 192], ctx=scope), 6)
    trig = k.x[:, 6:8, :]
    wbuf = [k.sb(f"window_weights_{i}", [P, KT, HALF], ctx=scope) for i in range(2)]
    W = Weights(k, wbuf, "window_w", [w_in[:, :, c:min(c + HALF, 3 * ATT)] for c in range(0, 3 * ATT, HALF)])

    scaled = qk[:, 0:8, :]
    rms_scale_stage(k, "norm_mix", k.x, scaled, 1e-6,
                    lambda t, chain: nc.vector.tensor_scalar_mul(scaled[:, t, :], k.x[:, t, :], k.root[:, t:t + 1]))
    transpose_stage(k, "turn_mix", lambda t: scaled[:, t, :], k.ht, KT, scale=mod[:, 1, :], shift=mod[:, 0, :])

    raw = qk[:, 0, :]
    angle, turns, t2 = qk[:, 1, :], qk[:, 2, :], qk[:, 3, :]
    st = Stage(k, "window_trig")
    here, sin_in, cos_in, cast = st.sem("arrived"), st.sem("sine_argument"), st.sem("cosine_argument"), st.sem("cast")
    parts = [6.28125, 0.00193500518798828125]
    parts.append(TWO_PI - sum(parts))
    with nc.Block() as block:
        @block.sync
        def _(sp):
            st.clear_previous(sp)
            sp.dma_start(raw.bitcast(I32), a["positions_2"][0].partition_broadcast(P)).then_inc(here, 16)
            W.load(sp, 0)
            W.load(sp, 1)

        @block.vector
        def _(dve):
            chain = Chain(st, dve, "dve_step")
            nc.vector.memset(ones, 1.0)
            dve.wait_ge(k.x_away, 16)
            dve.wait_ge(here, 16)
            chain(nc.vector.tensor_copy(t2, raw.bitcast(I32)))
            chain(nc.vector.tensor_scalar(angle, t2, k.freq, None, ALU.mult))
            chain(nc.vector.tensor_scalar(turns, angle, 1 / TWO_PI, ROUND, ALU.mult, ALU.add))
            chain(nc.vector.tensor_scalar(turns, turns, -ROUND, None, ALU.add))
            for c in parts:
                chain(nc.vector.scalar_tensor_tensor(angle, turns, -c, angle, ALU.mult, ALU.add))
            chain(nc.vector.tensor_scalar(angle, angle, 3.1415925, -3.1415925, ALU.min, ALU.max))
            nc.vector.tensor_copy(trig[:, 1, :], angle).then_inc(sin_in, 1)
            chain(nc.vector.tensor_scalar(t2, angle, float(np.pi / 2), None, ALU.add))
            chain(nc.vector.tensor_scalar(turns, t2, float(np.pi), -TWO_PI, ALU.is_gt, ALU.mult))
            chain(nc.vector.tensor_tensor(t2, t2, turns, ALU.add))
            nc.vector.tensor_scalar(trig[:, 0, :], t2, 3.1415925, -3.1415925, ALU.min, ALU.max).then_inc(cos_in, 1)

        @block.scalar
        def _(act):
            act.wait_ge(sin_in, 1)
            nc.scalar.activation(trig[:, 1, :], trig[:, 1, :], ACT.Sin)
            act.wait_ge(cos_in, 1)
            nc.scalar.activation(trig[:, 0, :], trig[:, 0, :], ACT.Sin)

    groups = []
    for tile in range(12):
        for half in range(2):
            who = "dve" if half else "act"
            s = slice(half * HALF, (half + 1) * HALF)
            c = tile // 4
            groups.append((c, (0, P, HALF), [(W.view(c)[:, i, tile % 4 * P:(tile % 4 + 1) * P], k.ht[:, i, s]) for i in range(KT)],
                           who, moving(nc, who, qk[:, tile, s])))
    for c, col, n in ((3, 0, 512), (4, 512, 256)):
        for t in range(NT):
            who = "dve" if t % 2 else "act"
            groups.append((c, (0, P, n), [(k.ht[:, i, t * P:(t + 1) * P], W.view(c)[:, i, 0:n]) for i in range(KT)],
                           who, moving_values(nc, who, place(t, col // P, (col + n) // P))))
    project_stage(k, "window_project", groups, W, loads=(2, 3, 4))

    st = Stage(k, "window_rope")
    products, read, cosined, step = (st.sem(n) for n in ("turned_rows", "sine_part_ready", "cosine_part_ready", "dve_step"))
    part = [wbuf[0][:, 2 * i:2 * i + 2, :].rearrange("p a s -> p (a s)") for i in range(2)]
    with nc.Block() as block:
        @block.sync
        def _(sp):
            st.clear_previous(sp)
            sp.sem_clear(k.x_away)

        @block.tensor
        def _(pe):
            for i in range(12):
                if i >= 3:
                    pe.wait_ge(read, i - 2)
                for half in range(2):
                    mm = nc.tensor.matmul(k.psum[:, 2 * (i % 3) + half, :], k.turn, qk[:, i, half * HALF:(half + 1) * HALF],
                                          start=True, stop=True)
                mm.then_inc(products, 1)

        @block.gpsimd
        def _(pool):
            nc.gpsimd.memset(k.x[0:64, 0:6, :], 0.0)
            for i in range(12):
                pool.wait_ge(products, i + 1)
                nc.gpsimd.tensor_tensor(qk[:, i, :], qk[:, i, :], trig[:, 0, :], ALU.mult).then_inc(cosined, 1)
            pool.wait_ge(cosined, 12)
            for i in range(6):
                pool.wait_ge(step, i + 1)
                nc.gpsimd.memset(qk[64:P, i, :], 0.0)

        @block.vector
        def _(dve):
            for i in range(12):
                dve.wait_ge(products, i + 1)
                if i >= 2:
                    dve.wait_ge(step, i - 1)
                nc.vector.tensor_tensor(part[i % 2], k.banks2(2 * (i % 3)), trig[:, 1, :], ALU.mult).then_inc(read, 1)
                dve.wait_ge(read, i + 1)
                dve.wait_ge(cosined, i + 1)
                if i < 6:
                    nc.vector.tensor_tensor(qk[0:64, i, :], qk[0:64, i, :], part[i % 2][0:64, :], ALU.add)
                    nc.vector.tensor_tensor(k.x[64:P, i, :], qk[64:P, i, :], part[i % 2][64:P, :], ALU.add).then_inc(step, 1)
                else:
                    nc.vector.tensor_tensor(qk[:, i, :], qk[:, i, :], part[i % 2], ALU.add).then_inc(step, 1)

    masks_row = trig.rearrange("p a s -> p (a s)")[:, 0:15 * P]
    st = Stage(k, "window_masks")
    here = st.sem("arrived")
    with nc.Block() as block:
        @block.sync
        def _(sp):
            st.clear_previous(sp)
            sp.dma_start(masks_row, nc.inline_tensor(window_masks(), "window_masks").ap()).then_inc(here, 16)
            sp.wait_ge(here, 16)

    def plan(t):
        runs = [(2, 0, t + 1), (0, max(t - 1, 0), min(t, 1) + 1), (1, max(t - 3, 0), min(t, 3) + 1)]
        return runs + ([(1, t - 4, 1)] if t >= 4 else [])

    def masks(t):
        wide = (t + 1) * P
        near = (min(t, 1) + 1) * P
        mid = (min(t, 3) + 1 + (t >= 4)) * P
        out = [(0, wide, masks_row[:, (7 - t) * P:8 * P]),
               (wide, near, masks_row[:, (8 if t else 9) * P:10 * P]),
               (wide + near, mid, masks_row[:, (13 - min(t, 3)) * P:(14 + (t >= 4)) * P])]
        if t >= 4:
            return [(0, wide + near + mid, masks_row[:, (7 - t) * P:15 * P])]
        return out

    buf = Buffers()
    buf.weights = [wbuf[0][:].rearrange("p a s -> p (a s)")[:, i * 2048:(i + 1) * 2048] for i in range(2)]
    buf.turned = [wbuf[1][:].rearrange("p a s -> p (a s)")[:, i * 2048:(i + 1) * 2048] for i in range(2)]

    def query(h, g, t):
        head = 4 * g + h
        return (k.x if head % 2 else qk)[:, head // 2, t * P:(t + 1) * P]

    attention_stage(k, "window", buf, query,
                    lambda h, g, c0, c1: qk[:, 6 + (4 * g + h) // 2, c0:c1],
                    lambda h, g, b: beside(4 * g + h, b),
                    lambda h, t: oat[64 * (h % 2):64 * (h % 2) + 64, h // 2, t * P:(t + 1) * P], 4, plan, masks, 0.125)
    loop_edge(k, [W])


def rwkv(k, a, w_in, vec, ort, scope):
    nc = k.nc
    low = k.sb("low_rank", [P, 2, S], ctx=scope)
    wr = k.sb("pair_weights", [P, 3, KT, P], ctx=scope)
    wl = k.sb("pair_low_weights", [P, 2, P], ctx=scope)
    raw = k.sb("unshifted", [P, 4 + S], ctx=scope)
    pv = k.sb("pair_vectors", [P, 16], ctx=scope)
    eps = pv[:, 14:15]
    tiles = k.sb("pair_tiles", [P, 11, S], ctx=scope)
    b = [tiles[:, i, :] for i in range(11)]
    ar = k.sb("decayed_a_and_r", [P, NCH, 2, CHUNK], ctx=scope)
    lb = k.sb("a_and_r_by_b", [P, NCH, 2, CHUNK], ctx=scope)
    lk = tiles[:, 9:11, :].rearrange("p q (n a c) -> p (q n) a c", a=2, c=CHUNK)
    state = k.sb("state", [P, 2, CHUNK], ctx=scope)
    small = k.sb("x_and_u", [P, 2, CHUNK], ctx=scope)
    k_loaded = k.sem("pair_weights_loaded")

    def by_chunk(t):
        return t.rearrange("p (n c) -> p n c", c=CHUNK)

    def load_pair(sp, p):
        for j in range(3):
            sp.dma_start(wr[:, j, :, :], w_in[:, :, bass.ds(p * P + (O_RWKV + j * D), P)]).then_inc(k_loaded, 16)

    lw = lb[:].rearrange("p n a c -> p (n a c)").rearrange("p (kt c) -> p kt c", c=256)
    st = Stage(k, "low_rank")
    here, products, kept, mixed, act_step = (st.sem(n) for n in ("arrived", "products_done", "raw_kept", "shifted", "act_step"))
    with nc.Block() as block:
        @block.sync
        def _(sp):
            st.clear_previous(sp)
            sp.dma_start(lw, w_in[:, :, O_LOW:O_LOW + 256]).then_inc(here, 16)
            load_pair(sp, 0)

        @block.tensor
        def _(pe):
            pe.wait_ge(here, 16)
            for j in range(2):
                for half in range(2):
                    mm = gemm(nc, k.bank(2 * j + half), [(lw[:, i, j * P:(j + 1) * P], k.ht[:, i, half * HALF:(half + 1) * HALF])
                                                        for i in range(KT)])
                mm.then_inc(products, 1)

        @block.scalar
        def _(act):
            for j in range(2):
                act.wait_ge(products, j + 1)
                if j:
                    act.wait_ge(mixed, 1)
                nc.scalar.copy(raw[:, 4:4 + S], k.banks2(2 * j)).then_inc(kept, 1)
            act.wait_ge(mixed, 2)
            nc.scalar.activation(low[0:64, 0, :], low[0:64, 0, :], ACT.Tanh)
            nc.scalar.activation(low[:, 1, :], low[:, 1, :], ACT.Sigmoid)

        @block.vector
        def _(dve):
            chain = Chain(st, dve, "dve_step")
            nc.vector.memset(raw[:, 0:4], 0.0)
            nc.vector.memset(eps, GN_EPS)
            for j in range(2):
                mu = vec[:, 96 + j:97 + j]
                chain(nc.vector.tensor_scalar(pv[:, 15:16], mu, -1.0, 1.0, ALU.mult, ALU.add))
                dve.wait_ge(kept, j + 1)
                chain(nc.vector.tensor_scalar_mul(low[:, j, :], raw[:, 4:4 + S], pv[:, 15:16]))
                nc.vector.scalar_tensor_tensor(low[:, j, :], raw[:, 3:3 + S], mu, low[:, j, :], ALU.mult, ALU.add).then_inc(mixed, 1)
                dve.wait_ge(mixed, j + 1)
    loop_edge(k)

    with nc.Fori(0, PAIRS) as p:
        pair_body(k, a, p, dict(low=low, wr=wr, wl=wl, raw=raw, pv=pv, b=b, ar=ar, lb=lb, lk=lk, state=state,
                                small=small, eps=eps, loaded=k_loaded, load=load_pair, by_chunk=by_chunk, vec=vec, ort=ort))
    st = Stage(k, "pair_end")
    with nc.Block() as block:
        @block.sync
        def _(sp):
            sp.wait_ge(k_loaded, 48)
            sp.sem_clear(k_loaded)


def pair_body(k, a, p, t):
    nc = k.nc
    low, wr, wl, raw, pv, b = t["low"], t["wr"], t["wl"], t["raw"], t["pv"], t["b"]
    ar, lb, lk, state, small = t["ar"], t["lb"], t["lk"], t["state"], t["small"]
    by_chunk = t["by_chunk"]
    (MU_R, MU_K, MU_V, W0, A0, KK, KA, RK, GW, GB, KEEP_R, KEEP_K, KEEP_V) = (pv[:, i:i + 1] for i in range(13))
    vec = t["vec"]

    st = Stage(k, "pair_project")
    products, kept, part, shifted, vectors, here = (
        st.sem(n) for n in ("products_done", "raw_kept", "kept_part_ready", "shifted", "vectors_ready", "arrived"))
    first, second = (0, 2, 4), (6, 0)
    with nc.Block() as block:
        @block.sync
        def _(sp):
            sp.dma_start(wl[0:64, 0, :], a["decay_w2_2"][0][:, bass.ds(p * P, P)]).then_inc(here, 16)
            sp.dma_start(wl[64:128, 0, :], a["iclr_a2_2"][0][:, bass.ds(p * P, P)]).then_inc(here, 16)
            sp.dma_start(wl[:, 1, :], a["gate_g2_2"][0][:, bass.ds(p * P, P)]).then_inc(here, 16)
            sp.wait_ge(here, 48)

        @block.tensor
        def _(pe):
            pe.wait_ge(t["loaded"], 48)
            for j in range(3):
                for half in range(2):
                    mm = gemm(nc, k.bank(first[j] + half), [(wr[:, j, i, :], k.ht[:, i, half * HALF:(half + 1) * HALF])
                                                           for i in range(KT)])
                mm.then_inc(products, 1)
            pe.wait_ge(here, 48)
            for j in range(2):
                if j:
                    pe.wait_ge(kept, 1)
                    pe.wait_ge(part, 1)
                r0 = 64 * j
                for half in range(2):
                    mm = nc.tensor.matmul(k.bank(second[j] + half), wl[r0:r0 + 64, 0, :],
                                          low[r0:r0 + 64, 0, half * HALF:(half + 1) * HALF], start=True, stop=True)
                mm.then_inc(products, 1)

        @block.vector
        def _(dve):
            chain = Chain(st, dve, "dve_step")
            table = vec[:, 16:96].rearrange("p (j q) -> p j q", q=8)
            chain(nc.vector.tensor_copy(pv[:, 0:10].unsqueeze(2), table[:, :, bass.ds(p, 1)]))
            nc.vector.tensor_scalar(pv[:, 10:13], pv[:, 0:3], -1.0, 1.0, ALU.mult, ALU.add).then_inc(vectors, 1)
            dve.wait_ge(vectors, 1)
            for j in range(3):
                dve.wait_ge(products, j + 1)
                nc.vector.tensor_scalar_mul(b[j], k.banks2(first[j]), (KEEP_R, KEEP_K, KEEP_V)[j]).then_inc(part, 1)
                dve.wait_ge(part, j + 1)
                dve.wait_ge(kept, j + 1)
                nc.vector.scalar_tensor_tensor(b[j], raw[:, 3:3 + S], (MU_R, MU_K, MU_V)[j], b[j],
                                               ALU.mult, ALU.add).then_inc(shifted, 1)

        @block.scalar
        def _(act):
            for j in range(3):
                act.wait_ge(products, j + 1)
                act.wait_ge(part, j + 1)
                if j:
                    act.wait_ge(shifted, j)
                nc.scalar.copy(raw[:, 4:4 + S], k.banks2(first[j])).then_inc(kept, 1)
            for j in range(2):
                act.wait_ge(products, 4 + j)
                nc.scalar.activation(b[3 + j], k.banks2(second[j]), ACT.Sigmoid, bias=(W0, A0)[j])

    st = Stage(k, "pair_prepare")
    names = ("logs_ready", "decays_ready", "squares_ready", "norms_done", "bonus_ready", "bonus_done", "clamped", "root_ready",
             "r_ready", "norm_used")
    logs, decays, squares, norms, bonus_in, bonus_done, clamped, rooted, r_ready, norm_used = (
        st.sem(n) for n in names)
    last_decay = by_chunk(b[6])[:, :, 63:64].broadcast_to([P, NCH, CHUNK])
    with nc.Block() as block:
        @block.sync
        def _(sp):
            st.clear_previous(sp)
            sp.sem_clear(t["loaded"])

        @block.scalar
        def _(act):
            chain = Chain(st, act, "act_step")
            nc.scalar.preload_act_table_set("natural_log_exp_and_others")
            nc.scalar.mul(b[7], b[1], KK)
            nc.scalar.activation(b[10], b[1], ACT.Square, scale=KK).then_inc(squares, 1)
            act.wait_ge(logs, 1)
            nc.scalar.activation(b[6], b[5], ACT.Exp, scale=-E_HALF)
            chain(nc.scalar.activation(b[9], b[9], ACT.Exp, scale=-E_HALF))
            nc.scalar.activation(b[5], b[5], ACT.Exp, scale=E_HALF).then_inc(decays, 1)
            act.wait_ge(clamped, 1)
            chain(nc.scalar.activation(b[10], b[10], ACT.Ln))
            nc.scalar.activation(b[10], b[10], ACT.Exp, scale=-0.5).then_inc(rooted, 1)

        @block.tensor
        def _(pe):
            for i, (ready, done, src) in enumerate(((squares, norms, b[10]), (bonus_in, bonus_done, b[8]))):
                pe.wait_ge(ready, 1)
                for half in range(2):
                    mm = nc.tensor.matmul(k.bank(2 * i + half), k.head_ones, src[:, half * HALF:(half + 1) * HALF],
                                          start=True, stop=True)
                mm.then_inc(done, 1)

        @block.vector
        def _(dve):
            chain = Chain(st, dve, "dve_step")
            one = k.one[:, 0:1].broadcast_to([P, CHUNK])
            for n in range(NCH):
                s = slice(n * CHUNK, (n + 1) * CHUNK)
                last = nc.vector.tensor_tensor_scan(b[5][:, s], one, b[3][:, s], 0.0, ALU.mult, ALU.add)
            chain(last)
            nc.vector.tensor_tensor(b[9], b[5], b[3], ALU.subtract).then_inc(logs, 1)
            chain(nc.vector.tensor_scalar(b[8], b[4], -1.0, KA, ALU.add, ALU.mult))
            dve.wait_ge(squares, 1)
            chain(nc.vector.scalar_tensor_tensor(b[1], b[8], 1.0, b[1], ALU.add, ALU.mult))
            nc.vector.scalar_tensor_tensor(b[8], b[0], RK, b[1], ALU.mult, ALU.mult).then_inc(bonus_in, 1)
            dve.wait_ge(norms, 1)
            nc.vector.tensor_scalar_max(b[10], k.banks2(0), 1e-24).then_inc(clamped, 1)
            dve.wait_ge(bonus_done, 1)
            nc.vector.tensor_tensor(b[8], k.banks2(2), b[2], ALU.mult)
            dve.wait_ge(decays, 1)
            dve.wait_ge(logs, 1)
            chain(nc.vector.tensor_tensor(b[3], b[1], b[5], ALU.mult))
            dve.wait_ge(rooted, 1)
            nc.vector.tensor_tensor(b[7], b[7], b[10], ALU.mult).then_inc(norm_used, 1)
            dve.wait_ge(norm_used, 1)
            chain(nc.vector.scalar_tensor_tensor(ar[:, :, 0, :], by_chunk(b[7]), -1.0, by_chunk(b[9]), ALU.mult, ALU.mult))
            chain(nc.vector.tensor_tensor(b[7], b[7], b[4], ALU.mult))
            chain(nc.vector.tensor_tensor(b[4], b[7], b[5], ALU.mult))
            nc.vector.tensor_tensor(by_chunk(b[9]), by_chunk(b[4]), last_decay, ALU.mult)

        @block.gpsimd
        def _(pool):
            pool.wait_ge(decays, 1)
            nc.gpsimd.tensor_tensor(ar[:, :, 1, :], by_chunk(b[0]), by_chunk(b[6]), ALU.mult).then_inc(r_ready, 1)
            pool.wait_ge(r_ready, 1)
            pool.wait_ge(norm_used, 1)
            nc.gpsimd.tensor_tensor(by_chunk(b[10]), by_chunk(b[3]), last_decay, ALU.mult)

    ends = raw[:, 4:4 + NCH]
    st = Stage(k, "pair_turn")
    turned, used = st.sem("turned"), st.sem("copied")
    sources = (b[2], b[9], b[10])
    dests = (b[0], b[1], b[5])
    with nc.Block() as block:
        @block.sync
        def _(sp):
            st.clear_previous(sp)
            t["load"](sp, p + 1)

        @block.tensor
        def _(pe):
            for j in range(3):
                for m in range(8):
                    mm = nc.tensor.transpose(k.psum[:, 2 * j + m // 4, (m % 4) * P:(m % 4 + 1) * P],
                                             sources[j][:, m * P:(m + 1) * P], k.ident)
                mm.then_inc(turned, 1)

        def quadrants(j):
            banks = k.psum[:, 2 * j:2 * j + 2, :].rearrange("p b (m c) -> p (b m) c", c=P)
            for parity in range(2):
                for h in range(2):
                    dst = dests[j][64 * h:64 * h + 64, :].rearrange("p (m q c) -> p m q c", q=2, c=CHUNK)[:, :, parity, :]
                    yield dst, banks[64 * parity:64 * parity + 64, :, 64 * h:64 * h + 64]

        @block.vector
        def _(dve):
            nc.vector.tensor_copy(ends, by_chunk(b[6])[:, :, 63])
            for j in (0, 2):
                dve.wait_ge(turned, j + 1)
                for i, (dst, src) in enumerate(quadrants(j)):
                    if j == 0 or i < 2:
                        last = nc.vector.tensor_copy(dst, src)
            last.then_inc(used, 1)

        @block.scalar
        def _(act):
            for j in (1, 2):
                act.wait_ge(turned, j + 1)
                if j == 2:
                    act.wait_ge(used, 1)
                for i, (dst, src) in enumerate(quadrants(j)):
                    if j == 1 or i >= 2:
                        nc.scalar.copy(dst, src)

    st = Stage(k, "pair_products")
    done = st.sem("products_done")
    with nc.Block() as block:
        @block.sync
        def _(sp):
            st.clear_previous(sp)

        @block.tensor
        def _(pe):
            for i, src in enumerate((b[4], b[3])):
                for n in range(NCH):
                    for h in range(2):
                        r = slice(64 * h, 64 * h + 64)
                        mm = nc.tensor.matmul(k.psum[r, 4 * i + n // 4, (n % 4) * P:(n % 4 + 1) * P],
                                              src[r, n * CHUNK:(n + 1) * CHUNK], ar[r, n, :, :].rearrange("p a c -> p (a c)"),
                                              start=True, stop=True)
                    if n % 4 == 3:
                        mm.then_inc(done, 1)

        @block.vector
        def _(dve):
            for i, dst in enumerate((lb, lk)):
                for q in range(4):
                    dve.wait_ge(done, 4 * i + q + 1)
                    nc.vector.tensor_tensor(dst[:, 4 * q:4 * q + 4, :, :].rearrange("p n a c -> p n (a c)"),
                                            k.bank(4 * i + q).rearrange("p (n c) -> p n c", c=P),
                                            k.tri.unsqueeze(1).broadcast_to([P, 4, P]), ALU.mult)

    st = Stage(k, "pair_inverse")
    zdone, zready, tdone, tadded, turned, moved, masked = (
        st.sem(n) for n in ("z_products_done", "z_ready", "t_products_done", "t_added", "turned", "moved", "z_masked"))
    inv, inv_t, z = b[6], b[7], b[2]
    LAST = 5

    def side(x, q):
        return x[:, HALF * q:HALF * (q + 1)].rearrange("p (m i c) -> p m i c", i=2, c=CHUNK)

    def psum_side(first, q):
        return (k.psum[:, first + 2 * q:first + 2 * q + 2, 0:4 * CHUNK]
                .rearrange("p i (m c) -> p m i c", c=CHUNK))

    order = [(i + j, j ^ h) for i in range(0, 8, 2) for h in range(2) for j in range(2)]
    with nc.Block() as block:
        @block.sync
        def _(sp):
            st.clear_previous(sp)

        @block.tensor
        def _(pe):
            def systems(q):
                for i, h in order:
                    n = 8 * q + i
                    at = ((n // 2) * 2 + h) * CHUNK
                    yield (slice(64 * h, 64 * h + 64), slice(64 * (n % 2), 64 * (n % 2) + 64), n,
                           slice(n * CHUNK, (n + 1) * CHUNK), slice(at, at + CHUNK))

            def tile(half, first, second, n, q):
                at = n % 8 // 2 * CHUNK
                return k.psum[half, first + 2 * q + second, at:at + CHUNK]

            def do_z(lev, q):
                if lev:
                    pe.wait_ge(tadded, 2 * (lev - 1) + q + 1)
                for hh, ch, n, cols, tcols in systems(q):
                    if lev:
                        mm = nc.tensor.matmul(tile(ch, 0, hh.start // 64, n, q), lb[hh, n, 0, :], inv[hh, cols],
                                              start=True, stop=True)
                    else:
                        mm = nc.tensor.matmul(tile(hh, 4, n % 2, n, q), lb[hh, n, 0, :], k.eye64[hh, :],
                                              start=True, stop=True)
                mm.then_inc(zdone, 1)

            def do_t(lev, q):
                pe.wait_ge(zready, 2 * (lev - 1) + q + 1)
                pe.wait_ge(moved, 2 * (lev - 1) + q + 1)
                for hh, ch, n, cols, tcols in systems(q):
                    out = tile(hh, 4, n % 2, n, q)
                    lhs, rhs = (inv_t, z) if lev < LAST else (z, inv_t)
                    mm = nc.tensor.matmul(out, lhs[ch, tcols], rhs[ch, tcols], start=True, stop=True)
                mm.then_inc(tdone, 1)

            def do_turn(lev, q):
                pe.wait_ge(tadded, 2 * lev + q + 1)
                for i in range(4):
                    mm = nc.tensor.transpose(k.psum[:, 4 + 2 * q, i * P:(i + 1) * P],
                                             inv[:, HALF * q + i * P:HALF * q + (i + 1) * P], k.ident)
                mm.then_inc(turned, 1)

            for q in range(2):
                do_z(0, q)
            for lev in range(LAST):
                for q in range(2):
                    do_turn(lev, q)
                    do_z(lev + 1, q)
                for q in range(2):
                    do_t(lev + 1, q)

        @block.vector
        def _(dve):
            eye = k.eye64.unsqueeze(1).unsqueeze(1).broadcast_to([P, 4, 2, CHUNK])
            for lev in range(LAST + 1):
                mask = k.level[lev].unsqueeze(1).unsqueeze(1).broadcast_to([P, 4, 2, CHUNK])
                for q in range(2):
                    dve.wait_ge(zdone, 2 * lev + q + 1)
                    if lev == 0:
                        nc.vector.tensor_tensor(side(inv, q), psum_side(4, q), mask, ALU.mult).then_inc(masked, 1)
                        dve.wait_ge(masked, q + 1)
                        nc.vector.tensor_tensor(side(inv, q), side(inv, q), eye, ALU.add).then_inc(tadded, 1)
                    elif lev < LAST:
                        nc.vector.tensor_tensor(side(z, q), psum_side(0, q), mask, ALU.mult).then_inc(zready, 1)
                    else:
                        nc.vector.tensor_tensor(side(z, q), psum_side(0, q), mask, ALU.mult).then_inc(masked, 1)
                        dve.wait_ge(masked, 2 + q + 1)
                        nc.vector.tensor_tensor(side(z, q), side(z, q), eye, ALU.add).then_inc(zready, 1)
                if 0 < lev < LAST:
                    for q in range(2):
                        dve.wait_ge(tdone, 2 * (lev - 1) + q + 1)
                        nc.vector.tensor_tensor(side(inv, q), side(inv, q), psum_side(4, q), ALU.add).then_inc(tadded, 1)

        @block.scalar
        def _(act):
            for lev in range(LAST):
                for q in range(2):
                    act.wait_ge(turned, 2 * lev + q + 1)
                    nc.scalar.copy(inv_t[:, HALF * q:HALF * (q + 1)], k.bank(4 + 2 * q)).then_inc(moved, 1)
            for q in range(2):
                act.wait_ge(tdone, 2 * (LAST - 1) + q + 1)
                nc.scalar.copy(side(inv, q), psum_side(4, q))

    st = Stage(k, "pair_scan")
    names = ("x_done", "x_ready", "u_done", "u_ready", "update_done", "state_ready", "y_done", "y_moved")
    xdone, xready, udone, uready, mdone, mready, ydone, ymoved = (st.sem(n) for n in names)
    vt, bt, kt, inv_t = b[0], b[1], b[5], b[6]
    y = b[3]
    xs, us = small[:, 0, :], small[:, 1, :]
    heads = (slice(0, 64), slice(64, 128))
    with nc.Block() as block:
        @block.sync
        def _(sp):
            st.clear_previous(sp)

        @block.tensor
        def _(pe):
            def product(n, bank, lhs, rhs, at=0, start=False, stop=False):
                for r in heads:
                    mm = nc.tensor.matmul(k.psum[r, bank, at:at + 64], lhs(r), rhs(r), start=start, stop=stop,
                                          skip_group_check=True)
                return mm

            def of(x, n):
                return lambda r: x[r, n * CHUNK:(n + 1) * CHUNK]

            def first_of_x(n):
                product(n, 0, lambda r: lk[r, n, 0, :], of(vt, n), start=True)

            first_of_x(0)
            for n in range(NCH):
                m = lambda r: state[r, n % 2, :]
                out = dict(bank=3 + n // 8, at=(n % 8) * 64)
                pe.wait_ge(mready, n + 1)
                product(n, 0, lambda r: ar[r, n, 0, :], m, stop=True).then_inc(xdone, 1)
                product(n, 2, of(kt, n), of(vt, n), start=True)
                pe.wait_ge(xready, n + 1)
                product(n, 1, of(inv_t, n), lambda r: xs[r, :], start=True, stop=True).then_inc(udone, 1)
                if n + 1 < NCH:
                    first_of_x(n + 1)
                product(n, lhs=of(vt, n), rhs=lambda r: lk[r, n, 1, :], start=True, **out)
                pe.wait_ge(uready, n + 1)
                product(n, 2, of(bt, n), lambda r: us[r, :], stop=True).then_inc(mdone, 1)
                product(n, lhs=m, rhs=lambda r: ar[r, n, 1, :], **out)
                product(n, lhs=lambda r: us[r, :], rhs=lambda r: lb[r, n, 1, :], stop=True, **out).then_inc(ydone, 1)

        @block.vector
        def _(dve):
            nc.vector.memset(state[:, 0, :], 0.0).then_inc(mready, 1)
            for n in range(NCH):
                dve.wait_ge(xdone, n + 1)
                nc.vector.tensor_copy(xs, k.psum[:, 0, 0:64]).then_inc(xready, 1)
                dve.wait_ge(udone, n + 1)
                if n:
                    dve.wait_ge(ydone, n)
                nc.vector.tensor_copy(us, k.psum[:, 1, 0:64]).then_inc(uready, 1)
                dve.wait_ge(mdone, n + 1)
                dve.wait_ge(mready, n + 1)
                nc.vector.scalar_tensor_tensor(state[:, (n + 1) % 2, :], state[:, n % 2, :], ends[:, n:n + 1],
                                               k.psum[:, 2, 0:64], ALU.mult, ALU.add).then_inc(mready, 1)

        @block.scalar
        def _(act):
            for i in range(2):
                act.wait_ge(ydone, 8 * (i + 1))
                nc.scalar.copy(y[:, i * HALF:(i + 1) * HALF], k.bank(3 + i))

    st = Stage(k, "pair_out")
    names = ("means_done", "centred", "squares_ready", "variances_done", "variance_logs_ready", "root_ready", "gate_done")
    means, centred, squares, variances, vready, rooted, gated = (st.sem(n) for n in names)
    ones = k.head_ones
    with nc.Block() as block:
        @block.sync
        def _(sp):
            st.clear_previous(sp)

        @block.tensor
        def _(pe):
            for half in range(2):
                mm = nc.tensor.matmul(k.bank(half), ones, y[:, half * HALF:(half + 1) * HALF], start=True, stop=True)
            mm.then_inc(means, 1)
            for half in range(2):
                mm = nc.tensor.matmul(k.bank(4 + half), wl[:, 1, :], low[:, 1, half * HALF:(half + 1) * HALF], start=True, stop=True)
            mm.then_inc(gated, 1)
            pe.wait_ge(squares, 1)
            for half in range(2):
                mm = nc.tensor.matmul(k.bank(2 + half), ones, b[7][:, half * HALF:(half + 1) * HALF], start=True, stop=True)
            mm.then_inc(variances, 1)

        @block.scalar
        def _(act):
            act.wait_ge(centred, 1)
            nc.scalar.activation(b[7], b[9], ACT.Square).then_inc(squares, 1)
            act.wait_ge(variances, 1)
            nc.scalar.activation(b[6], k.banks2(2), ACT.Ln, scale=1.0 / 64, bias=t["eps"]).then_inc(vready, 1)
            act.wait_ge(vready, 1)
            nc.scalar.activation(b[6], b[6], ACT.Exp, scale=-0.5).then_inc(rooted, 1)

        @block.vector
        def _(dve):
            chain = Chain(st, dve, "dve_step")
            dve.wait_ge(means, 1)
            nc.vector.scalar_tensor_tensor(b[9], k.banks2(0), -1.0 / 64, y, ALU.mult, ALU.add).then_inc(centred, 1)
            dve.wait_ge(rooted, 1)
            dve.wait_ge(centred, 1)
            chain(nc.vector.tensor_tensor(b[9], b[9], b[6], ALU.mult))
            chain(nc.vector.tensor_scalar(b[9], b[9], GW, GB, ALU.mult, ALU.add))
            chain(nc.vector.tensor_tensor(b[9], b[9], b[8], ALU.add))
            dve.wait_ge(gated, 1)
            nc.vector.tensor_tensor(t["ort"][:, bass.ds(p, 1), :].rearrange("p o s -> p (o s)"), b[9], k.banks2(4), ALU.mult)
    loop_edge(k)


def branches(k, a, w_in, oat, ort, merged, scope):
    nc = k.nc
    C = 256
    wg = [k.sb(f"gate_weights_{i}", [P, KT, 2, C], ctx=scope) for i in range(2)]
    wb = [k.sb(f"branch_weights_{i}", [P, 10, C], ctx=scope) for i in range(2)]
    wbr = a["w_branch_2"][0].rearrange("(kt p) c -> p kt c", p=P)
    st = Stage(k, "branches")
    loaded = [st.sem(f"loaded_{i}") for i in range(4)]
    products, sigmoid, joined, added = (st.sem(n) for n in ("products_done", "sigmoid_ready", "joined", "added"))
    sig = k.sb("branch_sigmoids", [P, 2, 512], ctx=scope)
    N = 4 * NT
    with nc.Block() as block:
        @block.sync
        def _(sp):
            st.clear_previous(sp)
            for c in range(4):
                if c >= 2:
                    sp.wait_ge(products, NT * (c - 1))
                if c == 2:
                    sp.dma_start(k.x[:], k.x_home).then_inc(k.x_back, 16)
                i = c % 2
                sp.dma_start(wg[i][:, :, 0, :], w_in[:, :, O_GA + c * C:O_GA + (c + 1) * C]).then_inc(loaded[c], 16)
                sp.dma_start(wg[i][:, :, 1, :], w_in[:, :, O_GR + c * C:O_GR + (c + 1) * C]).then_inc(loaded[c], 16)
                sp.dma_start(wb[i][:], wbr[:, :, c * C:(c + 1) * C]).then_inc(loaded[c], 16)

        @block.tensor
        def _(pe):
            for g in range(N):
                c, t = g // NT, g % NT
                i = c % 2
                tok = slice(t * P, (t + 1) * P)
                if t == 0:
                    pe.wait_ge(loaded[c], 48)
                if g >= 4:
                    pe.wait_ge(joined, g - 3)
                gemm(nc, k.bank(2 * (g % 4)), [(k.ht[:, j, tok], wg[i][:, j, :, :].rearrange("p a c -> p (a c)")) for j in range(KT)])
                gemm(nc, k.psum[:, 2 * (g % 4) + 1, 0:C], [(oat[:, j, tok], wb[i][:, j, :]) for j in range(2)])
                gemm(nc, k.psum[:, 2 * (g % 4) + 1, C:2 * C],
                     [(ort[:, j, tok], wb[i][:, 2 + j, :]) for j in range(KT)]).then_inc(products, 1)

        @block.scalar
        def _(act):
            for g in range(N):
                act.wait_ge(products, g + 1)
                if g >= 2:
                    act.wait_ge(added, g - 1)
                nc.scalar.activation(sig[:, g % 2, :], k.bank(2 * (g % 4)), ACT.Sigmoid).then_inc(sigmoid, 1)

        @block.vector
        def _(dve):
            for g in range(N):
                c, t = g // NT, g % NT
                s = sig[:, g % 2, :]
                dve.wait_ge(sigmoid, g + 1)
                nc.vector.tensor_tensor(s, s, k.bank(2 * (g % 4) + 1), ALU.mult).then_inc(joined, 1)
                dve.wait_ge(joined, g + 1)
                nc.vector.tensor_tensor(merged[:, t, c * C:(c + 1) * C], s[:, 0:C], s[:, C:2 * C], ALU.add).then_inc(added, 1)


def post_project(k, w, wbuf, y, post):
    nc = k.nc
    src = w.rearrange("(kt p) c -> p kt c", p=P)
    W = Weights(k, wbuf, "mix_out", [src[:, :, i * HALF:(i + 1) * HALF] for i in range(2)])
    groups = []
    for n in range(2):
        for t in range(NT):
            who = "dve" if t % 2 else "act"
            groups.append((n, (0, P, HALF), [(k.ht[:, i, t * P:(t + 1) * P], W.view(n)[:, i, :]) for i in range(KT)],
                           who, moving(nc, who, y[:, t, n * HALF:(n + 1) * HALF])))
    project_stage(k, "mix_out_project", groups, W, loads=(0, 1), then_wait=[(k.x_back, 16)])
    add_normed(k, "norm_mix_post", y, post)
    loop_edge(k, [W])


def add_normed(k, name, y, post, ready=None):
    nc = k.nc

    def then(t, chain):
        chain(nc.vector.scalar_tensor_tensor(y[:, t, :], y[:, t, :], k.root[:, t:t + 1], post, ALU.mult, ALU.mult))
        nc.vector.tensor_tensor(k.x[:, t, :], k.x[:, t, :], y[:, t, :], ALU.add)
    rms_scale_stage(k, name, y, k.ht, 1e-6, then, ready=ready)


def feed_forward(k, a, mod, post):
    nc = k.nc
    PARTS = 4
    with ExitStack() as own:
        f = k.sb("ffn_out", [P, NT, D], ctx=own)
        hid_high = k.sb("hidden_high", [P, KT, S], F32R, ctx=own)
        hid_value, hid_low = k.twofold("hidden", [P, KT, S], own)
        h_high, h_low = k.over("h_high", [P, KT, S], k.ht_at), k.over("h_low", [P, KT, S], k.x_at)
        w_high = [k.sb(f"ffn_weights_high_{i}", [P, 4 * HALF], F32R, ctx=own) for i in range(2)]
        w_two = [k.twofold(f"ffn_weights_{i}", [P, 4 * HALF], own) for i in range(2)]
        away, back = k.sem("ffn_x_stored"), k.sem("ffn_x_loaded")
        rms_scale_stage(k, "norm_ffn", k.x, f, 1e-6,
                        lambda t, chain: nc.vector.tensor_scalar_mul(f[:, t, :], k.x[:, t, :], k.root[:, t:t + 1]),
                        store=(k.x_home, k.x[:], away))
        loaded = [k.sem(f"ffn_weights_loaded_{c}") for c in range(8)]
        w1 = a["w_ff1_2"][0].rearrange("(kt p) c -> p kt c", p=P)
        w2 = a["w_ff2_2"][0].rearrange("(kt p) c -> p kt c", p=P)

        def load(sp, part, c):
            if c < 4:
                src = w1[:, :, bass.ds(part * D + c * 256, 256)]
            else:
                n, r = divmod(c - 4, 2)
                src = w2[:, bass.ds(part * KT + 4 * r, 4), n * HALF:(n + 1) * HALF]
            dst = w_two[c % 2][0][:].rearrange("p (kt c) -> p kt c", c=256 if c < 4 else HALF)
            sp.dma_start(dst, src).then_inc(loaded[c], 16)

        def weights(c, i, c0, c1):
            w = 256 if c < 4 else HALF
            return [part[:, i * w + c0:i * w + c1] for part in (w_high[c % 2], w_two[c % 2][1])]

        def split_chunk(pool, c, rounded, split, count):
            high, (value, low) = w_high[c % 2], w_two[c % 2]
            nc.gpsimd.tensor_copy(high[:], value[:]).then_inc(rounded, 1)
            pool.wait_ge(rounded, count)
            nc.gpsimd.tensor_tensor(low[:], value[:], high[:], ALU.subtract).then_inc(split, 1)

        class FirstChunks:

            def load(self, eng, c):
                load(eng, 0, c)

            def split(self, pool, chunks, rounded, done):
                pool.wait_ge(loaded[0], 16)
                split_chunk(pool, 0, rounded, done, 1)

        split_transpose_stage(k, "turn_ffn", lambda t: f[:, t, :], h_high, (k.x, h_low), mod[:, 3, :], mod[:, 2, :],
                              prefetch=(0, 1), splits=(0,), w=FirstChunks())
        st = Stage(k, "ffn_zero")
        with nc.Block() as block:
            @block.vector
            def _(dve):
                nc.vector.memset(f[:], 0.0)

            @block.sync
            def _(sp):
                st.clear_previous(sp)
                sp.sem_clear(away)
        loop_edge(k, [SemaphoreGroup(loaded[:1])])

        def ffn_part(part, last):
            st = Stage(k, "ffn_last_part" if last else "ffn_part")
            names = ("weights_rounded", "weights_split", "up_done", "down_done", "moved", "squared", "rounded",
                     "hidden_split", "added")
            wrounded, wsplit, up_done, down_done, moved, squared, rounded, split, added = (st.sem(n) for n in names)

            def chunk_used(eng, c):
                if c < 4:
                    eng.wait_ge(up_done, 4 * (c + 1))
                else:
                    eng.wait_ge(down_done, NT * (c - 3))

            def place(x, g):
                return x[:, g // 2, (g % 2) * HALF:(g % 2 + 1) * HALF]

            with nc.Block() as block:
                @block.sync
                def _(sp):
                    for c in range(2, 8):
                        chunk_used(sp, c - 2)
                        load(sp, part, c)
                        if last and c == 5:
                            sp.dma_start(k.x[:], k.x_home).then_inc(back, 16)
                    if not last:
                        chunk_used(sp, 6)
                        load(sp, part + 1, 0)
                        chunk_used(sp, 7)
                        sp.sem_clear(loaded[1])
                        load(sp, part + 1, 1)

                @block.gpsimd
                def _(pool):
                    for c in range(1, 8 if last else 9):
                        pool.wait_ge(loaded[c % 8], 16)
                        if c >= 2:
                            chunk_used(pool, c - 2)
                        split_chunk(pool, c, wrounded, wsplit, c)

                @block.tensor
                def _(pe):
                    for g in range(2 * KT):
                        tile, half = g // 2, g % 2
                        c = tile // 2
                        if g % 4 == 0 and c:
                            pe.wait_ge(wsplit, c)
                        if g >= 4:
                            pe.wait_ge(moved, g - 3)
                        s = slice(half * HALF, (half + 1) * HALF)
                        split_gemm(nc, k.bank(g % 4), [(weights(c, i, tile % 2 * P, tile % 2 * P + P), (h_high[:, i, s], h_low[:, i, s]))
                                                       for i in range(KT)]).then_inc(up_done, 1)
                    for n in range(2):
                        for r in range(2):
                            c = 4 + 2 * n + r
                            pe.wait_ge(wsplit, c)
                            pe.wait_ge(split, 16 if n else 8 * (r + 1))
                            if not n and not r:
                                pe.wait_ge(moved, 16)
                            for t in range(NT):
                                if n and not r:
                                    pe.wait_ge(added, t + 1)
                                tok = slice(t * P, (t + 1) * P)
                                split_gemm(nc, k.bank(t), [((hid_high[:, 4 * r + i, tok], hid_low[:, 4 * r + i, tok]),
                                                            weights(c, i, 0, HALF)) for i in range(4)],
                                           first=(r == 0), last=(r == 1)).then_inc(down_done, 1)

                @block.vector
                def _(dve):
                    def subtract(g):
                        dve.wait_ge(rounded, g + 1)
                        nc.vector.tensor_tensor(place(hid_low, g), place(hid_value, g), place(hid_high, g),
                                                ALU.subtract).then_inc(split, 1)

                    for g in range(2 * KT):
                        dve.wait_ge(moved, g + 1)
                        nc.vector.tensor_tensor(place(hid_value, g), place(hid_value, g), place(hid_value, g), ALU.mult).then_inc(squared, 1)
                        if g:
                            subtract(g - 1)
                    subtract(2 * KT - 1)
                    for n in range(2):
                        for t in range(NT):
                            dve.wait_ge(down_done, NT * (2 * n + 1) + t + 1)
                            s = f[:, t, n * HALF:(n + 1) * HALF]
                            nc.vector.tensor_tensor(s, s, k.bank(t), ALU.add).then_inc(added, 1)

                @block.scalar
                def _(act):
                    def round_high(g):
                        act.wait_ge(squared, g + 1)
                        nc.scalar.copy(place(hid_high, g), place(hid_value, g)).then_inc(rounded, 1)

                    for g in range(2 * KT):
                        act.wait_ge(up_done, g + 1)
                        nc.scalar.activation(place(hid_value, g), k.bank(g % 4), ACT.Relu).then_inc(moved, 1)
                        if g:
                            round_high(g - 1)
                    round_high(2 * KT - 1)
            loop_edge(k, [SemaphoreGroup(loaded if last else loaded[:1] + loaded[2:])])

        with nc.Fori(0, PARTS - 1) as part:
            ffn_part(part, False)
        ffn_part(PARTS - 1, True)
        add_normed(k, "norm_ffn_post", f, post[:, 1, :], ready=(back, 16))




def program(nc, a, out):
    with ExitStack() as ctx:
        k = Kernel(nc, ctx)
        common_tensors(k)
        first_block(k, a)
        second_block(k, a, out)



def kernel(**inputs):
    import numpy as _np
    import concourse.bacc as _bacc
    from concourse import mybir as _mybir
    from concourse.bass_utils import run_bass_kernel_spmd as _run

    nc = _bacc.Bacc("TRN2", target_bir_lowering=False, num_devices=1)
    arrays, args = {}, {}
    for name, value in inputs.items():
        value = _np.ascontiguousarray(value)
        arrays[f"in_{name}_dram"] = value
        args[name] = nc.dram_tensor(f"in_{name}_dram", value.shape, _mybir.dt.from_np(value.dtype), kind="ExternalInput").ap()
    out = nc.dram_tensor("out_dram", (1, S, D), _mybir.dt.float32, kind="ExternalOutput").ap()
    program(nc, args, out)
    r = _run(nc, [arrays], core_ids=[0])
    return r.results[0]["out_dram"]
```
